# Optimizing a Trainium2 kernel written in Bass

```python
import math
import jax, jax.numpy as jnp
from jax import lax
import numpy as np
import jax
import jax.numpy as jnp

D_MODEL = 1024
BATCH = 1
SEQ = 256
DEPTH = 2

N_MIXERS = 2
N_LAYERS_A = (DEPTH + 1) // 2
N_LAYERS_B = DEPTH // 2

A_HEADS = 4
A_QK_DIM = D_MODEL // (2 * A_HEADS)
A_V_DIM = D_MODEL // A_HEADS
A_CHUNK = 128
A_HQ = A_HEADS * A_QK_DIM
A_HV = A_HEADS * A_V_DIM
A_IN_COLS = 2 * A_HQ + 2 * A_HV + 2 * A_HEADS

B_HEADS = 8
B_HEAD_DIM = D_MODEL // (2 * B_HEADS)
B_V_DIM = 2 * B_HEAD_DIM
B_ROT_DIM = B_HEAD_DIM // 4
ROPE_THETA = 500000.0
Q_BLOCK = 128
B_IN_COLS = 3 * D_MODEL

N_EXPERTS = 16
N_GROUPS = 4
EXPERTS_PER_GROUP = N_EXPERTS // N_GROUPS
TOP_K = 2
D_EXPERT = 512
MOE_BLOCK = 128

EPS = 1e-6


def _rms(x, g):
    xf = x.astype(jnp.float32)
    y = xf * lax.rsqrt(jnp.mean(xf * xf, axis=-1, keepdims=True) + EPS)
    return y * g.astype(jnp.float32)

def _chunks(t):
    b_, h_, s_ = t.shape[:3]
    t = t.reshape(b_, h_, s_ // A_CHUNK, A_CHUNK, *t.shape[3:])
    return jnp.moveaxis(t, 2, 0)

def _mlstm_chunkwise(q, k, v, i_pre, log_f):
    b_, h_, s_, dk = q.shape
    dv = v.shape[-1]
    causal = jnp.tril(jnp.ones((A_CHUNK, A_CHUNK), dtype=bool))

    def step(carry, inp):
        C, n, m = carry
        qc, kc, vc, ic, fc = inp
        b = jnp.cumsum(fc, axis=-1)
        log_d = b[..., :, None] - b[..., None, :] + ic[..., None, :]
        log_d = jnp.where(causal, log_d, -jnp.inf)
        log_inter = b + m[..., None]
        m_t = jnp.maximum(jnp.max(log_d, axis=-1), log_inter)
        d = jnp.exp(log_d - m_t[..., None])
        inter = jnp.exp(log_inter - m_t)
        s = jnp.einsum('bhtd,bhsd->bhts', qc, kc) * d
        num = jnp.einsum('bhts,bhsv->bhtv', s, vc) + inter[..., None] * jnp.einsum('bhtd,bhdv->bhtv', qc, C)
        den = jnp.sum(s, axis=-1) + inter * jnp.einsum('bhtd,bhd->bht', qc, n)
        h = num / jnp.maximum(jnp.abs(den), jnp.exp(-m_t))[..., None]
        b_last = b[..., -1]
        log_w = b_last[..., None] - b + ic
        m_new = jnp.maximum(b_last + m, jnp.max(log_w, axis=-1))
        w = jnp.exp(log_w - m_new[..., None])
        decay = jnp.exp(b_last + m - m_new)
        kw = kc * w[..., None]
        C_new = decay[..., None, None] * C + jnp.einsum('bhsd,bhsv->bhdv', kw, vc)
        n_new = decay[..., None] * n + jnp.sum(kw, axis=2)
        return (C_new, n_new, m_new), h

    init = (jnp.zeros((b_, h_, dk, dv), jnp.float32), jnp.zeros((b_, h_, dk), jnp.float32),
            jnp.zeros((b_, h_), jnp.float32))
    _, hs = lax.scan(step, init, (_chunks(q), _chunks(k), _chunks(v), _chunks(i_pre), _chunks(log_f)))
    return jnp.moveaxis(hs, 0, 2).reshape(b_, h_, s_, dv)

def _mlstm_mixer(h, w_in, b_if, h_norm, w_out):
    b_, s_, _ = h.shape
    proj = h @ w_in.astype(h.dtype)
    q = proj[..., :A_HQ].reshape(b_, s_, A_HEADS, A_QK_DIM)
    k = proj[..., A_HQ:2 * A_HQ].reshape(b_, s_, A_HEADS, A_QK_DIM)
    v = proj[..., 2 * A_HQ:2 * A_HQ + A_HV].reshape(b_, s_, A_HEADS, A_V_DIM)
    o = proj[..., 2 * A_HQ + A_HV:2 * A_HQ + 2 * A_HV]
    gates = proj[..., 2 * A_HQ + 2 * A_HV:].astype(jnp.float32) + b_if.astype(jnp.float32)
    i_pre = jnp.transpose(gates[..., :A_HEADS], (0, 2, 1))
    log_f = jax.nn.log_sigmoid(jnp.transpose(gates[..., A_HEADS:], (0, 2, 1)))
    q = jnp.transpose(q, (0, 2, 1, 3)).astype(jnp.float32)
    k = jnp.transpose(k, (0, 2, 1, 3)).astype(jnp.float32) * (A_QK_DIM ** -0.5)
    v = jnp.transpose(v, (0, 2, 1, 3)).astype(jnp.float32)
    hout = _mlstm_chunkwise(q, k, v, i_pre, log_f)
    hout = _rms(jnp.transpose(hout, (0, 2, 1, 3)), h_norm.reshape(A_HEADS, A_V_DIM))
    hout = hout.reshape(b_, s_, A_HV) * jax.nn.sigmoid(o.astype(jnp.float32))
    return hout.astype(h.dtype) @ w_out.astype(h.dtype)

def _partial_rope(t, positions):
    half = B_ROT_DIM // 2
    inv_freq = ROPE_THETA ** (-jnp.arange(0, B_ROT_DIM, 2, dtype=jnp.float32) / B_ROT_DIM)
    ang = positions.astype(jnp.float32)[..., None] * inv_freq
    cos = jnp.cos(ang)[:, :, None, None, :]
    sin = jnp.sin(ang)[:, :, None, None, :]
    x1 = t[..., :half]
    x2 = t[..., half:B_ROT_DIM]
    return jnp.concatenate([x1 * cos - x2 * sin, x2 * cos + x1 * sin, t[..., B_ROT_DIM:]], axis=-1)

def _diff_attention(h, positions, w_in, q_norm, k_norm, lam_q1, lam_k1, lam_q2, lam_k2, o_norm, w_out, layer_idx):
    b_, s_, _ = h.shape
    proj = h @ w_in.astype(h.dtype)
    q = proj[..., :D_MODEL].reshape(b_, s_, B_HEADS, 2, B_HEAD_DIM)
    k = proj[..., D_MODEL:2 * D_MODEL].reshape(b_, s_, B_HEADS, 2, B_HEAD_DIM)
    v = proj[..., 2 * D_MODEL:].reshape(b_, s_, B_HEADS, B_V_DIM).astype(jnp.float32)
    q = _partial_rope(_rms(q, q_norm), positions)
    k = _partial_rope(_rms(k, k_norm), positions)
    q = jnp.transpose(q, (0, 2, 3, 1, 4)) * (B_HEAD_DIM ** -0.5)
    k = jnp.transpose(k, (0, 2, 3, 1, 4))
    v = jnp.transpose(v, (0, 2, 1, 3))
    lam_init = 0.8 - 0.6 * math.exp(-0.3 * layer_idx)
    lam = (jnp.exp(jnp.sum(lam_q1.astype(jnp.float32) * lam_k1.astype(jnp.float32)))
           - jnp.exp(jnp.sum(lam_q2.astype(jnp.float32) * lam_k2.astype(jnp.float32))) + lam_init)
    outs = []
    for j in range(s_ // Q_BLOCK):
        s0 = j * Q_BLOCK
        e = s0 + Q_BLOCK
        sc = jnp.einsum('bhcqd,bhckd->bhcqk', q[:, :, :, s0:e], k[:, :, :, :e])
        mask = (s0 + jnp.arange(Q_BLOCK))[:, None] >= jnp.arange(e)[None, :]
        p = jax.nn.softmax(jnp.where(mask, sc, -jnp.inf), axis=-1)
        a = p[:, :, 0] - lam * p[:, :, 1]
        outs.append(jnp.einsum('bhqk,bhkv->bhqv', a, v[:, :, :e]))
    o = jnp.concatenate(outs, axis=2)
    o = _rms(o, o_norm) * (1.0 - lam_init)
    o = jnp.transpose(o, (0, 2, 1, 3)).reshape(b_, s_, D_MODEL)
    return o.astype(h.dtype) @ w_out.astype(h.dtype)

def _grouped_moe(h, w_router, router_bias, w_gu, w_down):
    b_, s_, d_ = h.shape
    n_tok = b_ * s_
    xt = h.reshape(n_tok, d_)
    scores = jax.nn.sigmoid((xt @ w_router.astype(h.dtype)).astype(jnp.float32))
    biased = (scores + router_bias.astype(jnp.float32)).reshape(n_tok, N_GROUPS, EXPERTS_PER_GROUP)
    grp_score = jnp.sum(lax.top_k(biased, 2)[0], axis=-1)
    g_sel = jnp.argmax(grp_score, axis=-1)
    in_grp = jnp.take_along_axis(biased, g_sel[:, None, None], axis=1)[:, 0]
    _, local_idx = lax.top_k(in_grp, TOP_K)
    expert_idx = g_sel[:, None].astype(jnp.int32) * EXPERTS_PER_GROUP + local_idx.astype(jnp.int32)
    gate_w = jnp.take_along_axis(scores, expert_idx, axis=1)
    gate_w = gate_w / jnp.sum(gate_w, axis=-1, keepdims=True)
    n_assign = n_tok * TOP_K
    n_blocks = (n_assign + N_EXPERTS * (MOE_BLOCK - 1) + MOE_BLOCK - 1) // MOE_BLOCK
    cap = n_blocks * MOE_BLOCK
    flat_e = expert_idx.reshape(n_assign)
    flat_tok = jnp.repeat(jnp.arange(n_tok, dtype=jnp.int32), TOP_K)
    order = jnp.argsort(flat_e, stable=True)
    sorted_e = flat_e[order]
    sorted_tok = flat_tok[order]
    sorted_w = gate_w.reshape(n_assign)[order]
    counts = jnp.bincount(flat_e, length=N_EXPERTS).astype(jnp.int32)
    starts = jnp.cumsum(counts) - counts
    padded = ((counts + MOE_BLOCK - 1) // MOE_BLOCK) * MOE_BLOCK
    pad_ends = jnp.cumsum(padded)
    pad_starts = pad_ends - padded
    dest = pad_starts[sorted_e] + (jnp.arange(n_assign, dtype=jnp.int32) - starts[sorted_e])
    buf_tok = jnp.full((cap,), n_tok, jnp.int32).at[dest].set(sorted_tok)
    x_pad = jnp.concatenate([xt, jnp.zeros((1, d_), xt.dtype)], axis=0)
    xb = x_pad[buf_tok].reshape(n_blocks, MOE_BLOCK, d_)
    block_e = jnp.minimum(jnp.searchsorted(pad_ends, jnp.arange(n_blocks, dtype=jnp.int32) * MOE_BLOCK, side='right'),
                          N_EXPERTS - 1)

    def expert_block(args):
        xblk, e = args
        gu = xblk @ w_gu[e].astype(xblk.dtype)
        act = jax.nn.silu(gu[:, :D_EXPERT]) * gu[:, D_EXPERT:]
        return act @ w_down[e].astype(xblk.dtype)

    yb = lax.map(expert_block, (xb, block_e)).reshape(cap, d_)
    contrib = yb[dest].astype(jnp.float32) * sorted_w[:, None]
    y = jax.ops.segment_sum(contrib, sorted_tok, num_segments=n_tok)
    return y.reshape(b_, s_, d_).astype(h.dtype)

def first_inputs(seed: int = 0) -> dict:
    key = jax.random.key(seed)
    ks = jax.random.split(key, 24)
    f32 = jnp.float32
    nrm = lambda k, shape, s: jax.random.normal(k, shape, f32) * s
    offs = jax.random.randint(ks[2], (BATCH, 1), 0, 4096, dtype=jnp.int32)
    positions = offs + jnp.arange(SEQ, dtype=jnp.int32)[None, :]
    f_bias = jnp.linspace(3.0, 6.0, A_HEADS, dtype=f32)[None, :] + nrm(ks[8], (N_LAYERS_A, A_HEADS), 0.1)
    i_bias = nrm(ks[9], (N_LAYERS_A, A_HEADS), 0.1)
    return {
        "x": nrm(ks[0], (BATCH, SEQ, D_MODEL), 1.0),
        "c": nrm(ks[1], (BATCH, D_MODEL), 1.0),
        "positions": positions,
        "norm1": 1.0 + nrm(ks[3], (DEPTH, D_MODEL), 0.02),
        "norm2": 1.0 + nrm(ks[4], (DEPTH, D_MODEL), 0.02),
        "w_ada": nrm(ks[5], (DEPTH, D_MODEL, 6 * D_MODEL), 0.5 * D_MODEL ** -0.5),
        "b_ada": nrm(ks[6], (DEPTH, 6 * D_MODEL), 0.02),
        "a_w_in": nrm(ks[7], (N_LAYERS_A, D_MODEL, A_IN_COLS), D_MODEL ** -0.5),
        "a_b_if": jnp.concatenate([i_bias, f_bias], axis=-1),
        "a_h_norm": 1.0 + nrm(ks[10], (N_LAYERS_A, A_HV), 0.02),
        "a_w_out": nrm(ks[11], (N_LAYERS_A, A_HV, D_MODEL), A_HV ** -0.5),
        "b_w_in": nrm(ks[12], (N_LAYERS_B, D_MODEL, B_IN_COLS), D_MODEL ** -0.5),
        "b_q_norm": 1.0 + nrm(ks[13], (N_LAYERS_B, B_HEAD_DIM), 0.02),
        "b_k_norm": 1.0 + nrm(ks[14], (N_LAYERS_B, B_HEAD_DIM), 0.02),
        "b_lam_q1": nrm(ks[15], (N_LAYERS_B, B_HEAD_DIM), 0.1),
        "b_lam_k1": nrm(ks[16], (N_LAYERS_B, B_HEAD_DIM), 0.1),
        "b_lam_q2": nrm(ks[17], (N_LAYERS_B, B_HEAD_DIM), 0.1),
        "b_lam_k2": nrm(ks[18], (N_LAYERS_B, B_HEAD_DIM), 0.1),
        "b_o_norm": 1.0 + nrm(ks[19], (N_LAYERS_B, B_V_DIM), 0.02),
        "b_w_out": nrm(ks[20], (N_LAYERS_B, D_MODEL, D_MODEL), D_MODEL ** -0.5),
        "w_router": nrm(ks[21], (D_MODEL, N_EXPERTS), D_MODEL ** -0.5),
        "router_bias": nrm(ks[22], (N_EXPERTS,), 0.01),
        "moe_w_gu": nrm(ks[23], (DEPTH, N_EXPERTS, D_MODEL, 2 * D_EXPERT), D_MODEL ** -0.5),
        "moe_w_down": nrm(jax.random.fold_in(key, 99), (DEPTH, N_EXPERTS, D_EXPERT, D_MODEL), D_EXPERT ** -0.5),
    }

def first_block(x, c, positions, norm1, norm2, w_ada, b_ada, a_w_in, a_b_if, a_h_norm, a_w_out,
              b_w_in, b_q_norm, b_k_norm, b_lam_q1, b_lam_k1, b_lam_q2, b_lam_k2, b_o_norm, b_w_out,
              w_router, router_bias, moe_w_gu, moe_w_down):
    c_act = jax.nn.silu(c.astype(jnp.float32))
    for l in range(DEPTH):
        mod = (c_act @ w_ada[l].astype(jnp.float32) + b_ada[l].astype(jnp.float32))[:, None, :]
        sh1, sc1, g1, sh2, sc2, g2 = jnp.split(mod, 6, axis=-1)
        h = (_rms(x, norm1[l]) * (1.0 + sc1) + sh1).astype(x.dtype)
        j = l // N_MIXERS
        if l % N_MIXERS == 0:
            y = _mlstm_mixer(h, a_w_in[j], a_b_if[j], a_h_norm[j], a_w_out[j])
        else:
            y = _diff_attention(h, positions, b_w_in[j], b_q_norm[j], b_k_norm[j], b_lam_q1[j], b_lam_k1[j],
                                b_lam_q2[j], b_lam_k2[j], b_o_norm[j], b_w_out[j], l)
        x = (x.astype(jnp.float32) + g1 * y.astype(jnp.float32)).astype(x.dtype)
        h = (_rms(x, norm2[l]) * (1.0 + sc2) + sh2).astype(x.dtype)
        y = _grouped_moe(h, w_router, router_bias, moe_w_gu[l], moe_w_down[l])
        x = (x.astype(jnp.float32) + g2 * y.astype(jnp.float32)).astype(x.dtype)
    return x


RW_HEADS = 8
RW_HEAD = 64
RW_DIM = RW_HEADS * RW_HEAD
RW_LORA_W = 64
RW_LORA_A = 64
RW_LORA_G = 128
RW_SPLITS = [RW_DIM, 2 * RW_DIM, 3 * RW_DIM, 3 * RW_DIM + RW_LORA_W,
             3 * RW_DIM + RW_LORA_W + RW_LORA_A]
SG_GROUPS = 4
SG_CHUNK = 128
SG_GROUP_DIM = 128
SG_DIM = SG_GROUPS * SG_GROUP_DIM
AB_SHIFT_DIM = 3 * RW_DIM + RW_LORA_W + RW_LORA_A + RW_LORA_G
AB_IN_DIM = AB_SHIFT_DIM + 2 * SG_DIM
AB_MIX_DIM = RW_DIM + SG_DIM

MLA_HEADS = 16
MLA_Q_RANK = 256
MLA_KV_RANK = 256
MLA_NOPE = 64
MLA_ROPE = 32
MLA_V = 64
MLA_QK = MLA_NOPE + MLA_ROPE
MLA_IN_DIM = MLA_Q_RANK + MLA_KV_RANK + MLA_ROPE
MLA_MIX_DIM = MLA_HEADS * MLA_V
ROPE_THETA_2 = 10000.0

MEM_LEN = 256
XA_HEADS = 4
XA_HEAD = D_MODEL // XA_HEADS

MOE_GROUPS = 4
MOE_PER_GROUP = 8
MOE_EXPERTS = MOE_GROUPS * MOE_PER_GROUP
MOE_TOPK = 2
MOE_FF = 512

DN_ALPHA = (2 * DEPTH) ** 0.25
DN_BETA = (8 * DEPTH) ** -0.25
LN_EPS = 1e-5
RMS_EPS = 1e-6
RW_GN_EPS = 64e-5
N_EVEN = (DEPTH + 1) // 2
N_ODD = DEPTH // 2


def _standardize(x, eps):
    xf = x.astype(jnp.float32)
    mu = jnp.mean(xf, -1, keepdims=True)
    var = jnp.mean(jnp.square(xf - mu), -1, keepdims=True)
    return ((xf - mu) * lax.rsqrt(var + eps)).astype(x.dtype)

def layer_norm(x, g, b, eps=LN_EPS):
    return _standardize(x, eps) * g + b

def rms_norm(x, g, eps=RMS_EPS):
    xf = x.astype(jnp.float32)
    return (xf * lax.rsqrt(jnp.mean(xf * xf, -1, keepdims=True) + eps)).astype(x.dtype) * g

def token_shift(p):
    return jnp.pad(p, ((0, 0), (1, 0), (0, 0)))[:, :-1]

def rwkv7_recurrence(r, w, k, v, kk, a):
    B, S, H, N = r.shape

    def step(state, inp):
        r_t, w_t, k_t, v_t, kk_t, a_t = inp
        sa = jnp.einsum('bhvk,bhk->bhv', state, -kk_t)
        state = (state * w_t[:, :, None, :]
                 + sa[..., None] * (kk_t * a_t)[:, :, None, :]
                 + v_t[..., None] * k_t[:, :, None, :])
        return state, jnp.einsum('bhvk,bhk->bhv', state, r_t)

    xs = tuple(jnp.moveaxis(t.astype(jnp.float32), 1, 0) for t in (r, w, k, v, kk, a))
    state0 = jnp.zeros((B, H, N, N), jnp.float32)
    _, y = lax.scan(step, state0, xs)
    return jnp.moveaxis(y, 0, 1)

def rwkv7_mix(p, w0, w2, a0, a2, g2, k_k, k_a, r_k, gn_g, gn_b):
    B, S, _ = p.shape
    heads = lambda t: t.reshape(B, S, RW_HEADS, RW_HEAD)
    r, k, v, w_lo, a_lo, g_lo = jnp.split(p, RW_SPLITS, axis=-1)
    w_log = -jax.nn.softplus(-(w0 + jnp.tanh(w_lo) @ w2)) - 0.5
    decay = jnp.exp(-jnp.exp(w_log.astype(jnp.float32)))
    a = jax.nn.sigmoid(a0 + a_lo @ a2)
    g = jax.nn.sigmoid(g_lo) @ g2
    kk = heads(k * k_k).astype(jnp.float32)
    kk = kk / jnp.maximum(jnp.sqrt(jnp.sum(kk * kk, -1, keepdims=True)), 1e-12)
    k = k * (1.0 + (a - 1.0) * k_a)
    r_h, k_h, v_h = heads(r), heads(k), heads(v)
    y = rwkv7_recurrence(r_h, heads(decay), k_h, v_h, kk, heads(a))
    y = _standardize(y, RW_GN_EPS).astype(p.dtype).reshape(B, S, RW_DIM) * gn_g + gn_b
    bonus = jnp.sum(r_h * k_h * r_k, -1, keepdims=True) * v_h
    return (y + bonus.reshape(B, S, RW_DIM)) * g

def spatial_gating(pu, pv, ln_g, ln_b, ws, bs):
    B, S, _ = pu.shape
    n_chunk = S // SG_CHUNK
    u = jax.nn.gelu(pu)
    z = jax.nn.gelu(pv).reshape(B, n_chunk, SG_CHUNK, SG_GROUPS, SG_GROUP_DIM)
    z = layer_norm(z, ln_g, ln_b)
    causal = jnp.tril(jnp.ones((SG_CHUNK, SG_CHUNK), dtype=bool))
    wm = jnp.where(causal, ws, jnp.zeros_like(ws))
    zs = jnp.einsum('gts,bcsgd->bctgd', wm, z) + bs.T[:, :, None]
    return u * zs.reshape(B, S, SG_DIM)

def mixer_ab(x, w_in, mu, w0, w2, a0, a2, g2, k_k, k_a, r_k, gn_g, gn_b,
             ln_g, ln_b, ws, bs, w_out):
    p = x @ w_in
    ps = p[..., :AB_SHIFT_DIM]
    pu = p[..., AB_SHIFT_DIM:AB_SHIFT_DIM + SG_DIM]
    pv = p[..., AB_SHIFT_DIM + SG_DIM:]
    ps = ps + (token_shift(ps) - ps) * mu
    ya = rwkv7_mix(ps, w0, w2, a0, a2, g2, k_k, k_a, r_k, gn_g, gn_b)
    yb = spatial_gating(pu, pv, ln_g, ln_b, ws, bs)
    return jnp.concatenate([ya, yb], axis=-1) @ w_out

def rope(x):
    S = x.shape[1]
    half = x.shape[-1] // 2
    inv = ROPE_THETA_2 ** (-jnp.arange(half, dtype=jnp.float32) / half)
    ang = jnp.arange(S, dtype=jnp.float32)[:, None] * inv[None, :]
    cos = jnp.cos(ang)[None, :, None, :]
    sin = jnp.sin(ang)[None, :, None, :]
    xf = x.astype(jnp.float32)
    x1, x2 = xf[..., :half], xf[..., half:]
    return jnp.concatenate([x1 * cos - x2 * sin, x1 * sin + x2 * cos], -1).astype(x.dtype)

def causal_block_attention(q, k, v):
    B, S, H, Dk = q.shape
    n_blk = S // Q_BLOCK
    scale = Dk ** -0.5
    qb = jnp.moveaxis(q.reshape(B, n_blk, Q_BLOCK, H, Dk), 1, 0)
    k_idx = jnp.arange(S)

    def one_block(args):
        q_blk, i = args
        s = jnp.einsum('bqhd,bkhd->bhqk', q_blk, k).astype(jnp.float32) * scale
        q_idx = i * Q_BLOCK + jnp.arange(Q_BLOCK)
        s = jnp.where(k_idx[None, :] <= q_idx[:, None], s, -jnp.inf)
        pr = jax.nn.softmax(s, axis=-1).astype(v.dtype)
        return jnp.einsum('bhqk,bkhd->bqhd', pr, v)

    o = lax.map(one_block, (qb, jnp.arange(n_blk)))
    return jnp.moveaxis(o, 0, 1).reshape(B, S, H, v.shape[-1])

def mla(x, w_in, q_norm, kv_norm, wq_b, wkv_b, w_out):
    B, S, _ = x.shape
    p = x @ w_in
    cq = p[..., :MLA_Q_RANK]
    ckv = p[..., MLA_Q_RANK:MLA_Q_RANK + MLA_KV_RANK]
    k_pe = p[..., MLA_Q_RANK + MLA_KV_RANK:]
    q = (rms_norm(cq, q_norm) @ wq_b).reshape(B, S, MLA_HEADS, MLA_QK)
    kv = (rms_norm(ckv, kv_norm) @ wkv_b).reshape(B, S, MLA_HEADS, MLA_NOPE + MLA_V)
    q_nope, q_pe = q[..., :MLA_NOPE], rope(q[..., MLA_NOPE:])
    k_nope, v = kv[..., :MLA_NOPE], kv[..., MLA_NOPE:]
    k_pe = rope(k_pe[:, :, None, :])
    qf = jnp.concatenate([q_nope, q_pe], -1)
    kf = jnp.concatenate([k_nope, jnp.broadcast_to(k_pe, (B, S, MLA_HEADS, MLA_ROPE))], -1)
    o = causal_block_attention(qf, kf, v)
    return o.reshape(B, S, MLA_MIX_DIM) @ w_out

def mem_cross_attention(x, mem, wq, wkv, wo):
    B, S, D = x.shape
    M = mem.shape[1]
    q = (x @ wq).reshape(B, S, XA_HEADS, XA_HEAD)
    kv = (mem @ wkv).reshape(B, M, 2, XA_HEADS, XA_HEAD)
    k, v = kv[:, :, 0], kv[:, :, 1]
    s = jnp.einsum('bqhd,bmhd->bhqm', q, k).astype(jnp.float32) * (XA_HEAD ** -0.5)
    pr = jax.nn.softmax(s, axis=-1).astype(v.dtype)
    o = jnp.einsum('bhqm,bmhd->bqhd', pr, v)
    return o.reshape(B, S, D) @ wo

def grouped_experts(xf, expert, gate, w_gate, w_up, w_down):
    T, D = xf.shape
    A = T * MOE_TOPK
    n_blk = -(-A // MOE_BLOCK) + MOE_EXPERTS
    L = n_blk * MOE_BLOCK
    flat_e = expert.reshape(-1)
    order = jnp.argsort(flat_e)
    sorted_e = flat_e[order]
    tok = (order // MOE_TOPK).astype(jnp.int32)
    counts = jnp.bincount(flat_e, length=MOE_EXPERTS)
    padded = (counts + MOE_BLOCK - 1) // MOE_BLOCK * MOE_BLOCK
    pad_end = jnp.cumsum(padded)
    pad_start = pad_end - padded
    start = jnp.cumsum(counts) - counts
    dest = (pad_start[sorted_e] + jnp.arange(A) - start[sorted_e]).astype(jnp.int32)
    row_tok = jnp.full((L,), T, dtype=jnp.int32).at[dest].set(tok)
    blk_expert = jnp.minimum(
        jnp.searchsorted(pad_end, jnp.arange(n_blk) * MOE_BLOCK, side='right'),
        MOE_EXPERTS - 1)
    x_rows = jnp.concatenate([xf, jnp.zeros((1, D), xf.dtype)], 0)[row_tok]
    x_rows = x_rows.reshape(n_blk, MOE_BLOCK, D)

    def expert_block(args):
        xb, e = args
        h = jax.nn.silu(xb @ w_gate[e]) * (xb @ w_up[e])
        return h @ w_down[e]

    y_rows = lax.map(expert_block, (x_rows, blk_expert)).reshape(L, D)
    y_assign = y_rows[dest] * gate.reshape(-1)[order][:, None]
    return jax.ops.segment_sum(y_assign, tok, num_segments=T)

def hier_moe(x, w_group, b_group, w_expert, b_expert, w_gate, w_up, w_down):
    B, S, D = x.shape
    xf = x.reshape(-1, D)
    T = xf.shape[0]
    g_logits = (xf @ w_group).astype(jnp.float32) + b_group
    g_prob = jax.nn.softmax(g_logits, axis=-1)
    grp = jnp.argmax(g_logits, axis=-1)
    p_grp = jnp.take_along_axis(g_prob, grp[:, None], axis=-1)
    e_logits = ((xf @ w_expert).astype(jnp.float32) + b_expert).reshape(
        T, MOE_GROUPS, MOE_PER_GROUP)
    e_logits = jnp.take_along_axis(e_logits, grp[:, None, None], axis=1)[:, 0]
    top_v, top_i = lax.top_k(e_logits, MOE_TOPK)
    gate = (jax.nn.softmax(top_v, axis=-1) * p_grp).astype(x.dtype)
    expert = (grp[:, None] * MOE_PER_GROUP + top_i).astype(jnp.int32)
    y = grouped_experts(xf, expert, gate, w_gate, w_up, w_down)
    return y.reshape(B, S, D)

def second_inputs(seed: int = 0) -> dict:
    key = jax.random.key(seed)
    ks = iter(jax.random.split(key, 48))

    def normal(shape, scale):
        return jax.random.normal(next(ks), shape, jnp.float32) * scale

    def gain(shape):
        return 1.0 + normal(shape, 0.02)

    D = D_MODEL
    NE, NO, L = N_EVEN, N_ODD, DEPTH
    return {
        'x': normal((BATCH, SEQ, D), 1.0),
        'mem': normal((BATCH, MEM_LEN, D), 1.0),
        'ab_w_in': normal((NE, D, AB_IN_DIM), D ** -0.5),
        'ab_mu': jax.random.uniform(next(ks), (NE, AB_SHIFT_DIM), jnp.float32),
        'rw_w0': jax.random.uniform(next(ks), (NE, RW_DIM), jnp.float32, -6.5, -1.5),
        'rw_w2': normal((NE, RW_LORA_W, RW_DIM), 0.5 * RW_LORA_W ** -0.5),
        'rw_a0': normal((NE, RW_DIM), 0.3),
        'rw_a2': normal((NE, RW_LORA_A, RW_DIM), RW_LORA_A ** -0.5),
        'rw_g2': normal((NE, RW_LORA_G, RW_DIM), RW_LORA_G ** -0.5),
        'rw_k_k': 0.85 + normal((NE, RW_DIM), 0.05),
        'rw_k_a': 1.0 + normal((NE, RW_DIM), 0.05),
        'rw_r_k': normal((NE, RW_HEADS, RW_HEAD), 0.1),
        'rw_gn_g': gain((NE, RW_DIM)),
        'rw_gn_b': normal((NE, RW_DIM), 0.02),
        'sg_ln_g': gain((NE, SG_GROUPS, SG_GROUP_DIM)),
        'sg_ln_b': normal((NE, SG_GROUPS, SG_GROUP_DIM), 0.02),
        'sg_ws': normal((NE, SG_GROUPS, SG_CHUNK, SG_CHUNK), 0.5 * SG_CHUNK ** -0.5),
        'sg_b': 1.0 + normal((NE, SG_GROUPS, SG_CHUNK), 0.1),
        'ab_w_out': normal((NE, AB_MIX_DIM, D), DN_BETA * AB_MIX_DIM ** -0.5),
        'mla_w_in': normal((NO, D, MLA_IN_DIM), D ** -0.5),
        'mla_q_norm': gain((NO, MLA_Q_RANK)),
        'mla_kv_norm': gain((NO, MLA_KV_RANK)),
        'mla_wq_b': normal((NO, MLA_Q_RANK, MLA_HEADS * MLA_QK), MLA_Q_RANK ** -0.5),
        'mla_wkv_b': normal((NO, MLA_KV_RANK, MLA_HEADS * (MLA_NOPE + MLA_V)), MLA_KV_RANK ** -0.5),
        'mla_w_out': normal((NO, MLA_MIX_DIM, D), DN_BETA * MLA_MIX_DIM ** -0.5),
        'ln1_g': gain((L, D)),
        'ln1_b': normal((L, D), 0.02),
        'xa_wq': normal((L, D, D), D ** -0.5),
        'xa_wkv': normal((L, D, 2 * D), D ** -0.5),
        'xa_wo': normal((L, D, D), DN_BETA * D ** -0.5),
        'ln2_g': gain((L, D)),
        'ln2_b': normal((L, D), 0.02),
        'moe_w_group': normal((L, D, MOE_GROUPS), D ** -0.5),
        'moe_b_group': normal((L, MOE_GROUPS), 0.01),
        'moe_w_expert': normal((L, D, MOE_EXPERTS), D ** -0.5),
        'moe_b_expert': normal((L, MOE_EXPERTS), 0.01),
        'moe_w_gate': normal((L, MOE_EXPERTS, D, MOE_FF), D ** -0.5),
        'moe_w_up': normal((L, MOE_EXPERTS, D, MOE_FF), D ** -0.5),
        'moe_w_down': normal((L, MOE_EXPERTS, MOE_FF, D), DN_BETA * MOE_FF ** -0.5),
        'ln3_g': gain((L, D)),
        'ln3_b': normal((L, D), 0.02),
    }

def second_block(x, mem, ab_w_in, ab_mu, rw_w0, rw_w2, rw_a0, rw_a2, rw_g2, rw_k_k,
              rw_k_a, rw_r_k, rw_gn_g, rw_gn_b, sg_ln_g, sg_ln_b, sg_ws, sg_b,
              ab_w_out, mla_w_in, mla_q_norm, mla_kv_norm, mla_wq_b, mla_wkv_b,
              mla_w_out, ln1_g, ln1_b, xa_wq, xa_wkv, xa_wo, ln2_g, ln2_b,
              moe_w_group, moe_b_group, moe_w_expert, moe_b_expert, moe_w_gate,
              moe_w_up, moe_w_down, ln3_g, ln3_b):
    h = x
    for layer in range(DEPTH):
        j = layer // 2
        if layer % 2 == 0:
            mix = mixer_ab(h, ab_w_in[j], ab_mu[j], rw_w0[j], rw_w2[j], rw_a0[j],
                           rw_a2[j], rw_g2[j], rw_k_k[j], rw_k_a[j], rw_r_k[j],
                           rw_gn_g[j], rw_gn_b[j], sg_ln_g[j], sg_ln_b[j], sg_ws[j],
                           sg_b[j], ab_w_out[j])
        else:
            mix = mla(h, mla_w_in[j], mla_q_norm[j], mla_kv_norm[j], mla_wq_b[j],
                      mla_wkv_b[j], mla_w_out[j])
        h = layer_norm(DN_ALPHA * h + mix, ln1_g[layer], ln1_b[layer])
        xa = mem_cross_attention(h, mem, xa_wq[layer], xa_wkv[layer], xa_wo[layer])
        h = layer_norm(DN_ALPHA * h + xa, ln2_g[layer], ln2_b[layer])
        ff = hier_moe(h, moe_w_group[layer], moe_b_group[layer], moe_w_expert[layer],
                      moe_b_expert[layer], moe_w_gate[layer], moe_w_up[layer],
                      moe_w_down[layer])
        h = layer_norm(DN_ALPHA * h + ff, ln3_g[layer], ln3_b[layer])
    return h


def setup_inputs(seed=0):
    out = dict(first_inputs(seed))
    for name, value in second_inputs(seed + 1).items():
        if name != "x":
            out[name + "_2"] = value
    return out


def reference(
    x, c, positions, norm1, norm2, w_ada, b_ada, a_w_in, a_b_if, a_h_norm, a_w_out, b_w_in,
    b_q_norm, b_k_norm, b_lam_q1, b_lam_k1, b_lam_q2, b_lam_k2, b_o_norm, b_w_out, w_router,
    router_bias, moe_w_gu, moe_w_down, mem_2, ab_w_in_2, ab_mu_2, rw_w0_2, rw_w2_2, rw_a0_2,
    rw_a2_2, rw_g2_2, rw_k_k_2, rw_k_a_2, rw_r_k_2, rw_gn_g_2, rw_gn_b_2, sg_ln_g_2, sg_ln_b_2,
    sg_ws_2, sg_b_2, ab_w_out_2, mla_w_in_2, mla_q_norm_2, mla_kv_norm_2, mla_wq_b_2,
    mla_wkv_b_2, mla_w_out_2, ln1_g_2, ln1_b_2, xa_wq_2, xa_wkv_2, xa_wo_2, ln2_g_2, ln2_b_2,
    moe_w_group_2, moe_b_group_2, moe_w_expert_2, moe_b_expert_2, moe_w_gate_2, moe_w_up_2,
    moe_w_down_2, ln3_g_2, ln3_b_2,
):
    x = first_block(
        x, c, positions, norm1, norm2, w_ada, b_ada, a_w_in, a_b_if, a_h_norm, a_w_out, b_w_in,
        b_q_norm, b_k_norm, b_lam_q1, b_lam_k1, b_lam_q2, b_lam_k2, b_o_norm, b_w_out, w_router,
        router_bias, moe_w_gu, moe_w_down,
    )
    return second_block(
        x, mem_2, ab_w_in_2, ab_mu_2, rw_w0_2, rw_w2_2, rw_a0_2, rw_a2_2, rw_g2_2, rw_k_k_2,
        rw_k_a_2, rw_r_k_2, rw_gn_g_2, rw_gn_b_2, sg_ln_g_2, sg_ln_b_2, sg_ws_2, sg_b_2,
        ab_w_out_2, mla_w_in_2, mla_q_norm_2, mla_kv_norm_2, mla_wq_b_2, mla_wkv_b_2,
        mla_w_out_2, ln1_g_2, ln1_b_2, xa_wq_2, xa_wkv_2, xa_wo_2, ln2_g_2, ln2_b_2,
        moe_w_group_2, moe_b_group_2, moe_w_expert_2, moe_b_expert_2, moe_w_gate_2, moe_w_up_2,
        moe_w_down_2, ln3_g_2, ln3_b_2,
    )


_drawn_inputs = setup_inputs


def setup_inputs(seed=0):
    import zlib

    import numpy as np

    out = dict(_drawn_inputs(seed))
    spreads = {}
    factors = {'a_h_norm': 3.146,
     'b_q_norm': 5.425,
     'b_k_norm': 7.773,
     'b_lam_k1': 2.699,
     'b_lam_k2': 3.351,
     'b_o_norm': 3.678,
     'rw_w2_2': 8.0,
     'rw_a0_2': 2.877,
     'rw_k_k_2': 8.0,
     'rw_k_a_2': 4.887,
     'rw_gn_g_2': 8.0,
     'rw_gn_b_2': 7.707,
     'sg_ln_g_2': 8.0,
     'sg_ln_b_2': 8.0,
     'sg_b_2': 2.749,
     'mla_q_norm_2': 8.0,
     'mla_kv_norm_2': 8.0,
     'moe_b_group_2': 8.0,
     'moe_b_expert_2': 8.0}
    for name, (base, spread) in spreads.items():
        noise = np.random.default_rng([zlib.crc32(name.encode()), seed]).standard_normal(out[name].shape)
        drawn = base * np.exp(spread * noise) if base else spread * noise
        out[name] = jnp.asarray(drawn.astype(out[name].dtype))
    for name, factor in factors.items():
        out[name] = (out[name] * factor).astype(out[name].dtype)
    return out
```

```python
from contextlib import ExitStack, contextmanager
import math

import numpy as np

import concourse.bass as bass
from concourse import mybir

F32 = mybir.dt.float32
I32 = mybir.dt.int32
ALU = mybir.AluOpType
ACT = mybir.ActivationFunctionType
AX_X = mybir.AxisListType.X

P = 128
D = 1024
KT = D // P
S = 256
TT = S // P
RING = 6
SLOT = 4096
BUF = 2048
NBUF = 10
BANK = 512
STAGE_SEM0 = 200

EPS = 1e-6
LN_EPS = 1e-5
GN_EPS = 64e-5
ALPHA = 4 ** 0.25
LAM_INIT = 0.8 - 0.6 * math.exp(-0.3 * 1)
NEG = -1e30
RC = 32
CAP1, CAP2 = 80, 64



def shape_constants():
    p = np.arange(P)
    c = {}
    c["ident"] = np.eye(P)
    c["ones"] = np.ones((P, P))
    c["ones64"] = (p[:, None] // 64 == p[None, :] // 64) * 1.0
    c["causal_add"] = np.where(p[:, None] >= p[None, :], 0.0, NEG)
    c["key_le"] = (p[:, None] <= p[None, :]) * 1.0
    c["key_lt"] = (p[:, None] < p[None, :]) * 1.0
    c["iota"] = np.broadcast_to(p[None, :], (P, P))
    same32 = p[:, None] // RC == p[None, :] // RC
    same16 = p[:, None] // 16 == p[None, :] // 16
    c["rw_d"] = (same16 & (p[:, None] > p[None, :])) * 1.0
    c["rw_dT"] = (same16 & (p[:, None] < p[None, :])) * 1.0
    c["rw_oT"] = (same32 & ~same16 & (p[:, None] < p[None, :])) * 1.0
    c["rw_ltT"] = (same32 & (p[:, None] < p[None, :])) * 1.0
    c["rw_leT"] = (same32 & (p[:, None] <= p[None, :])) * 1.0
    rot = np.zeros((P, P))
    for b in (0, 64):
        for i in range(8):
            rot[b + i + 8, b + i] = -1.0
            rot[b + i, b + i + 8] = 1.0
    c["rot_b"] = rot
    rot = np.zeros((P, P))
    for i in range(16):
        rot[64 + i + 16, 64 + i] = -1.0
        rot[64 + i, 64 + i + 16] = 1.0
    c["rot_m"] = rot
    sel = np.zeros((P, 4 * P))
    for h in range(4):
        sel[h, h * P:(h + 1) * P] = 1.0
    c["sel"] = sel
    inv = (np.float32(500000.0) ** (-np.arange(0, 16, 2, dtype=np.float32) / np.float32(16))).astype(np.float32)
    f = np.zeros(P, np.float32)
    for b in (0, 64):
        f[b:b + 8] = inv
        f[b + 8:b + 16] = inv
    c["inv_b"] = np.ascontiguousarray(np.broadcast_to(f[:, None], (P, 2)))
    inv = (np.float32(10000.0) ** (-np.arange(16, dtype=np.float32) / np.float32(16))).astype(np.float32)
    f = np.zeros(P, np.float32)
    f[64:80] = inv
    f[80:96] = inv
    ang = (np.arange(S, dtype=np.float32)[None, :] * f[:, None]).astype(np.float32)
    c["cos_m"] = np.cos(ang)
    c["sin_m"] = np.sin(ang)
    names, at, parts = {}, 0, []
    for k, v in c.items():
        names[k] = (at, v.shape[1])
        at += v.shape[1]
        parts.append(np.asarray(v, np.float32))
    return names, np.ascontiguousarray(np.concatenate(parts, axis=1))


VECTORS = [
    ("c", 8), ("norm1", 16), ("norm2", 16), ("b_ada", 96), ("a_h_norm", 8),
    ("b_q_norm", 1), ("b_k_norm", 1), ("b_o_norm", 1),
    ("ab_mu_2", 14), ("rw_w0_2", 4), ("rw_a0_2", 4), ("rw_k_k_2", 4), ("rw_k_a_2", 4),
    ("rw_r_k_2", 4), ("rw_gn_g_2", 4), ("rw_gn_b_2", 4),
    ("mla_q_norm_2", 2), ("mla_kv_norm_2", 2),
    ("ln1_g_2", 16), ("ln1_b_2", 16), ("ln2_g_2", 16), ("ln2_b_2", 16), ("ln3_g_2", 16), ("ln3_b_2", 16),
    ("b_if", 2),
]
VCOL = {}
_at = 0
for _n, _w in VECTORS:
    VCOL[_n] = (_at, _w)
    _at += _w
NVEC = _at

ROWS = [
    ("router_bias", 16), ("moe_b_group_2", 8), ("moe_b_expert_2", 64),
    ("lam", 256), ("sg_ln_g_2", 512), ("sg_ln_b_2", 512), ("sg_b_2", 512),
]
RCOL = {}
_at = 0
for _n, _w in ROWS:
    RCOL[_n] = (_at, _w)
    _at += _w
NROW = _at


@contextmanager
def stage(nc, tag, names):
    names = names.split()
    with ExitStack() as held:
        sems = [held.enter_context(nc.semaphore(f"{tag}_{n}", num=STAGE_SEM0 + i)) for i, n in enumerate(names)]
        with nc.Block() as block:
            yield (block, *sems)
        nc.all_engine_barrier(sems_to_clear=range(STAGE_SEM0, STAGE_SEM0 + len(names)))


def linker(eng, sem):
    count = [0]

    def link(ins):
        count[0] += 1
        ins.then_inc(sem, 1)
        eng.wait_ge(sem, count[0])
    return link


class Chip:

    def __init__(self, nc, t, ctx, cnames):
        self.nc, self.t = nc, t

        def sb(name, shape, dt=F32):
            return ctx.enter_context(nc.sbuf_tensor(name, shape, dt))

        self.ring = sb("ring", [P, RING, SLOT])
        self.X = sb("X", [P, KT, S])
        self.H = sb("H", [P, KT, S])
        self.big = sb("scratch", [P, NBUF * BUF])
        self.B = [self.big[:, i * BUF:(i + 1) * BUF] for i in range(NBUF)]
        self.PS = ctx.enter_context(nc.psum_tensor("PS", [P, 8, BANK], F32))
        self.vec = sb("vec", [P, NVEC])
        self.mod = sb("mod", [P, 48])
        self.small = sb("small", [P, 64])
        self.route = sb("route", [P, 132 + P])
        self.flag = sb("flag", [1, 1], I32)
        self.ident = sb("ident", [P, P])
        self.ones = sb("ones", [P, P])
        self.ones64 = sb("ones64", [P, P])
        self.consts = t["consts"]
        self.cnames = cnames
        self.slot_loaded = [ctx.enter_context(nc.semaphore(f"slot_loaded{i}")) for i in range(RING)]
        self.slot_free = [ctx.enter_context(nc.semaphore(f"slot_free{i}")) for i in range(RING)]
        self.plan = []
        self.used = 0

    def v(self, name, j=0, w=1):
        at, _ = VCOL[name]
        return self.vec[:, at + j:at + j + w]

    def const(self, name):
        at, w = self.cnames[name]
        return self.consts[:, at:at + w]

    def row(self, name, j=0, w=None):
        at, ww = RCOL[name]
        w = ww if w is None else w
        return self.t["rows"][0:1, at + j:at + j + w].to_broadcast([P, w])

    def unit(self, u):
        _, a, b = self.plan[u].shape
        return self.ring[:, u % RING, 0:a * b].rearrange("p (a b) -> p a b", b=b)

    def loaded(self, eng, u):
        eng.wait_ge(self.slot_loaded[u % RING], 16 * (u // RING + 1))

    def freed(self, u):
        return self.slot_free[u % RING]

    def load(self, sp, v):
        if v >= len(self.plan):
            return
        if v >= RING:
            sp.wait_ge(self.slot_free[v % RING], v // RING)
        sp.dma_start(self.unit(v), self.plan[v]).then_inc(self.slot_loaded[v % RING], 16)

    def refill(self, sp, u0, n):
        for u in range(u0, u0 + n):
            self.load(sp, u + RING)


def w_units(w, widths=None):
    k, n = w.shape
    v = w.rearrange("(k p) n -> p k n", p=P)
    out, at = [], 0
    widths = widths or [min(SLOT // (k // P), n)] * (n // min(SLOT // (k // P), n))
    for b in widths:
        out.append(v[:, :, at:at + b])
        at += b
    assert at == n
    return out


def load_small(C, tag, items):
    with stage(C.nc, tag, "landed") as (block, landed):
        @block.sync
        def _(sp):
            for dst, src in items:
                sp.dma_start(dst, src).then_inc(landed, 16)
            sp.wait_ge(landed, 16 * len(items))



def project(C, tag, tiles, units, evict, on="act", nb=4):
    nc = C.nc
    u0 = C.used
    last_of = {}
    for i, (u, _, _, _) in enumerate(tiles):
        if u is not None:
            last_of[u] = i
    with stage(nc, tag, "summed evicted") as (block, summed, evicted):
        @block.sync
        def _(sp):
            C.refill(sp, u0, units)

        @block.tensor
        def _(pe):
            seen = -1
            for i, (u, pairs, M, N) in enumerate(tiles):
                if u is not None and u > seen:
                    C.loaded(pe, u0 + u)
                    seen = u
                if i >= nb:
                    pe.wait_ge(evicted, i - nb + 1)
                for k, (lhsT, rhs) in enumerate(pairs):
                    last = nc.tensor.matmul(C.PS[0:M, i % nb, 0:N], lhsT, rhs,
                                            start=(k == 0), stop=(k == len(pairs) - 1))
                last.then_inc(summed, 1)

        def evictions(eng):
            for i, (u, _, M, N) in enumerate(tiles):
                eng.wait_ge(summed, i + 1)
                if u is not None and last_of[u] == i:
                    eng.sem_inc(C.freed(u0 + u), 1)
                evict(eng, i, C.PS[0:M, i % nb, 0:N]).then_inc(evicted, 1)

        if on == "act":
            @block.scalar
            def _(act):
                evictions(act)
        else:
            @block.vector
            def _(dve):
                evictions(dve)
    C.used += units


def cm_tiles(C, u, x, cols=None, m=P, kt=KT, at=0):
    w = C.unit(C.used + u)
    cols = cols or w.shape[2] - at
    return [(u, [(w[:, k, at + j * m:at + (j + 1) * m], x[:, k, :]) for k in range(kt)], m, S)
            for j in range(cols // m)]


def tm_tiles(C, u, x, kt=KT, cols=slice(None)):
    w = C.unit(C.used + u)
    return [(u, [(x[:, k, tt * P:(tt + 1) * P], w[:, k, cols]) for k in range(kt)], P, w[:, 0, cols].free_size())
            for tt in range(TT)]



def norm(C, tag, src, groups, per, mat, n, eps, sq, out, post, center=None, floor=None):
    nc = C.nc
    v = lambda x: x if len(x.shape) == 3 else x.rearrange("p (j t) -> p j t", t=S)
    src, sq = v(src), v(sq)
    with stage(nc, tag, "chain squared mean_sum square_sum variance root") as (
            block, chain, squared, mean_sum, square_sum, variance, root):
        sums = C.PS[:, 0:max(1, groups * S // BANK), :].rearrange("p b (h t) -> p (b h) t", t=S)

        @block.vector
        def _(dve):
            link = linker(dve, chain)
            x = src
            if center is not None:
                dve.wait_ge(mean_sum, 1)
                x = v(center)
                for g in range(groups):
                    for j in range(g * per, (g + 1) * per):
                        link(nc.vector.scalar_tensor_tensor(x[:, j, :], sums[:, g, :], -1.0 / n, src[:, j, :],
                                                            ALU.mult, ALU.add))
            nc.vector.tensor_tensor(sq[:, 0:groups * per, :], x[:, 0:groups * per, :],
                                    x[:, 0:groups * per, :], ALU.mult).then_inc(squared, 1)
            dve.wait_ge(square_sum, 1)
            nc.vector.tensor_scalar(out, sums[:, 0:groups, :], 1.0 / n, eps, ALU.mult, ALU.add).then_inc(variance, 1)
            dve.wait_ge(root, 1)
            if floor is not None:
                link(nc.vector.tensor_scalar(out, out, floor, None, ALU.max))
            link(nc.vector.reciprocal(out, out))
            post(link)

        @block.scalar
        def _(act):
            act.wait_ge(variance, 1)
            nc.scalar.activation(out, out, ACT.Sqrt).then_inc(root, 1)

        @block.tensor
        def _(pe):
            if center is not None:
                for g in range(groups):
                    for j in range(per):
                        last = nc.tensor.matmul(sums[:, g, :], mat, src[:, g * per + j, :],
                                                start=(j == 0), stop=(j == per - 1))
                last.then_inc(mean_sum, 1)
            pe.wait_ge(squared, 1)
            for g in range(groups):
                for j in range(per):
                    last = nc.tensor.matmul(sums[:, g, :], mat, sq[:, g * per + j, :],
                                            start=(j == 0), stop=(j == per - 1))
            last.then_inc(square_sum, 1)


def modulated_norm(C, tag, gain, shift, scale):
    nc = C.nc
    a = C.small[:, 0:KT]
    r = C.B[1][:, 0:S]

    def post(link):
        link(nc.vector.tensor_scalar(a, scale, 1.0, None, ALU.add))
        link(nc.vector.tensor_tensor(a, a, gain, ALU.mult))
        link(nc.vector.tensor_tensor(C.H[:, :, :], C.X[:, :, :], r.unsqueeze(1).to_broadcast([P, KT, S]), ALU.mult))
        for k in range(KT):
            link(nc.vector.tensor_scalar(C.H[:, k, :], C.H[:, k, :], a[:, k:k + 1], shift[:, k:k + 1],
                                         ALU.mult, ALU.add))
    norm(C, tag, C.X[:, :, :], 1, KT, C.ones[:, :], D, EPS, C.B[0], r.unsqueeze(1), post)


def layer_norm(C, tag, src, g, b):
    nc = C.nc
    r = C.B[1][:, 0:S]
    cen = C.B[2].rearrange("p (j t) -> p j t", t=S)

    def post(link):
        link(nc.vector.tensor_tensor(cen, cen, r.unsqueeze(1).to_broadcast([P, KT, S]), ALU.mult))
        for k in range(KT):
            link(nc.vector.tensor_scalar(C.X[:, k, :], cen[:, k, :], g[:, k:k + 1], b[:, k:k + 1],
                                         ALU.mult, ALU.add))
    norm(C, tag, src, 1, KT, C.ones[:, :], D, LN_EPS, C.B[0], r.unsqueeze(1), post, center=C.B[2])



def ada(C, tag, l):
    nc = C.nc
    u0, n = C.used, 12
    cact = C.small[:, 8:16]
    with stage(nc, tag, "cact ksum unit_done") as (block, c_ready, summed, unit_done):
        @block.sync
        def _(sp):
            C.refill(sp, u0, n)

        @block.scalar
        def _(act):
            nc.scalar.activation(cact, C.v("c", 0, 8), ACT.Silu).then_inc(c_ready, 1)

        @block.tensor
        def _(pe):
            pe.wait_ge(c_ready, 1)
            for u in range(n):
                C.loaded(pe, u0 + u)
                w = C.unit(u0 + u)
                for j in range(4):
                    for k in range(KT):
                        last = nc.tensor.matmul(C.PS[:, 0, 4 * u + j:4 * u + j + 1], w[:, k, j * P:(j + 1) * P],
                                                cact[:, k:k + 1], start=(k == 0), stop=(k == KT - 1))
                last.then_inc(C.freed(u0 + u), 1)
            last = nc.tensor.matmul(C.PS[:, 1, 0:1], C.ident[:, :], cact[:, 0:1], start=True, stop=True)
            last.then_inc(summed, 1)

        @block.vector
        def _(dve):
            dve.wait_ge(summed, 1)
            nc.vector.tensor_tensor(C.mod[:, :], C.PS[:, 0, 0:48], C.v("b_ada", 48 * l, 48), ALU.add)
    C.used += n


def add_residual(C, gate):
    def evict(dve, i, ps):
        return C.nc.vector.scalar_tensor_tensor(C.X[:, i, :], ps, gate[:, i:i + 1], C.X[:, i, :], ALU.mult, ALU.add)
    return evict


def add_alpha(C, dst):
    def evict(dve, i, ps):
        return C.nc.vector.scalar_tensor_tensor(dst[:, i, :], C.X[:, i, :], ALPHA, ps, ALU.mult, ALU.add)
    return evict



def attention(C, tag, items, scale, causal, maps, scores, values, combine, buf, mask):
    nc = C.nc
    dest, lam = combine
    n = len(items)
    W = maps * 2 * P
    T = [buf[:, i * W:(i + 1) * W].rearrange("p (m k) -> p m k", m=maps) for i in range(2)]
    at = 2 * W
    E = [buf[:, at + i * W:at + (i + 1) * W].rearrange("p (m k) -> p m k", m=maps) for i in range(2)]
    at += 2 * W
    PT = [buf[:, at + i * 2 * P:at + (i + 1) * 2 * P].rearrange("p (b q) -> p b q", b=2) for i in range(2)]
    at += 4 * P
    st = buf[:, at:at + 16]
    mx = [st[:, 4 * i:4 * i + maps] for i in range(2)]
    sm = [st[:, 8 + 4 * i:8 + 4 * i + maps] for i in range(2)]
    nks = [(qb + 1 if causal else TT) for _, qb in items]
    with stage(nc, tag, "chain scored biased expd probs transposed probs_T pv_done out") as (
            block, chain, scored, biased, expd, probs, transposed, probs_T, pv_done, out):

        @block.tensor
        def _(pe):
            for i in range(n + 2):
                if i < n:
                    h, qb = items[i]
                    if i >= 2:
                        pe.wait_ge(biased, i - 1)
                    for m in range(maps):
                        pairs = scores(h, m, qb, nks[i])
                        for k, (lhsT, rhs) in enumerate(pairs):
                            last = nc.tensor.matmul(C.PS[:, 6 * m + i % 2, 0:nks[i] * P], lhsT, rhs,
                                                    start=(k == 0), stop=(k == len(pairs) - 1))
                    last.then_inc(scored, 1)
                if 1 <= i <= n:
                    j = i - 1
                    pe.wait_ge(probs, j + 1)
                    if j >= 2:
                        pe.wait_ge(probs_T, j - 1)
                    for b in range(nks[j]):
                        last = nc.tensor.transpose(C.PS[:, 2 + j % 2, b * P:(b + 1) * P],
                                                   E[j % 2][:, 0, b * P:(b + 1) * P], C.ident[:, :])
                    last.then_inc(transposed, 1)
                if i >= 2:
                    j = i - 2
                    h, qb = items[j]
                    pe.wait_ge(probs_T, j + 1)
                    if j >= 2:
                        pe.wait_ge(out, j - 1)
                    parts = values(h, 0)
                    for x in range(len(parts)):
                        for b in range(nks[j]):
                            vv, M, col = values(h, b)[x]
                            last = nc.tensor.matmul(C.PS[0:M, 4 + j % 2, col * P:(col + 1) * P], vv,
                                                    PT[j % 2][:, b, :], start=(b == 0), stop=(b == nks[j] - 1))
                    last.then_inc(pv_done, 1)

        @block.vector
        def _(dve):
            link = linker(dve, chain)
            for i in range(n + 1):
                if i < n:
                    qb, nk = items[i][1], nks[i]
                    dve.wait_ge(scored, i + 1)
                    if i >= 2:
                        dve.wait_ge(expd, i - 1)
                    for m in range(maps):
                        free = (nk - 1) * P if causal else nk * P
                        if free:
                            link(nc.vector.tensor_scalar(T[i % 2][:, m, 0:free], C.PS[:, 6 * m + i % 2, 0:free], scale, None, ALU.mult))
                        if causal:
                            link(nc.vector.scalar_tensor_tensor(T[i % 2][:, m, free:free + P], C.PS[:, 6 * m + i % 2, free:free + P],
                                                                scale, mask, ALU.mult, ALU.add))
                    link(nc.vector.tensor_reduce(mx[i % 2], T[i % 2][:, :, 0:nk * P], AX_X, ALU.max))
                    link(nc.vector.tensor_scalar(mx[i % 2], mx[i % 2], -1.0, None, ALU.mult))
                    dve.sem_inc(biased, 1)
                if i >= 1:
                    j = i - 1
                    e, s = E[j % 2], sm[j % 2]
                    w = nks[j] * P
                    dve.wait_ge(expd, j + 1)
                    link(nc.vector.reciprocal(s, s))
                    if maps == 2:
                        link(nc.vector.tensor_scalar(e[:, 1, 0:w], e[:, 1, 0:w], s[:, 1:2], lam, ALU.mult, ALU.mult))
                        link(nc.vector.scalar_tensor_tensor(e[:, 0, 0:w], e[:, 0, 0:w], s[:, 0:1], e[:, 1, 0:w],
                                                            ALU.mult, ALU.subtract))
                    else:
                        link(nc.vector.tensor_scalar(e[:, 0, 0:w], e[:, 0, 0:w], s[:, 0:1], None, ALU.mult))
                    dve.sem_inc(probs, 1)

        @block.scalar
        def _(act):
            for i in range(n + 2):
                if i < n:
                    act.wait_ge(biased, i + 1)
                    if i >= 2:
                        act.wait_ge(transposed, i - 1)
                    for m in range(maps):
                        last = nc.scalar.activation(E[i % 2][:, m, 0:nks[i] * P], T[i % 2][:, m, 0:nks[i] * P], ACT.Exp,
                                                    bias=mx[i % 2][:, m:m + 1], accum_out=sm[i % 2][:, m:m + 1])
                    last.then_inc(expd, 1)
                if 1 <= i <= n:
                    j = i - 1
                    act.wait_ge(transposed, j + 1)
                    if j >= 2:
                        act.wait_ge(pv_done, j - 1)
                    nc.scalar.copy(PT[j % 2][:, 0:nks[j], :],
                                   C.PS[:, 2 + j % 2, 0:nks[j] * P].rearrange("p (b q) -> p b q", q=P)).then_inc(probs_T, 1)
                if i >= 2:
                    j = i - 2
                    h, qb = items[j]
                    act.wait_ge(pv_done, j + 1)
                    _, M, _ = values(h, 0)[0]
                    parts = len(values(h, 0))
                    nc.scalar.copy(dest(h, qb), C.PS[0:M, 4 + j % 2, 0:parts * P].rearrange(
                        "p (b q) -> p b q", b=parts)).then_inc(out, 1)


def tiles3(x, j0=0, n=KT):
    return x[:, j0 * S:(j0 + n) * S].rearrange("p (j t) -> p j t", t=S)



def mlstm(C):
    nc, t = C.nc, C.t
    Q, K_ = tiles3(C.B[0], 0, 4), tiles3(C.B[0], 4, 4)
    V = C.B[1].rearrange("p (t v) -> p t v", t=TT)
    O = tiles3(C.B[2])
    NUM = tiles3(C.B[3])
    misc = C.B[4]
    wg = misc[:, 0:64].rearrange("p (k n) -> p k n", n=8)
    sel = misc[0:4, 64:64 + 512].rearrange("p (h m) -> p h m", h=4)
    key_le = misc[:, 576:704]
    key_le_row = key_le
    B5 = C.B[5]
    gi, gf, tmp, ones4 = (B5[0:4, i * S:(i + 1) * S] for i in range(4))
    u, negm, emt, bc = (B5[0:4, (4 + i) * S:(5 + i) * S] for i in range(4))
    ucol = misc[:, 704:712]
    load_small(C, "mlc", [(wg, t["a_w_in"].rearrange("(k p) n -> p k n", p=P)[:, :, 3072:3080]),
                          (sel, C.const("sel")[0:4, :].rearrange("p (h m) -> p h m", h=4)),
                          (key_le, C.const("key_le"))])

    tiles = cm_tiles(C, 0, C.H) + cm_tiles(C, 1, C.H) + tm_tiles(C, 2, C.H) + tm_tiles(C, 3, C.H) \
        + cm_tiles(C, 4, C.H) + cm_tiles(C, 5, C.H) \
        + [(None, [(wg[:, k, 4 * g:4 * g + 4], C.H[:, k, :]) for k in range(KT)], 4, S) for g in range(2)]

    def evict(act, i, ps):
        if i < 4:
            return nc.scalar.copy(Q[:, i, :], ps)
        if i < 8:
            return nc.scalar.mul(K_[:, i - 4, :], ps, 128 ** -0.5)
        if i < 12:
            a, tt = divmod(i - 8, 2)
            return nc.scalar.copy(V[:, tt, a * 512:(a + 1) * 512], ps)
        if i < 20:
            return nc.scalar.activation(O[:, i - 12, :], ps, ACT.Sigmoid)
        return nc.scalar.activation((gi, gf)[i - 20], ps, ACT.Identity, bias=C.v("b_if", i - 20)[0:4, :])
    project(C, "ml_in", tiles, 6, evict)

    with stage(nc, "ml_gate", "chain abs_z log1p u_ready u_T") as (block, chain, abs_z, log1p, u_ready, u_T):
        @block.vector
        def _(dve):
            link = linker(dve, chain)
            link(nc.vector.memset(ones4, 1.0))
            link(nc.vector.scalar_tensor_tensor(tmp, gf, -1.0, gf, ALU.mult, ALU.max))
            dve.sem_inc(abs_z, 1)
            dve.wait_ge(log1p, 2)
            link(nc.vector.scalar_tensor_tensor(tmp, gf, 0.0, tmp, ALU.min, ALU.subtract))
            link(nc.vector.tensor_tensor_scan(bc, ones4, tmp, 0.0, ALU.mult, ALU.add))
            link(nc.vector.tensor_tensor(u, gi, bc, ALU.subtract))
            dve.sem_inc(u_ready, 1)
            link(nc.vector.tensor_tensor_scan(negm, ones4, u, 0.0, ALU.mult, ALU.max))
            link(nc.vector.tensor_scalar(negm, negm, -1.0, None, ALU.mult))
            link(nc.vector.tensor_tensor(emt, negm, bc, ALU.subtract))
            dve.wait_ge(u_T, 1)
            link(nc.vector.tensor_copy(ucol, C.PS[:, 0, 0:8]))
            dve.sem_inc(u_ready, 1)

        @block.scalar
        def _(act):
            act.wait_ge(abs_z, 1)
            nc.scalar.activation(tmp, tmp, ACT.Exp, scale=-1.0).then_inc(log1p, 1)
            act.wait_ge(log1p, 1)
            nc.scalar.activation(tmp, tmp, ACT.Ln, bias=1.0).then_inc(log1p, 1)
            act.wait_ge(u_ready, 2)
            nc.scalar.activation(emt, emt, ACT.Exp)

        @block.tensor
        def _(pe):
            pe.wait_ge(u_ready, 1)
            for tt in range(TT):
                last = nc.tensor.transpose(C.PS[:, 0, 4 * tt:4 * tt + 4], u[:, tt * P:(tt + 1) * P], C.ident[0:4, 0:4])
            last.then_inc(u_T, 1)

    Dm = [tiles3(C.B[6], 2 * i, 2) for i in range(2)]
    Wm = [tiles3(C.B[6], 4 + 2 * i, 2) for i in range(2)]
    r = C.B[7][:, 0:S]
    dn = C.B[7][:, S:2 * S]
    with stage(nc, "ml_mix", "chain bcast clamped expd scored weighted summed taken") as (
            block, chain, bcast, clamped, expd, scored, weighted, summed, taken):
        @block.tensor
        def _(pe):
            for h in range(4):
                if h:
                    pe.wait_ge(taken, h)
                nc.tensor.matmul(C.PS[:, 0, 0:S], sel[:, h, :], negm, start=True, stop=True)
                nc.tensor.matmul(C.PS[:, 1, 0:S], sel[:, h, :], emt, start=True, stop=True).then_inc(bcast, 1)
                for st in range(TT):
                    last = nc.tensor.matmul(C.PS[:, 2 + st, 0:S], K_[:, h, st * P:(st + 1) * P], Q[:, h, :],
                                            start=True, stop=True)
                last.then_inc(scored, 1)
                pe.wait_ge(weighted, h + 1)
                w = Wm[h % 2]
                for st in range(TT):
                    nc.tensor.matmul(C.PS[:, 4, 0:S], C.ones[:, :], w[:, st, :], start=(st == 0), stop=(st == 1))
                for vt in range(2):
                    for st in range(TT):
                        last = nc.tensor.matmul(C.PS[:, 5 + vt, 0:S], V[:, st, h * 256 + vt * P:h * 256 + (vt + 1) * P],
                                                w[:, st, :], start=(st == 0), stop=(st == 1))
                last.then_inc(summed, 1)

        @block.vector
        def _(dve):
            link = linker(dve, chain)
            for h in range(4):
                d, w = Dm[h % 2], Wm[h % 2]
                dve.wait_ge(bcast, h + 1)
                for st in range(TT):
                    link(nc.vector.tensor_scalar(d[:, st, :], C.PS[:, 0, 0:S], ucol[:, 4 * st + h:4 * st + h + 1], 0.0,
                                                 ALU.add, ALU.min))
                dve.sem_inc(clamped, 1)
                dve.wait_ge(expd, h + 1)
                dve.wait_ge(scored, h + 1)
                for st in range(TT):
                    link(nc.vector.tensor_tensor(d[:, st, st * P:(st + 1) * P], d[:, st, st * P:(st + 1) * P], key_le, ALU.mult))
                link(nc.vector.memset(d[:, 1, 0:P], 0.0))
                for st in range(TT):
                    link(nc.vector.tensor_tensor(w[:, st, :], C.PS[:, 2 + st, 0:S], d[:, st, :], ALU.mult))
                dve.sem_inc(weighted, 1)
                dve.wait_ge(summed, h + 1)
                link(nc.vector.tensor_copy(r, C.PS[:, 4, 0:S]))
                link(nc.vector.scalar_tensor_tensor(dn, r, -1.0, r, ALU.mult, ALU.max))
                link(nc.vector.tensor_tensor(dn, dn, C.PS[:, 1, 0:S], ALU.max))
                link(nc.vector.reciprocal(r, dn))
                for vt in range(2):
                    link(nc.vector.tensor_tensor(NUM[:, 2 * h + vt, :], C.PS[:, 5 + vt, 0:S], r, ALU.mult))
                dve.sem_inc(taken, 1)

        @block.scalar
        def _(act):
            for h in range(4):
                act.wait_ge(clamped, h + 1)
                nc.scalar.activation(Dm[h % 2], Dm[h % 2], ACT.Exp).then_inc(expd, 1)

    R4 = tiles3(C.B[5], 0, 4)

    def post(link):
        for j in range(8):
            link(nc.vector.scalar_tensor_tensor(NUM[:, j, :], NUM[:, j, :], C.v("a_h_norm", j), R4[:, j // 2, :],
                                                ALU.mult, ALU.mult))
        link(nc.vector.tensor_tensor(NUM, NUM, O, ALU.mult))
    norm(C, "ml_norm", NUM, 4, 2, C.ones[:, :], 256, EPS, C.B[4], R4, post)
    tiles = cm_tiles(C, 0, NUM) + cm_tiles(C, 1, NUM)
    project(C, "ml_out", tiles, 2, add_residual(C, C.mod[:, 16:24]), on="dve")



def diff_attention(C):
    nc, t = C.nc, C.t
    Q, K_ = tiles3(C.B[0]), tiles3(C.B[1])
    V = C.B[2].rearrange("p (t v) -> p t v", t=TT)
    O = tiles3(C.B[3])
    m = C.B[9]
    rot, mask, inv = m[:, 0:P], m[:, P:2 * P], m[:, 256:257]
    cos, sin, ang, k = (m[:, 512 + i * S:512 + (i + 1) * S] for i in range(4))
    posi = m[:, 1536:1792].bitcast(I32)
    lamr = m[:, 1792:2048]
    lam = C.small[:, 16:24]
    load_small(C, "dac", [(rot, C.const("rot_b")), (mask, C.const("causal_add")), (m[:, 256:258], C.const("inv_b")),
                          (posi, t["positions"].to_broadcast([P, S])), (lamr, C.row("lam"))])

    tiles = sum([cm_tiles(C, u, C.H) for u in range(4)], []) + tm_tiles(C, 4, C.H) + tm_tiles(C, 5, C.H)

    def evict(act, i, ps):
        if i < 8:
            return nc.scalar.copy(Q[:, i, :], ps)
        if i < 16:
            return nc.scalar.copy(K_[:, i - 8, :], ps)
        a, tt = divmod(i - 16, 2)
        return nc.scalar.copy(V[:, tt, a * 512:(a + 1) * 512], ps)
    project(C, "da_in", tiles, 6, evict)

    c1 = 6.28125
    c2 = float(np.float32(np.round((2 * math.pi - c1) * 2 ** 21) / 2 ** 21))
    c3 = float(np.float32(2 * math.pi - c1 - c2))
    half = float(np.nextafter(np.float32(math.pi), np.float32(0)))
    with stage(nc, "da_rope", "chain reduced sines lam_sum lam_exp") as (block, chain, reduced, sines, lam_sum, lam_exp):
        @block.vector
        def _(dve):
            link = linker(dve, chain)
            link(nc.vector.tensor_copy(ang, posi))
            link(nc.vector.tensor_scalar(ang, ang, inv, None, ALU.mult))
            link(nc.vector.tensor_scalar(k, ang, 1 / (2 * math.pi), 12582912.0, ALU.mult, ALU.add))
            link(nc.vector.tensor_scalar(k, k, 12582912.0, None, ALU.subtract))
            for c in (c1, c2, c3):
                link(nc.vector.scalar_tensor_tensor(ang, k, -c, ang, ALU.mult, ALU.add))
            link(nc.vector.tensor_scalar(ang, ang, half, -half, ALU.min, ALU.max))
            link(nc.vector.scalar_tensor_tensor(k, ang, -1.0, ang, ALU.mult, ALU.max))
            link(nc.vector.tensor_scalar(k, k, -1.0, math.pi / 2, ALU.mult, ALU.add))
            dve.sem_inc(reduced, 1)
            for i in range(2):
                a, b = lamr[:, 128 * i:128 * i + 64], lamr[:, 128 * i + 64:128 * i + 128]
                link(nc.vector.tensor_tensor(a, a, b, ALU.mult))
                link(nc.vector.tensor_reduce(lam[:, i:i + 1], a, AX_X, ALU.add))
            dve.sem_inc(lam_sum, 1)
            dve.wait_ge(lam_exp, 1)
            link(nc.vector.tensor_scalar(lam[:, 4:5], lam[:, 2:3], lam[:, 3:4], LAM_INIT, ALU.subtract, ALU.add))
            link(nc.vector.tensor_scalar(C.small[:, 24:25], C.v("b_o_norm"), 1.0 - LAM_INIT, None, ALU.mult))

        @block.scalar
        def _(act):
            act.wait_ge(reduced, 1)
            nc.scalar.activation(sin, ang, ACT.Sin)
            nc.scalar.activation(cos, k, ACT.Sin)
            act.wait_ge(lam_sum, 1)
            nc.scalar.activation(lam[:, 2:4], lam[:, 0:2], ACT.Exp).then_inc(lam_exp, 1)

    R8 = tiles3(C.B[5])
    for name, X in (("q", Q), ("k", K_)):
        def post(link):
            link(nc.vector.scalar_tensor_tensor(X, X, C.v(f"b_{name}_norm"), R8, ALU.mult, ALU.mult))
        norm(C, f"da_{name}n", X, 8, 1, C.ones64[:, :], 64, EPS, C.B[4], R8, post)
        rope(C, f"da_{name}r", X, rot, cos, sin, C.B[4], P)

    attention(C, "da_att", [(h, qb) for h in range(8) for qb in range(TT)], 64 ** -0.5, True, 2,
              lambda h, mm, qb, nk: [(Q[64 * mm:64 * mm + 64, h, qb * P:(qb + 1) * P], K_[64 * mm:64 * mm + 64, h, 0:nk * P])],
              lambda h, kb: [(V[:, kb, h * P:(h + 1) * P], P, 0)],
              (lambda h, qb: O[:, h:h + 1, qb * P:(qb + 1) * P], lam[:, 4:5]), C.big[:, 5 * BUF:7 * BUF], mask)

    def post(link):
        link(nc.vector.scalar_tensor_tensor(O, O, C.small[:, 24:25], R8, ALU.mult, ALU.mult))
    norm(C, "da_on", O, 8, 1, C.ones[:, :], P, EPS, C.B[4], R8, post)
    project(C, "da_out", cm_tiles(C, 0, O) + cm_tiles(C, 1, O), 2, add_residual(C, C.mod[:, 16:24]), on="dve")


def rope(C, tag, X, rot, cos, sin, tmp, rows):
    nc = C.nc
    T = tiles3(tmp)
    rows = slice(0, rows)
    with stage(nc, tag, "chain turned") as (block, chain, turned):
        @block.tensor
        def _(pe):
            for j in range(8):
                last = nc.tensor.matmul(C.PS[rows, j // 2, (j % 2) * S:(j % 2 + 1) * S], rot[rows, rows], X[rows, j, :],
                                        start=True, stop=True)
            last.then_inc(turned, 1)

        @block.vector
        def _(dve):
            link = linker(dve, chain)
            dve.wait_ge(turned, 1)
            n = rows.stop
            ps = C.PS[rows, 0:4, :].rearrange("p b (h t) -> p (b h) t", t=S)
            link(nc.vector.tensor_tensor(T[rows, :, :], ps, sin[rows, :].unsqueeze(1).to_broadcast([n, 8, S]), ALU.mult))
            link(nc.vector.tensor_tensor(X[rows, :, :], X[rows, :, :], cos[rows, :].unsqueeze(1).to_broadcast([n, 8, S]), ALU.mult))
            link(nc.vector.tensor_tensor(X[rows, :, :], X[rows, :, :], T[rows, :, :], ALU.add))



def mla(C):
    nc, t = C.nc, C.t
    QS = [tiles3(C.B[0]), tiles3(C.B[1])]
    KS = [tiles3(C.B[2]), tiles3(C.B[3])]
    V = C.B[4].rearrange("p (t v) -> p t v", t=TT)
    CQ, CKV = tiles3(C.B[5], 0, 2), tiles3(C.B[5], 2, 2)
    kpe = C.B[5][:, 4 * S:5 * S]
    R = C.B[5][:, 5 * S:6 * S]
    O = tiles3(C.B[6])
    m = C.B[9]
    rot, mask = m[:, 0:P], m[:, P:2 * P]
    cos, sin = m[:, 256:512], m[:, 512:768]
    load_small(C, "mlac", [(rot, C.const("rot_m")), (mask, C.const("causal_add")), (cos, C.const("cos_m")),
                           (sin, C.const("sin_m"))])
    tiles = cm_tiles(C, 0, C.X) + cm_tiles(C, 1, C.X, m=96)

    def evict(act, i, ps):
        if i < 4:
            return nc.scalar.copy((CQ if i < 2 else CKV)[:, i % 2, :], ps)
        return nc.scalar.copy(kpe[0:96, :], ps)
    project(C, "mla_in", tiles, 2, evict)
    for name, X, w in (("q", CQ, "mla_q_norm_2"), ("kv", CKV, "mla_kv_norm_2")):
        def post(link):
            for j in range(2):
                link(nc.vector.scalar_tensor_tensor(X[:, j, :], X[:, j, :], C.v(w, j), R, ALU.mult, ALU.mult))
        norm(C, f"mla_{name}n", X, 1, 2, C.ones[:, :], 256, EPS, C.B[7], R.unsqueeze(1), post)

    wkv = C.unit(C.used + 1)
    tiles = cm_tiles(C, 0, CQ, m=96, kt=2) \
        + [(1, [(wkv[:, k, h * P:h * P + 64], CKV[:, k, :]) for k in range(2)], 64, S) for h in range(16)] \
        + [(1, [(CKV[:, k, tt * P:(tt + 1) * P],
                 wkv[:, k, g * 1024:(g + 1) * 1024].rearrange("p (h c) -> p h c", c=P)[:, :, 64:128]) for k in range(2)],
            P, 512) for g in range(2) for tt in range(TT)]

    def evict(act, i, ps):
        if i < 16:
            return nc.scalar.copy(QS[i // 8][0:96, i % 8, :], ps)
        if i < 32:
            return nc.scalar.copy(KS[(i - 16) // 8][0:64, i % 8, :], ps)
        g, tt = divmod(i - 32, 2)
        return nc.scalar.copy(V[:, tt, g * 512:(g + 1) * 512], ps)
    project(C, "mla_qkv", tiles, 2, evict)
    with stage(nc, "mla_kpe", "chain") as (block, chain):
        @block.vector
        def _(dve):
            for g in range(2):
                nc.vector.tensor_copy(KS[g][64:96, :, :], kpe[64:96, :].unsqueeze(1).to_broadcast([32, 8, S]))
    for g in range(2):
        rope(C, f"mla_rq{g}", QS[g], rot, cos, sin, C.B[7], 96)
        rope(C, f"mla_rk{g}", KS[g], rot, cos, sin, C.B[7], 96)
    attention(C, "mla_att", [(h, qb) for h in range(16) for qb in range(TT)], 96 ** -0.5, True, 1,
              lambda h, mm, qb, nk: [(QS[h // 8][0:96, h % 8, qb * P:(qb + 1) * P], KS[h // 8][0:96, h % 8, 0:nk * P])],
              lambda h, kb: [(V[:, kb, h * 64:(h + 1) * 64], 64, 0)],
              (lambda h, qb: O[64 * (h % 2):64 * (h % 2) + 64, h // 2:h // 2 + 1, qb * P:(qb + 1) * P], None),
              C.big[:, 7 * BUF:9 * BUF], mask)
    T = tiles3(C.B[0])
    project(C, "mla_out", cm_tiles(C, 0, O) + cm_tiles(C, 1, O), 2, add_alpha(C, T), on="dve")
    return T



def cross_attention(C, tag):
    nc = C.nc
    M = tiles3(C.B[0])
    Q, K_ = tiles3(C.B[1]), tiles3(C.B[2])
    V = C.B[3].rearrange("p (t v) -> p t v", t=TT)
    O = tiles3(C.B[4])
    load_small(C, tag + "m", [(M, C.t["mem_T"])])
    tiles = cm_tiles(C, 0, C.X) + cm_tiles(C, 1, C.X) + cm_tiles(C, 2, M) + cm_tiles(C, 3, M) \
        + tm_tiles(C, 4, M) + tm_tiles(C, 5, M)

    def evict(act, i, ps):
        if i < 8:
            return nc.scalar.copy(Q[:, i, :], ps)
        if i < 16:
            return nc.scalar.copy(K_[:, i - 8, :], ps)
        a, tt = divmod(i - 16, 2)
        return nc.scalar.copy(V[:, tt, a * 512:(a + 1) * 512], ps)
    project(C, tag + "in", tiles, 6, evict)
    attention(C, tag + "att", [(h, qb) for h in range(4) for qb in range(TT)], 256 ** -0.5, False, 1,
              lambda h, mm, qb, nk: [(Q[:, 2 * h + k, qb * P:(qb + 1) * P], K_[:, 2 * h + k, :]) for k in range(2)],
              lambda h, kb: [(V[:, kb, h * 256 + x * P:h * 256 + (x + 1) * P], P, x) for x in range(2)],
              (lambda h, qb: O[:, 2 * h:2 * h + 2, qb * P:(qb + 1) * P], None), C.big[:, 5 * BUF:7 * BUF], None)
    T = tiles3(C.B[0])
    project(C, tag + "out", cm_tiles(C, 0, O) + cm_tiles(C, 1, O), 2, add_alpha(C, T), on="dve")
    return T



class Moe:

    def __init__(self, C, E, cap):
        self.E, self.cap = E, cap
        self.htok = C.B[6].rearrange("p (t d) -> p t d", t=TT)
        self.yacc = tiles3(C.B[7])
        b = C.big[:, 8 * BUF:10 * BUF]
        self.xg = b[:, 0:8 * cap].rearrange("p (k c) -> p k c", k=KT)
        self.yg = b[0:cap, 1024:2048]
        self.gT = [b[0:cap, 2048 + i * S:2048 + (i + 1) * S] for i in range(2)]
        self.sil = b[:, 2560:2560 + 4 * cap]
        self.act = b[:, 3072:3072 + 4 * cap]
        self.pick = b[:, 3584:3584 + 2 * cap].rearrange("p (t c) -> p t c", t=TT)
        self.pick_w = b[:, 3840:3840 + 2 * cap].rearrange("p (t c) -> p t c", t=TT)
        w = E + 1
        self.rank = C.route[:, 0:2 * w].rearrange("p (t e) -> p t e", t=TT)
        self.gate = C.route[:, 2 * w:4 * w].rearrange("p (t e) -> p t e", t=TT)
        self.iota = C.route[:, 132:132 + P]
        self.flag = C.flag
        self.ow = (C.big[:, 0:4096].rearrange("p (k n) -> p k n", k=KT),
                   C.big[:, 4096:8192].rearrange("p (k n) -> p k n", k=KT),
                   C.big[:, 8192:12288].rearrange("p (k n) -> p k n", k=4))


def pick_first(nc, link, v, iota1, hot, tmp, mx, shape):
    link(nc.vector.tensor_reduce(mx, v, AX_X, ALU.max))
    link(nc.vector.tensor_tensor(tmp, v, mx.unsqueeze(2).to_broadcast(shape), ALU.is_equal))
    link(nc.vector.scalar_tensor_tensor(tmp, tmp, -1000.0, iota1.unsqueeze(1).to_broadcast(shape), ALU.mult, ALU.add))
    link(nc.vector.tensor_reduce(mx, tmp, AX_X, ALU.min))
    link(nc.vector.tensor_tensor(hot, tmp, mx.unsqueeze(2).to_broadcast(shape), ALU.is_equal))


def route(C, tag, M, X, w_router, rows, hier):
    nc = C.nc
    E, G = M.E, 4
    per = E // G
    NL = E + G if hier else E
    b = C.B[0]
    wr = b[:, 0:KT * NL].rearrange("p (k n) -> p k n", k=KT)
    br = b[:, 288:288 + NL]
    lt = b[:, 384:384 + P]
    o = [512]

    def take(n, w=None):
        at = o[0]
        o[0] += TT * n
        return b[:, at:at + TT * n].rearrange("p (t n) -> p t n", t=TT)
    lg, sc = take(NL), take(NL)
    tmp, h1, h2, mk, sel, gs = take(E), take(E), take(E), take(E), take(E), take(E)
    pair = take(24)
    gtmp, ghot = take(G), take(G)
    mx, s1, s2, s3 = (take(1).rearrange("p t n -> p (t n)") for _ in range(4))
    cnt = take(E)
    load_small(C, tag + "c", [(wr[:, :, a:a + w.shape[1]], w.rearrange("(k p) n -> p k n", p=P)) for a, w in w_router]
               + rows(br) + [(lt, C.const("key_lt")), (M.iota, C.const("iota"))])
    iota1 = C.small[:, 32:32 + E]
    ghot_in = b[:, 1900:1912]
    sh, gsh = [P, TT, E], [P, TT, G]
    with stage(nc, tag, "chain logits sig chosen ranks ex") as (block, chain, logits, sig, chosen, ranks, ex):
        @block.tensor
        def _(pe):
            for tt in range(TT):
                for k in range(KT):
                    last = nc.tensor.matmul(C.PS[:, tt, 0:NL], X[:, k, tt * P:(tt + 1) * P], wr[:, k, :],
                                            start=(k == 0), stop=(k == KT - 1))
            last.then_inc(logits, 1)
            for tt in range(TT):
                for k in range(KT):
                    last = nc.tensor.transpose(C.PS[:, 4 + 2 * tt + k // 4, (k % 4) * P:(k % 4 + 1) * P],
                                               X[:, k, tt * P:(tt + 1) * P], C.ident[:, :])
            last.then_inc(logits, 1)
            pe.wait_ge(chosen, 1)
            nc.tensor.matmul(C.PS[:, 2, 0:E], lt, sel[:, 0, :], start=True, stop=True)
            nc.tensor.matmul(C.PS[:, 2, 64:64 + E], lt, sel[:, 1, :], start=True, stop=False)
            nc.tensor.matmul(C.PS[:, 2, 64:64 + E], C.ones[:, :], sel[:, 0, :], start=False, stop=True)
            for tt in range(TT):
                last = nc.tensor.matmul(C.PS[:, 3, 0:E], C.ones[:, :], sel[:, tt, :], start=(tt == 0), stop=(tt == 1))
            last.then_inc(ranks, 1)

        @block.scalar
        def _(act):
            act.wait_ge(logits, 1)
            lps = C.PS[:, 0:2, 0:NL]
            if hier:
                nc.scalar.copy(lg, lps).then_inc(sig, 1)
            else:
                nc.scalar.activation(lg, lps, ACT.Sigmoid).then_inc(sig, 1)
            act.wait_ge(logits, 2)
            for tt in range(TT):
                nc.scalar.copy(M.htok[:, tt, :], C.PS[:, 4 + 2 * tt:6 + 2 * tt, :].rearrange("p b n -> p (b n)"))
            if hier:
                act.wait_ge(ex, 1)
                nc.scalar.activation(ghot_in[:, 0:10], ghot_in[:, 0:10], ACT.Exp).then_inc(sig, 1)

        @block.vector
        def _(dve):
            link = linker(dve, chain)
            dve.wait_ge(sig, 1)
            link(nc.vector.tensor_scalar(iota1, M.iota[:, 0:E], 1001.0, None, ALU.add))
            link(nc.vector.tensor_tensor(sc, lg, br.unsqueeze(1).to_broadcast([P, TT, NL]), ALU.add))
            if hier:
                gsc, esc = sc[:, :, 0:G], sc[:, :, G:NL]
            else:
                esc = sc
                gsc = gtmp
                v = sc.rearrange("p t (g e) -> p (t g) e", e=per)
                pv = pair.rearrange("p t n -> p (t n)")[:, 0:48].rearrange("p (g n) -> p g n", n=6)
                TG = TT * G
                link(nc.vector.tensor_tensor(pv[:, :, 0:3], v[:, :, 1:4], v[:, :, 0:1].to_broadcast([P, TG, 3]), ALU.add))
                link(nc.vector.tensor_tensor(pv[:, :, 3:5], v[:, :, 2:4], v[:, :, 1:2].to_broadcast([P, TG, 2]), ALU.add))
                link(nc.vector.tensor_tensor(pv[:, :, 5:6], v[:, :, 3:4], v[:, :, 2:3], ALU.add))
                link(nc.vector.tensor_reduce(gsc.rearrange("p t g -> p (t g)"), pv, AX_X, ALU.max))
            gt = gs[:, :, 0:G]
            if hier:
                link(nc.vector.tensor_reduce(s3, gsc, AX_X, ALU.max))
                gin = ghot_in[:, 0:8].rearrange("p (t g) -> p t g", t=TT)
                link(nc.vector.tensor_tensor(gin, gsc, s3.unsqueeze(2).to_broadcast(gsh), ALU.subtract))
            pick_first(nc, link, gsc, iota1[:, 0:G], ghot, gt, mx, gsh)
            link(nc.vector.tensor_scalar(gt, ghot, 1.0, -NEG, ALU.subtract, ALU.mult))
            for tt in range(TT):
                g3 = lambda x: x[:, tt, :].rearrange("p (g e) -> p g e", e=per)
                link(nc.vector.tensor_tensor(g3(mk), g3(esc), ghot[:, tt, :].unsqueeze(2).to_broadcast([P, G, per]), ALU.mult))
                link(nc.vector.tensor_tensor(g3(mk), g3(mk), gt[:, tt, :].unsqueeze(2).to_broadcast([P, G, per]), ALU.add))
            if hier:
                link(nc.vector.tensor_reduce(s1, mk, AX_X, ALU.max))
            pick_first(nc, link, mk, iota1, h1, tmp, mx, sh)
            link(nc.vector.scalar_tensor_tensor(mk, h1, 2 * NEG, mk, ALU.mult, ALU.add))
            if hier:
                link(nc.vector.tensor_reduce(s2, mk, AX_X, ALU.max))
                link(nc.vector.tensor_tensor(ghot_in[:, 8:10], s2, s1, ALU.subtract))
                dve.sem_inc(ex, 1)
            pick_first(nc, link, mk, iota1, h2, tmp, mx, sh)
            link(nc.vector.tensor_tensor(sel, h1, h2, ALU.add))
            dve.sem_inc(chosen, 1)
            link(nc.vector.memset(M.gate[:, :, E:E + 1], 0.0))
            link(nc.vector.memset(M.rank[:, :, E:E + 1], -1.0))
            gate = M.gate[:, :, 0:E]
            if hier:
                dve.wait_ge(sig, 2)
                e2 = ghot_in[:, 8:10]
                link(nc.vector.tensor_reduce(s1, ghot_in[:, 0:8].rearrange("p (t g) -> p t g", t=TT), AX_X, ALU.add))
                link(nc.vector.tensor_scalar(s2, e2, 1.0, None, ALU.add))
                link(nc.vector.tensor_tensor(s1, s1, s2, ALU.mult))
                link(nc.vector.reciprocal(s1, s1))
                link(nc.vector.tensor_tensor(s2, s1, e2, ALU.mult))
                link(nc.vector.tensor_tensor(gate, h1, s1.unsqueeze(2).to_broadcast(sh), ALU.mult))
                link(nc.vector.tensor_tensor(tmp, h2, s2.unsqueeze(2).to_broadcast(sh), ALU.mult))
                link(nc.vector.tensor_tensor(gate, gate, tmp, ALU.add))
            else:
                link(nc.vector.tensor_tensor(tmp, lg, sel, ALU.mult))
                link(nc.vector.tensor_reduce(s1, tmp, AX_X, ALU.add))
                link(nc.vector.reciprocal(s1, s1))
                link(nc.vector.tensor_tensor(gate, tmp, s1.unsqueeze(2).to_broadcast(sh), ALU.mult))
            dve.wait_ge(ranks, 1)
            rank = M.rank[:, :, 0:E]
            link(nc.vector.scalar_tensor_tensor(tmp, C.PS[:, 2, 0:128].rearrange("p (t n) -> p t n", t=TT)[:, :, 0:E], 1.0,
                                                sel, ALU.add, ALU.mult))
            link(nc.vector.tensor_scalar(rank, tmp, -1.0, None, ALU.add))
            link(nc.vector.tensor_reduce(mx[:, 0:1], C.PS[:, 3, 0:E], AX_X, ALU.max))
            link(nc.vector.tensor_scalar(mx[:, 0:1], mx[:, 0:1], float(M.cap), None, ALU.is_gt))
            link(nc.vector.tensor_copy(M.flag[:, :], mx[0:1, 0:1]))


def build_pick(nc, M, e, done):
    col = bass.ds(e, 1)
    for tt in range(TT):
        nc.vector.tensor_scalar(M.pick[:, tt, :], M.iota[:, 0:M.cap], M.rank[:, tt, col], None, ALU.is_equal)
        last = nc.vector.tensor_scalar(M.pick_w[:, tt, :], M.iota[:, 0:M.cap], M.rank[:, tt, col], M.gate[:, tt, col],
                                       ALU.is_equal, ALU.mult)
    last.then_inc(done, 1)


def gather(C, M, done):
    nc, cap = C.nc, M.cap
    for k in range(KT):
        for tt in range(TT):
            nc.tensor.matmul(C.PS[:, k // 4, (k % 4) * cap:(k % 4 + 1) * cap], M.htok[:, tt, k * P:(k + 1) * P],
                             M.pick[:, tt, :], start=(tt == 0), stop=(tt == 1))
    for tt in range(TT):
        last = nc.tensor.transpose(C.PS[0:cap, 2, tt * P:(tt + 1) * P], M.pick_w[:, tt, :], C.ident[:, :])
    last.then_inc(done, 1)


def up_product(C, M, w, bank):
    nc, cap = C.nc, M.cap
    for f in range(4):
        for k in range(KT):
            last = nc.tensor.matmul(C.PS[:, bank, f * cap:(f + 1) * cap], w[:, k, f * P:(f + 1) * P], M.xg[:, k, :],
                                    start=(k == 0), stop=(k == KT - 1))
    return last


def down_product(C, M, w, half, bank):
    nc, cap = C.nc, M.cap
    for f in range(4):
        last = nc.tensor.matmul(C.PS[0:cap, bank, :], M.act[:, f * cap:(f + 1) * cap], w[:, f, half * 512:(half + 1) * 512],
                                start=(f == 0), stop=(f == 3))
    return last


def scatter_quarter(C, M, q, gT, bank):
    nc = C.nc
    for j in range(2):
        d = 2 * q + j
        last = nc.tensor.matmul(C.PS[:, bank, j * S:(j + 1) * S], M.yg[:, d * P:(d + 1) * P], gT, start=True, stop=True)
    return last


def take_gathered(C, M, gT, done):
    nc, cap = C.nc, M.cap
    for g in range(2):
        nc.scalar.copy(M.xg[:, 4 * g:4 * g + 4, :], C.PS[:, g, 0:4 * cap].rearrange("p (k c) -> p k c", c=cap))
    nc.scalar.copy(gT, C.PS[0:cap, 2, 0:S]).then_inc(done, 1)


def accumulate(C, M, q, bank, done):
    nc = C.nc
    y = M.yacc[:, 2 * q:2 * q + 2, :].rearrange("p j t -> p (j t)")
    nc.vector.tensor_tensor(y, y, C.PS[:, bank, :], ALU.add).then_inc(done, 1)


def experts(C, tag, M, sources):
    nc = C.nc
    E, u0 = M.E, C.used
    pairs = E // 2
    SB = (7, 5, 6, 7)
    names = "picked gathered taken gate_done up_done silu_done act_ready down_done y_taken scattered added"
    with stage(nc, tag, names) as (block, picked, gathered, taken, gate_done, up_done, silu_done, act_ready,
                                   down_done, y_taken, scattered, added):
        @block.sync
        def _(sp):
            with sp.Fori(0, pairs - 1) as i:
                for j in range(6):
                    v = u0 + RING + j
                    src = sources[j % 3](2 * i + (2 + j // 3))
                    sp.wait_ge(C.slot_free[v % RING], i + v // RING)
                    sp.dma_start(C.unit(v), src).then_inc(C.slot_loaded[v % RING], 16)
            C.refill(sp, u0 + 6 * (pairs - 1), 6)

        @block.tensor
        def _(pe):
            pe.wait_ge(picked, 1)
            gather(C, M, gathered)
            with pe.Fori(0, pairs) as i:
                for h in range(2):
                    e = 2 * i + h
                    u = u0 + 3 * h
                    pe.wait_ge(taken, e + 1)
                    pe.wait_ge(C.slot_loaded[u % RING], i * 16 + 16 * (u // RING + 1))
                    up_product(C, M, C.unit(u), 3).then_inc(gate_done, 1)
                    u += 1
                    pe.wait_ge(C.slot_loaded[u % RING], i * 16 + 16 * (u // RING + 1))
                    up_product(C, M, C.unit(u), 4).then_inc(up_done, 1)
                    pe.wait_ge(y_taken, 2 * e + 1)
                    pe.wait_ge(added, 4 * e + 1)
                    for q in range(4):
                        if q == 3:
                            pe.wait_ge(added, 4 * e + 2)
                        scatter_quarter(C, M, q, M.gT[1 - h], SB[q]).then_inc(scattered, 1)
                    pe.wait_ge(picked, e + 2)
                    gather(C, M, gathered)
                    u += 1
                    pe.wait_ge(act_ready, e + 1)
                    pe.wait_ge(added, 4 * e + 4)
                    pe.wait_ge(C.slot_loaded[u % RING], i * 16 + 16 * (u // RING + 1))
                    down_product(C, M, C.unit(u), 0, 5).then_inc(down_done, 1)
                    down_product(C, M, C.unit(u), 1, 6).then_inc(down_done, 1)
            pe.wait_ge(y_taken, 2 * E + 1)
            pe.wait_ge(added, 4 * E + 1)
            for q in range(4):
                if q == 3:
                    pe.wait_ge(added, 4 * E + 2)
                scatter_quarter(C, M, q, M.gT[1], SB[q]).then_inc(scattered, 1)

        @block.scalar
        def _(act):
            act.wait_ge(gathered, 1)
            take_gathered(C, M, M.gT[0], taken)
            with act.Fori(0, pairs) as i:
                for h in range(2):
                    e = 2 * i + h
                    act.wait_ge(gate_done, e + 1)
                    act.sem_inc(C.freed(u0 + 3 * h), 1)
                    nc.scalar.activation(M.sil, C.PS[:, 3, 0:4 * M.cap], ACT.Silu).then_inc(silu_done, 1)
                    act.wait_ge(gathered, e + 2)
                    take_gathered(C, M, M.gT[1 - h], taken)
                    for half in range(2):
                        act.wait_ge(down_done, 2 * e + (half + 1))
                        if half:
                            act.sem_inc(C.freed(u0 + 3 * h + 2), 1)
                        nc.scalar.copy(M.yg[:, half * 512:(half + 1) * 512], C.PS[0:M.cap, 5 + half, :]).then_inc(y_taken, 1)

        @block.vector
        def _(dve):
            nc.vector.memset(M.yg, 0.0).then_inc(y_taken, 1)
            nc.vector.memset(M.gT[1], 0.0)
            nc.vector.memset(M.yacc, 0.0).then_inc(added, 1)
            build_pick(nc, M, 0, picked)
            with dve.Fori(0, pairs) as i:
                for h in range(2):
                    e = 2 * i + h
                    dve.wait_ge(gathered, e + 1)
                    build_pick(nc, M, e + 1, picked)
                    dve.wait_ge(silu_done, e + 1)
                    dve.wait_ge(up_done, e + 1)
                    dve.sem_inc(C.freed(u0 + 3 * h + 1), 1)
                    nc.vector.tensor_tensor(M.act, M.sil, C.PS[:, 4, 0:4 * M.cap], ALU.mult).then_inc(act_ready, 1)
                    for q in range(4):
                        dve.wait_ge(scattered, 4 * e + (q + 1))
                        accumulate(C, M, q, SB[q], added)
            for q in range(4):
                dve.wait_ge(scattered, 4 * E + q + 1)
                accumulate(C, M, q, SB[q], added)
    C.used += 6 * pairs


def experts_overflow(C, tag, M, sources):
    nc = C.nc
    E, blocks = M.E, -(-S // M.cap) - 1
    names = "loaded picked gathered taken up_done silu_done act_ready down_done y_taken scattered added"
    with stage(nc, tag, names) as (block, loaded, picked, gathered, taken, up_done, silu_done, act_ready, down_done,
                                   y_taken, scattered, added):
        def over_experts(eng, body, before=None):
            more = eng.value_load(M.flag[0:1, 0:1])
            with eng.If(more > 0):
                with eng.Fori(0, blocks) as b:
                    if before:
                        before(b)
                    with eng.Fori(0, E) as e:
                        body(b * E + e, e)

        @block.sync
        def _(sp):
            def body(n, e):
                srcs = [s(e) for s in sources]
                sp.wait_ge(down_done, n + 1)
                for dst, src in zip(M.ow, srcs):
                    sp.dma_start(dst, src).then_inc(loaded, 16)
            over_experts(sp, body)

        @block.tensor
        def _(pe):
            pe.sem_inc(down_done, 1)

            def body(n, e):
                pe.wait_ge(added, n + 1)
                pe.wait_ge(picked, n + 1)
                gather(C, M, gathered)
                pe.wait_ge(taken, n + 1)
                pe.wait_ge(loaded, n * 48 + 48)
                up_product(C, M, M.ow[0], 3)
                up_product(C, M, M.ow[1], 4).then_inc(up_done, 1)
                pe.wait_ge(act_ready, n + 1)
                down_product(C, M, M.ow[2], 0, 5)
                down_product(C, M, M.ow[2], 1, 6).then_inc(down_done, 1)
                pe.wait_ge(y_taken, n + 1)
                for q in range(4):
                    last = scatter_quarter(C, M, q, M.gT[0], q)
                last.then_inc(scattered, 1)
            over_experts(pe, body)

        @block.scalar
        def _(act):
            def body(n, e):
                act.wait_ge(gathered, n + 1)
                take_gathered(C, M, M.gT[0], taken)
                act.wait_ge(up_done, n + 1)
                nc.scalar.activation(M.sil, C.PS[:, 3, 0:4 * M.cap], ACT.Silu).then_inc(silu_done, 1)
                act.wait_ge(down_done, n + 2)
                nc.scalar.copy(M.yg, C.PS[0:M.cap, 5:7, :].rearrange("p b n -> p (b n)")).then_inc(y_taken, 1)
            over_experts(act, body)

        @block.vector
        def _(dve):
            dve.sem_inc(added, 1)

            def before(b):
                dve.wait_ge(added, b * E + 1)
                nc.vector.tensor_scalar(M.rank, M.rank, -float(M.cap), None, ALU.add)
                dve.drain()

            def body(n, e):
                build_pick(nc, M, e, picked)
                dve.wait_ge(silu_done, n + 1)
                nc.vector.tensor_tensor(M.act, M.sil, C.PS[:, 4, 0:4 * M.cap], ALU.mult).then_inc(act_ready, 1)
                dve.wait_ge(scattered, n + 1)
                y = M.yacc.rearrange("p j t -> p (j t)")
                nc.vector.tensor_tensor(y, y, C.PS[:, 0:4, :].rearrange("p b n -> p (b n)"), ALU.add).then_inc(added, 1)
            over_experts(dve, body, before)


def moe1(C, tag, l):
    t = C.t
    M = Moe(C, 16, CAP1)
    route(C, tag + "r", M, C.H, [(0, t["w_router"])], lambda br: [(br, C.row("router_bias"))], False)
    gu = t["moe_w_gu"][l].rearrange("e (k p) n -> e p k n", p=P)
    dn = t["moe_w_down"][l].rearrange("e (k p) n -> e p k n", p=P)
    src = (lambda e: gu[e, :, :, 0:512], lambda e: gu[e, :, :, 512:1024], lambda e: dn[e])
    experts(C, tag + "e", M, src)
    experts_overflow(C, tag + "o", M, src)
    nc = C.nc
    with stage(nc, tag + "x", "done") as (block, done):
        @block.vector
        def _(dve):
            for k in range(KT):
                nc.vector.scalar_tensor_tensor(C.X[:, k, :], M.yacc[:, k, :], C.mod[:, 40 + k:41 + k], C.X[:, k, :],
                                               ALU.mult, ALU.add)


def moe2(C, tag, l):
    t = C.t
    M = Moe(C, 32, CAP2)
    route(C, tag + "r", M, C.X, [(0, t["moe_w_group_2"][l]), (4, t["moe_w_expert_2"][l])],
          lambda br: [(br[:, 0:4], C.row("moe_b_group_2", 4 * l, 4)), (br[:, 4:36], C.row("moe_b_expert_2", 32 * l, 32))], True)
    v = lambda w: w[l].rearrange("e (k p) n -> e p k n", p=P)
    g, u, d = v(t["moe_w_gate_2"]), v(t["moe_w_up_2"]), v(t["moe_w_down_2"])
    src = (lambda e: g[e], lambda e: u[e], lambda e: d[e])
    experts(C, tag + "e", M, src)
    experts_overflow(C, tag + "o", M, src)
    T = M.yacc
    nc = C.nc
    with stage(nc, tag + "x", "done") as (block, done):
        @block.vector
        def _(dve):
            nc.vector.scalar_tensor_tensor(T, C.X[:, :, :], ALPHA, T, ALU.mult, ALU.add)
    return T



def spatial_gating(C, U, Z, out):
    nc, t = C.nc, C.t
    W = C.B[3]
    ws = W[:, 0:512].rearrange("p (g t) -> p g t", g=4)
    lng, lnb = W[:, 512:1024], W[:, 1024:1536]
    bs = W[:, 1536:2048].rearrange("p (g t) -> p g t", g=4)
    q = C.B[4][:, 0:1024]
    le = C.B[4][:, 1024:1152]
    mean, var = C.B[4][:, 1152:1160], C.B[4][:, 1160:1168]
    load_small(C, "sgc", [(ws, t["sg_ws_T"]), (lng, C.row("sg_ln_g_2")), (lnb, C.row("sg_ln_b_2")),
                          (W[:, 1536:2048], C.row("sg_b_2")), (le, C.const("key_le"))])
    z = Z.rearrange("p t (g c) -> p (t g) c", g=4)
    q3 = q.rearrange("p (a c) -> p a c", c=P)
    full = lambda x: x.unsqueeze(2).to_broadcast([P, 8, P])
    with stage(nc, "sg", "chain var root gained mixed") as (block, chain, var_done, root, gained, mixed):
        @block.vector
        def _(dve):
            link = linker(dve, chain)
            link(nc.vector.tensor_tensor(ws, ws, le.unsqueeze(1).to_broadcast([P, 4, P]), ALU.mult))
            link(nc.vector.tensor_reduce(mean, z, AX_X, ALU.add))
            link(nc.vector.tensor_scalar(mean, mean, 1.0 / P, None, ALU.mult))
            link(nc.vector.tensor_tensor(z, z, full(mean), ALU.subtract))
            link(nc.vector.tensor_tensor(q3, z, z, ALU.mult))
            link(nc.vector.tensor_reduce(var, q3, AX_X, ALU.add))
            link(nc.vector.tensor_scalar(var, var, 1.0 / P, LN_EPS, ALU.mult, ALU.add))
            dve.sem_inc(var_done, 1)
            dve.wait_ge(root, 1)
            link(nc.vector.reciprocal(var, var))
            link(nc.vector.tensor_tensor(z, z, full(var), ALU.mult))
            for tt in range(TT):
                link(nc.vector.tensor_tensor(Z[:, tt, :], Z[:, tt, :], lng, ALU.mult))
                link(nc.vector.tensor_tensor(Z[:, tt, :], Z[:, tt, :], lnb, ALU.add))
            dve.sem_inc(gained, 1)
            dve.wait_ge(mixed, 1)
            for g in range(4):
                for tt in range(TT):
                    i = 2 * g + tt
                    c = slice(tt * P, (tt + 1) * P)
                    link(nc.vector.tensor_tensor(q3[:, i, :], C.PS[:, i // 4, (i % 4) * P:(i % 4 + 1) * P], bs[:, g, :], ALU.add))
                    link(nc.vector.tensor_tensor(out[:, g, c], q3[:, i, :], U[:, g, c], ALU.mult))

        @block.scalar
        def _(act):
            act.wait_ge(var_done, 1)
            nc.scalar.activation(var, var, ACT.Sqrt).then_inc(root, 1)

        @block.tensor
        def _(pe):
            pe.wait_ge(gained, 1)
            for g in range(4):
                for tt in range(TT):
                    i = 2 * g + tt
                    last = nc.tensor.matmul(C.PS[:, i // 4, (i % 4) * P:(i % 4 + 1) * P], Z[:, tt, g * P:(g + 1) * P],
                                            ws[:, g, :], start=True, stop=True)
            last.then_inc(mixed, 1)


def mixer_ab(C):
    nc, t = C.nc, C.t
    B = C.B
    half = lambda b, i: tiles3(b, 4 * i, 4)
    PR = C.big[:, 0:14 * S].rearrange("p (j t) -> p j t", t=S)
    DF = C.big[:, 3 * BUF:3 * BUF + 14 * S].rearrange("p (j t) -> p j t", t=S)
    U = half(B[2], 0)
    Z = B[2][:, 1024:2048].rearrange("p (t c) -> p t c", t=TT)
    MIX = tiles3(B[9])

    tiles = sum([cm_tiles(C, u, C.X) for u in range(5)], []) + tm_tiles(C, 5, C.X)

    def evict(act, i, ps):
        if i < 14:
            return nc.scalar.copy(PR[:, i, :], ps)
        if i < 18:
            return nc.scalar.activation(U[:, i - 14, :], ps, ACT.Gelu_apprx_tanh)
        return nc.scalar.activation(Z[:, i - 18, :], ps, ACT.Gelu_apprx_tanh)
    project(C, "ab_in", tiles, 6, evict)
    spatial_gating(C, U, Z, MIX[:, 4:8, :])

    w2, g2 = B[5][:, 0:512], B[5][:, 512:1024]
    load_small(C, "rwc", [(w2[0:64, :], t["rw_w2_2"]), (w2[64:128, :], t["rw_a2_2"]), (g2, t["rw_g2_2"])])
    with stage(nc, "rw_shift", "chain shifted") as (block, chain, shifted):
        @block.vector
        def _(dve):
            link = linker(dve, chain)
            link(nc.vector.tensor_tensor(DF[:, :, 1:S], PR[:, :, 0:S - 1], PR[:, :, 1:S], ALU.subtract))
            link(nc.vector.tensor_scalar(DF[:, :, 0:1], PR[:, :, 0:1], -1.0, None, ALU.mult))
            for j in range(14):
                link(nc.vector.scalar_tensor_tensor(PR[:, j, :], DF[:, j, :], C.v("ab_mu_2", j), PR[:, j, :],
                                                    ALU.mult, ALU.add))
            dve.sem_inc(shifted, 1)

        @block.scalar
        def _(act):
            act.wait_ge(shifted, 1)
            nc.scalar.activation(PR[0:64, 12, :], PR[0:64, 12, :], ACT.Tanh)
            nc.scalar.activation(PR[:, 13, :], PR[:, 13, :], ACT.Sigmoid)
    r, k, v = PR[:, 0:4, :], PR[:, 4:8, :], PR[:, 8:12, :]
    A, G = half(B[3], 0), half(B[3], 1)
    LW, CS = half(B[4], 0), half(B[4], 1)
    tiles = [(None, [(w2[0:64, j * P:(j + 1) * P], PR[0:64, 12, :])], P, S) for j in range(4)] \
        + [(None, [(w2[64:128, j * P:(j + 1) * P], PR[64:128, 12, :])], P, S) for j in range(4)] \
        + [(None, [(g2[:, j * P:(j + 1) * P], PR[:, 13, :])], P, S) for j in range(4)]

    def evict(act, i, ps):
        if i < 4:
            return nc.scalar.activation(LW[:, i, :], ps, ACT.Sigmoid, bias=C.v("rw_w0_2", i))
        if i < 8:
            return nc.scalar.activation(A[:, i - 4, :], ps, ACT.Sigmoid, bias=C.v("rw_a0_2", i - 4))
        return nc.scalar.copy(G[:, i - 8, :], ps)
    project(C, "rw_lora", tiles, 0, evict)

    KK, BV = half(B[5], 0), half(B[5], 1)
    K2, E = half(B[6], 0), half(B[6], 1)
    At, Bt, Kt, Rt = half(B[7], 0), half(B[7], 1), half(B[8], 0), half(B[8], 1)
    RN = half(B[8], 1)
    BON = A
    flat = lambda x: x.rearrange("p j t -> p (j t)")
    PC = C.small[:, 32:64].rearrange("p (j c) -> p j c", j=4)
    with stage(nc, "rw_kk", "chain") as (block, chain):
        @block.vector
        def _(dve):
            for j in range(4):
                nc.vector.tensor_scalar(KK[:, j, :], k[:, j, :], C.v("rw_k_k_2", j), None, ALU.mult)

    def post(link):
        link(nc.vector.tensor_tensor(KK, KK, RN, ALU.mult))
        link(nc.vector.tensor_tensor(BV, KK, A, ALU.mult))
        for j in range(4):
            link(nc.vector.tensor_scalar(K2[:, j, :], A[:, j, :], 1.0, C.v("rw_k_a_2", j), ALU.subtract, ALU.mult))
        link(nc.vector.scalar_tensor_tensor(K2, K2, 1.0, k, ALU.add, ALU.mult))
        link(nc.vector.tensor_scalar(LW, LW, -math.exp(-0.5), None, ALU.mult))
        link(nc.vector.memset(E, 1.0))
        link(nc.vector.memset(flat(E).rearrange("p (n c) -> p n c", c=RC)[:, :, 0:1], 0.0))
        link(nc.vector.tensor_tensor_scan(flat(CS), flat(E), flat(LW), 0.0, ALU.mult, ALU.add))
        link(nc.vector.tensor_tensor(LW, CS, LW, ALU.subtract))
        for j in range(4):
            link(nc.vector.scalar_tensor_tensor(E[:, j, :], r[:, j, :], C.v("rw_r_k_2", j), K2[:, j, :], ALU.mult, ALU.mult))
    norm(C, "rw_kkn", KK, 4, 1, C.ones64[:, :], 1, 0.0, At, RN, post, floor=1e-12)

    with stage(nc, "rw_scale", "chain expd used bonus") as (block, chain, expd, used, bonus):
        @block.tensor
        def _(pe):
            for j in range(4):
                last = nc.tensor.matmul(C.PS[:, j // 2, (j % 2) * S:(j % 2 + 1) * S], C.ones64[:, :], E[:, j, :],
                                        start=True, stop=True)
            last.then_inc(bonus, 1)

        @block.scalar
        def _(act):
            nc.scalar.activation(At, LW, ACT.Exp).then_inc(expd, 1)
            nc.scalar.activation(Rt, CS, ACT.Exp).then_inc(expd, 1)
            nc.scalar.activation(Bt, CS, ACT.Exp, scale=-1.0).then_inc(expd, 1)

        @block.vector
        def _(dve):
            link = linker(dve, chain)
            dve.wait_ge(bonus, 1)
            link(nc.vector.tensor_tensor(BON, C.PS[:, 0:2, :].rearrange("p b (h t) -> p (b h) t", t=S), v, ALU.mult))
            dve.wait_ge(expd, 3)
            link(nc.vector.tensor_copy(PC, flat(Rt).rearrange("p (j c u) -> p j c u", j=4, u=RC)[:, :, :, RC - 1]))
            link(nc.vector.tensor_tensor(Kt, K2, Bt, ALU.mult))
            link(nc.vector.tensor_tensor(Bt, BV, Bt, ALU.mult))
            link(nc.vector.tensor_tensor(Rt, r, Rt, ALU.mult))
            link(nc.vector.scalar_tensor_tensor(At, At, -1.0, KK, ALU.mult, ALU.mult))

    Btok, Ktok = (B[4][:, i * 1024:(i + 1) * 1024].rearrange("p (t c) -> p t c", t=TT) for i in range(2))
    Htok, Vtok = (B[2][:, i * 1024:(i + 1) * 1024].rearrange("p (t c) -> p t c", t=TT) for i in range(2))
    with stage(nc, "rw_tok", "turned") as (block, turned):
        srcs = ((v, Vtok), (Bt, Btok), (Kt, Ktok))

        @block.tensor
        def _(pe):
            for n, (src, _) in enumerate(srcs):
                for tt in range(TT):
                    for j in range(4):
                        last = nc.tensor.transpose(C.PS[:, 2 * n + tt, j * P:(j + 1) * P], src[:, j, tt * P:(tt + 1) * P],
                                                   C.ident[:, :])
                last.then_inc(turned, 1)

        @block.scalar
        def _(act):
            for n, (_, dst) in enumerate(srcs):
                act.wait_ge(turned, n + 1)
                nc.scalar.copy(dst, C.PS[:, 2 * n:2 * n + 2, :])

    m8 = lambda x: x.rearrange("p (h c) -> p h c", c=P)
    UM, UT = m8(B[0][:, 0:1024]), m8(B[0][:, 1024:2048])
    OT, NT = m8(B[1][:, 0:1024]), m8(B[1][:, 1024:2048])
    X0 = m8(B[9][:, 0:1024])
    Hf = C.H[:, :, :].rearrange("p j t -> p (j t)")
    WT = m8(Hf[:, 0:1024])
    masks = [Hf[:, 1024 + i * P:1024 + (i + 1) * P] for i in range(5)]
    load_small(C, "rwm", [(masks[i], C.const(n)) for i, n in enumerate(("rw_d", "rw_dT", "rw_oT", "rw_ltT", "rw_leT"))])
    m_d, m_dT, m_oT, m_ltT, m_leT = (x.unsqueeze(1).to_broadcast([P, 8, P]) for x in masks)
    ident8 = C.ident[:, :].unsqueeze(1).to_broadcast([P, 8, P])
    MB, MK = (b.rearrange("p (t h c) -> p t h c", t=TT, h=8) for b in (B[5], B[6]))
    GT = At
    Y, Zs = UM, UT

    def bank8(b):
        return C.PS[:, b:b + 2, :].rearrange("p b (h c) -> p (b h) c", c=P)

    for tb in range(TT):
        tc = slice(tb * P, (tb + 1) * P)
        rows = [(slice(64 * (i // 4), 64 * (i // 4) + 64), i % 4) for i in range(8)]
        hcol = [slice(P * (i % 4) + 64 * (i // 4), P * (i % 4) + 64 * (i // 4) + 64) for i in range(8)]

        def products(pe, bank, lhs, rhs):
            for i, (rw, pair) in enumerate(rows):
                last = nc.tensor.matmul(bank8(bank)[:, i, :], lhs[rw, pair, tc], rhs[rw, pair, tc], start=True, stop=True)
            return last

        def each(bank, lhs, rhs):
            for i in range(8):
                last = nc.tensor.matmul(bank8(bank)[:, i, 0:rhs.shape[2]], lhs[:, i, :], rhs[:, i, :], start=True, stop=True)
            return last

        with stage(nc, f"rw_mat{tb}", "chain product masked turned a_taken") as (block, chain, product, masked, turned, a_taken):
            @block.tensor
            def _(pe):
                products(pe, 0, Bt, At).then_inc(product, 1)
                products(pe, 2, At, Bt).then_inc(product, 1)
                products(pe, 4, Kt, At).then_inc(product, 1)
                products(pe, 6, Bt, Rt).then_inc(product, 1)
                pe.wait_ge(masked, 1)
                products(pe, 0, Kt, Rt).then_inc(product, 1)
                pe.wait_ge(masked, 2)
                for j in range(4):
                    last = nc.tensor.transpose(C.PS[:, 2, j * P:(j + 1) * P], At[:, j, tc], C.ident[:, :])
                last.then_inc(turned, 1)
                pe.wait_ge(masked, 3)
                for i in range(8):
                    last = nc.tensor.matmul(C.PS[:, 4, i * 64:(i + 1) * 64], NT[:, i, :], Vtok[:, tb, hcol[i]], start=True, stop=True)
                last.then_inc(turned, 1)

            @block.vector
            def _(dve):
                link = linker(dve, chain)
                dve.wait_ge(product, 1)
                link(nc.vector.tensor_tensor(UT, bank8(0), m_dT, ALU.mult))
                link(nc.vector.tensor_tensor(OT, bank8(0), m_oT, ALU.mult))
                dve.sem_inc(masked, 1)
                dve.wait_ge(product, 2)
                link(nc.vector.tensor_tensor(UM, bank8(2), m_d, ALU.mult))
                dve.sem_inc(masked, 1)
                dve.wait_ge(product, 3)
                link(nc.vector.tensor_tensor(NT, bank8(4), m_ltT, ALU.mult))
                dve.sem_inc(masked, 1)
                link(nc.vector.tensor_tensor(WT, UT, ident8, ALU.add))
                dve.wait_ge(product, 5)
                link(nc.vector.tensor_tensor(MB[:, tb, :, :], bank8(6), m_leT, ALU.mult))
                link(nc.vector.tensor_tensor(MK[:, tb, :, :], bank8(0), m_leT, ALU.mult))

            @block.scalar
            def _(act):
                act.wait_ge(turned, 1)
                for hh in range(2):
                    nc.scalar.copy(X0[:, 4 * hh:4 * hh + 4, 0:64],
                                   C.PS[:, 2, :].rearrange("p (j c) -> p j c", c=P)[:, :, 64 * hh:64 * hh + 64])
                act.wait_ge(turned, 2)
                nc.scalar.copy(X0[:, :, 64:128], C.PS[:, 4, :].rearrange("p (i c) -> p i c", c=64))

        with stage(nc, f"rw_inv{tb}", "chain squared grown taken applied solved gturned") as (
                block, chain, squared, grown, taken, applied, solved, gturned):
            @block.tensor
            def _(pe):
                for n in range(3):
                    if n:
                        pe.wait_ge(taken, 2 * n)
                    each(0, UT, UM)
                    if n < 2:
                        each(2, UM, UT)
                    last = nc.tensor.transpose(C.PS[:, 7, 0:P], C.ident[:, :], C.ident[:, :])
                    last.then_inc(squared, 1)
                    pe.wait_ge(taken, 2 * n + 2)
                    if n:
                        pe.wait_ge(grown, n)
                    each(4, UM, WT).then_inc(applied, 1)
                pe.wait_ge(grown, 3)
                each(0, WT, X0).then_inc(applied, 1)
                pe.wait_ge(solved, 1)
                each(2, OT, Y).then_inc(applied, 1)
                pe.wait_ge(solved, 2)
                each(4, WT, Zs).then_inc(applied, 1)
                pe.wait_ge(solved, 3)
                gt = X0.rearrange("p h c -> p (h c)")
                for j in range(4):
                    last = nc.tensor.transpose(C.PS[:, 6, j * P:(j + 1) * P], gt[:, j * P:(j + 1) * P], C.ident[:, :])
                last.then_inc(gturned, 1)

            @block.scalar
            def _(act):
                for n in range(3):
                    act.wait_ge(squared, n + 1)
                    if n:
                        act.wait_ge(applied, n)
                    nc.scalar.copy(UM, bank8(0)).then_inc(taken, 1)
                    if n < 2:
                        nc.scalar.copy(UT, bank8(2)).then_inc(taken, 1)
                    else:
                        act.sem_inc(taken, 1)
                act.wait_ge(gturned, 1)
                nc.scalar.copy(GT[:, :, tc], C.PS[:, 6, :].rearrange("p (j c) -> p j c", c=P))

            @block.vector
            def _(dve):
                link = linker(dve, chain)
                for n in range(3):
                    dve.wait_ge(applied, n + 1)
                    link(nc.vector.tensor_tensor(WT, WT, bank8(4), ALU.add))
                    dve.sem_inc(grown, 1)
                dve.wait_ge(applied, 4)
                link(nc.vector.tensor_copy(Y, bank8(0)))
                dve.sem_inc(solved, 1)
                dve.wait_ge(applied, 5)
                link(nc.vector.tensor_copy(Zs, bank8(2)))
                dve.sem_inc(solved, 1)
                dve.wait_ge(applied, 6)
                g = X0.rearrange("p h c -> p (h c)")[:, 0:512].rearrange("p (j x c) -> p x j c", x=2, c=64)
                hh = Htok[:, tb, :].rearrange("p (j x c) -> p x j c", x=2, c=64)
                for x in range(2):
                    ys, ps = Y[:, 4 * x:4 * x + 4, :], bank8(4)[:, 4 * x:4 * x + 4, :]
                    link(nc.vector.tensor_tensor(g[:, x], ys[:, :, 0:64], ps[:, :, 0:64], ALU.add))
                    link(nc.vector.tensor_tensor(hh[:, x], ys[:, :, 64:128], ps[:, :, 64:128], ALU.add))
                dve.sem_inc(solved, 1)

    ST = B[0][:, 0:512].rearrange("p (j c) -> p j c", c=P)
    TMP = B[0][:, 512:1024].rearrange("p (j c) -> p j c", c=P)
    YT, YI = half(B[1], 0), half(B[1], 1)
    bd = C.ones64[:, :].unsqueeze(1).to_broadcast([P, 4, P])
    ps4 = lambda b, rw=slice(0, P): C.PS[rw, b, :].rearrange("p (j c) -> p j c", c=P)
    with stage(nc, "rw_seq", "chain state read sa update all_sa intra") as (block, chain, state, read, sa, update, all_sa, intra):
        @block.tensor
        def _(pe):
            for c in range(S // RC):
                tb, at = divmod(c * RC, P)
                rw = slice(at, at + RC)
                col = slice(c * RC, (c + 1) * RC)
                pe.wait_ge(state, c + 1)
                for j in range(4):
                    last = nc.tensor.matmul(ps4(0, rw)[:, j, :], GT[:, j, col], ST[:, j, :], start=True, stop=True)
                last.then_inc(read, 1)
                for j in range(4):
                    last = nc.tensor.matmul(C.PS[:, 2 + j // 2, (j % 2) * S + c * RC:(j % 2) * S + (c + 1) * RC],
                                            ST[:, j, :], Rt[:, j, col], start=True, stop=True)
                pe.wait_ge(sa, c + 1)
                for j in range(4):
                    jc = slice(j * P, (j + 1) * P)
                    nc.tensor.matmul(ps4(1)[:, j, :], Ktok[rw, tb, jc], Vtok[rw, tb, jc], start=True, stop=False)
                    last = nc.tensor.matmul(ps4(1)[:, j, :], Btok[rw, tb, jc], Htok[rw, tb, jc], start=False, stop=True)
                last.then_inc(update, 1)
            for tb in range(TT):
                for i in range(8):
                    o = C.PS[64 * (i // 4):64 * (i // 4) + 64, 4 + (i % 4) // 2, ((i % 4) % 2) * S + tb * P:((i % 4) % 2) * S + (tb + 1) * P]
                    hc = slice(P * (i % 4) + 64 * (i // 4), P * (i % 4) + 64 * (i // 4) + 64)
                    nc.tensor.matmul(o, Htok[:, tb, hc], MB[:, tb, i, :], start=True, stop=False)
                    last = nc.tensor.matmul(o, Vtok[:, tb, hc], MK[:, tb, i, :], start=False, stop=True)
            last.then_inc(intra, 1)

        @block.vector
        def _(dve):
            link = linker(dve, chain)
            link(nc.vector.memset(ST, 0.0))
            dve.sem_inc(state, 1)
            for c in range(S // RC):
                tb, at = divmod(c * RC, P)
                rw = slice(at, at + RC)
                dve.wait_ge(read, c + 1)
                link(nc.vector.tensor_tensor(Htok[rw, tb, :], Htok[rw, tb, :], C.PS[rw, 0, :], ALU.add))
                dve.sem_inc(sa, 1)
                dve.wait_ge(update, c + 1)
                link(nc.vector.tensor_tensor(TMP, ps4(1), bd, ALU.mult))
                link(nc.vector.tensor_tensor(TMP, TMP, ST, ALU.add))
                link(nc.vector.tensor_tensor(ST, TMP, PC[:, :, c:c + 1].to_broadcast([P, 4, P]), ALU.mult))
                dve.sem_inc(state, 1)
            dve.wait_ge(intra, 1)
            t4 = lambda b: C.PS[:, b:b + 2, :].rearrange("p b (h t) -> p (b h) t", t=S)
            link(nc.vector.tensor_copy(YT, t4(4)))
            link(nc.vector.tensor_tensor(YT, YT, t4(2), ALU.add))

    def post(link):
        link(nc.vector.tensor_tensor(YI, YI, RN, ALU.mult))
        for j in range(4):
            link(nc.vector.tensor_scalar(YI[:, j, :], YI[:, j, :], C.v("rw_gn_g_2", j), C.v("rw_gn_b_2", j), ALU.mult, ALU.add))
        link(nc.vector.tensor_tensor(YI, YI, BON, ALU.add))
        link(nc.vector.tensor_tensor(MIX[:, 0:4, :], YI, G, ALU.mult))
    norm(C, "rw_gn", YT, 4, 1, C.ones64[:, :], 64, GN_EPS, B[7][:, 0:1024], RN, post, center=YI)
    T = tiles3(B[0])
    project(C, "ab_out", cm_tiles(C, 0, MIX) + cm_tiles(C, 1, MIX), 2, add_alpha(C, T), on="dve")
    return T



def weight_plan(t):
    plan = []
    for l in range(2):
        plan += w_units(t["w_ada"][l])
        if l == 0:
            plan += w_units(t["a_w_in"][:, 0:3072]) + w_units(t["a_w_out"])
        else:
            plan += w_units(t["b_w_in"]) + w_units(t["b_w_out"])
        gu = t["moe_w_gu"][l].rearrange("e (k p) n -> e p k n", p=P)
        dn = t["moe_w_down"][l].rearrange("e (k p) n -> e p k n", p=P)
        for e in range(16):
            plan += [gu[e, :, :, 0:512], gu[e, :, :, 512:1024], dn[e]]
    for l in range(2):
        if l == 0:
            plan += w_units(t["ab_w_in_2"], [512, 512, 512, 256, 512, 512]) + w_units(t["ab_w_out_2"])
        else:
            w = t["mla_w_in_2"]
            plan += w_units(w[:, 0:512]) + [w.rearrange("(k p) n -> p k n", p=P)[:, :, 448:544]]
            plan += w_units(t["mla_wq_b_2"]) + w_units(t["mla_wkv_b_2"]) + w_units(t["mla_w_out_2"])
        plan += w_units(t["xa_wq_2"][l]) + w_units(t["xa_wkv_2"][l]) + w_units(t["xa_wo_2"][l])
        v = [t[n][l].rearrange("e (k p) n -> e p k n", p=P) for n in ("moe_w_gate_2", "moe_w_up_2", "moe_w_down_2")]
        for e in range(32):
            plan += [x[e] for x in v]
    return plan


def two_blocks(nc, t, cnames, out):
    with ExitStack() as ctx:
        C = Chip(nc, t, ctx, cnames)
        C.plan = weight_plan(t)
        with stage(nc, "start", "landed") as (block, landed):
            @block.sync
            def _(sp):
                small = [(C.vec[:, :], t["vec"]), (C.ident[:, :], C.const("ident")), (C.ones[:, :], C.const("ones")),
                         (C.ones64[:, :], C.const("ones64")), (C.X[:, :, :], t["x_T"])]
                for dst, src in small:
                    sp.dma_start(dst, src).then_inc(landed, 16)
                for v in range(RING):
                    C.load(sp, v)
                sp.wait_ge(landed, 16 * len(small))
        for l in range(2):
            ada(C, f"ada{l}", l)
            modulated_norm(C, f"n1_{l}", C.v("norm1", 8 * l, 8), C.mod[:, 0:8], C.mod[:, 8:16])
            (mlstm, diff_attention)[l](C)
            modulated_norm(C, f"n2_{l}", C.v("norm2", 8 * l, 8), C.mod[:, 24:32], C.mod[:, 32:40])
            moe1(C, f"moe1_{l}", l)
        for l in range(2):
            ln = lambda n, src: layer_norm(C, f"ln{n}_{l}", src, C.v(f"ln{n}_g_2", 8 * l, 8), C.v(f"ln{n}_b_2", 8 * l, 8))
            ln(1, (mixer_ab, mla)[l](C))
            ln(2, cross_attention(C, f"xa{l}"))
            ln(3, moe2(C, f"moe2_{l}", l))
        assert C.used == len(C.plan)
        with stage(nc, "end", "stored") as (block, stored):
            @block.sync
            def _(sp):
                sp.dma_start(out, C.X[:, :, :]).then_inc(stored, 16)
                sp.wait_ge(stored, 16)



def column(a):
    return np.ascontiguousarray(np.asarray(a, np.float32).reshape(-1, P).T)


def lay_out(x):
    parts = []
    for n, w in VECTORS:
        if n == "b_if":
            a = np.zeros((P, 2), np.float32)
            a[0:4] = np.asarray(x["a_b_if"]).reshape(2, 4).T
        elif n in ("b_q_norm", "b_k_norm"):
            a = column(np.tile(np.asarray(x[n]).reshape(-1), 2))
        else:
            a = column(x[n])
        assert a.shape == (P, w), (n, a.shape)
        parts.append(a)
    arrays = {"vec": np.concatenate(parts, axis=1)}
    rows = []
    for n, w in ROWS:
        if n == "lam":
            a = np.concatenate([np.asarray(x["b_lam_" + s]).reshape(-1) for s in ("q1", "k1", "q2", "k2")])
        else:
            a = np.asarray(x[n]).reshape(-1)
        assert a.shape == (w,), n
        rows.append(a)
    arrays["rows"] = np.concatenate(rows)[None, :]
    by_channel = lambda a: np.ascontiguousarray(np.asarray(a).reshape(S, KT, P).transpose(2, 1, 0))
    arrays["x_T"] = by_channel(x["x"])
    arrays["mem_T"] = by_channel(x["mem_2"])
    arrays["positions"] = np.asarray(x["positions"]).reshape(1, S)
    arrays["sg_ws_T"] = np.ascontiguousarray(np.asarray(x["sg_ws_2"])[0].transpose(2, 0, 1))
    for n in ("w_ada", "a_w_in", "a_w_out", "b_w_in", "b_w_out", "w_router", "moe_w_gu", "moe_w_down", "ab_w_in_2",
              "rw_w2_2", "rw_a2_2", "rw_g2_2", "ab_w_out_2", "mla_w_in_2", "mla_wq_b_2", "mla_wkv_b_2", "mla_w_out_2",
              "xa_wq_2", "xa_wkv_2", "xa_wo_2", "moe_w_group_2", "moe_w_expert_2", "moe_w_gate_2", "moe_w_up_2",
              "moe_w_down_2"):
        a = np.asarray(x[n])
        arrays[n] = a.reshape(a.shape[1:]) if a.shape[0] == 1 else a
    return arrays


def prepare(nc, x):
    arrays = lay_out(x)
    cnames, consts = shape_constants()
    arrays["consts"] = consts
    t = {n: nc.dram_tensor(f"in_{n}", a.shape, mybir.dt.from_np(a.dtype), kind="ExternalInput").ap() for n, a in arrays.items()}
    return {f"in_{n}": a for n, a in arrays.items()}, t, cnames


def kernel(**inputs):
    import concourse.bacc as bacc
    from concourse.bass_utils import run_bass_kernel_spmd

    nc = bacc.Bacc("TRN2", target_bir_lowering=False, num_devices=1)
    arrays, t, cnames = prepare(nc, inputs)
    out = nc.dram_tensor("out_T", (P, KT, S), F32, kind="ExternalOutput").ap()
    two_blocks(nc, t, cnames, out)
    result = run_bass_kernel_spmd(nc, [arrays], core_ids=[0])
    y = result.results[0]["out_T"]
    return np.ascontiguousarray(y.transpose(2, 1, 0)).reshape(1, S, D)
```

```python
from contextlib import ExitStack, contextmanager
import math

import numpy as np

import concourse.bass as bass
from concourse import mybir

F32 = mybir.dt.float32
I32 = mybir.dt.int32
ALU = mybir.AluOpType
ACT = mybir.ActivationFunctionType
AX_X = mybir.AxisListType.X

P = 128
D = 1024
KT = D // P
S = 256
TT = S // P
RING = 6
SLOT = 4096
BUF = 2048
NBUF = 10
BANK = 512
STAGE_SEM0 = 200

EPS = 1e-6
LN_EPS = 1e-5
GN_EPS = 64e-5
ALPHA = 4 ** 0.25
LAM_INIT = 0.8 - 0.6 * math.exp(-0.3 * 1)
NEG = -1e30
RC = 32
CAP = 64
MAXLEFT = 2 * S // CAP



def shape_constants():
    p = np.arange(P)
    c = {}
    c["ident"] = np.eye(P)
    c["ones"] = np.ones((P, P))
    c["ones64"] = (p[:, None] // 64 == p[None, :] // 64) * 1.0
    c["causal_add"] = np.where(p[:, None] >= p[None, :], 0.0, NEG)
    c["key_le"] = (p[:, None] <= p[None, :]) * 1.0
    c["key_lt"] = (p[:, None] < p[None, :]) * 1.0
    c["iota"] = np.broadcast_to(np.arange(S)[None, :], (P, S))
    same32 = p[:, None] // RC == p[None, :] // RC
    same16 = p[:, None] // 16 == p[None, :] // 16
    c["rw_d"] = (same16 & (p[:, None] > p[None, :])) * 1.0
    c["rw_dT"] = (same16 & (p[:, None] < p[None, :])) * 1.0
    c["rw_oT"] = (same32 & ~same16 & (p[:, None] < p[None, :])) * 1.0
    c["rw_ltT"] = (same32 & (p[:, None] < p[None, :])) * 1.0
    c["rw_leT"] = (same32 & (p[:, None] <= p[None, :])) * 1.0
    rot = np.zeros((P, P))
    for b in (0, 64):
        for i in range(8):
            rot[b + i + 8, b + i] = -1.0
            rot[b + i, b + i + 8] = 1.0
    c["rot_b"] = rot
    rot = np.zeros((P, P))
    for i in range(16):
        rot[64 + i + 16, 64 + i] = -1.0
        rot[64 + i, 64 + i + 16] = 1.0
    c["rot_m"] = rot
    sel = np.zeros((P, 4 * P))
    for h in range(4):
        sel[h, h * P:(h + 1) * P] = 1.0
    c["sel"] = sel
    inv = (np.float32(500000.0) ** (-np.arange(0, 16, 2, dtype=np.float32) / np.float32(16))).astype(np.float32)
    f = np.zeros(P, np.float32)
    for b in (0, 64):
        f[b:b + 8] = inv
        f[b + 8:b + 16] = inv
    c["inv_b"] = np.ascontiguousarray(np.broadcast_to(f[:, None], (P, 2)))
    inv = (np.float32(10000.0) ** (-np.arange(16, dtype=np.float32) / np.float32(16))).astype(np.float32)
    f = np.zeros(P, np.float32)
    f[64:80] = inv
    f[80:96] = inv
    ang = (np.arange(S, dtype=np.float32)[None, :] * f[:, None]).astype(np.float32)
    c["cos_m"] = np.cos(ang)
    c["sin_m"] = np.sin(ang)
    names, at, parts = {}, 0, []
    for k, v in c.items():
        names[k] = (at, v.shape[1])
        at += v.shape[1]
        parts.append(np.asarray(v, np.float32))
    return names, np.ascontiguousarray(np.concatenate(parts, axis=1))


VECTORS = [
    ("c", 8), ("norm1", 16), ("norm2", 16), ("b_ada", 96), ("a_h_norm", 8),
    ("b_q_norm", 1), ("b_k_norm", 1), ("b_o_norm", 1),
    ("ab_mu_2", 14), ("rw_w0_2", 4), ("rw_a0_2", 4), ("rw_k_k_2", 4), ("rw_k_a_2", 4),
    ("rw_r_k_2", 4), ("rw_gn_g_2", 4), ("rw_gn_b_2", 4),
    ("mla_q_norm_2", 2), ("mla_kv_norm_2", 2),
    ("ln1_g_2", 16), ("ln1_b_2", 16), ("ln2_g_2", 16), ("ln2_b_2", 16), ("ln3_g_2", 16), ("ln3_b_2", 16),
    ("b_if", 2),
]
VCOL = {}
_at = 0
for _n, _w in VECTORS:
    VCOL[_n] = (_at, _w)
    _at += _w
NVEC = _at

ROWS = [
    ("router_bias", 16), ("moe_b_group_2", 8), ("moe_b_expert_2", 64),
    ("lam", 256), ("sg_ln_g_2", 512), ("sg_ln_b_2", 512), ("sg_b_2", 512),
]
RCOL = {}
_at = 0
for _n, _w in ROWS:
    RCOL[_n] = (_at, _w)
    _at += _w
NROW = _at


@contextmanager
def stage(nc, tag, names):
    names = names.split()
    with ExitStack() as held:
        sems = [held.enter_context(nc.semaphore(f"{tag}_{n}", num=STAGE_SEM0 + i)) for i, n in enumerate(names)]
        with nc.Block() as block:
            yield (block, *sems)
        nc.all_engine_barrier(sems_to_clear=range(STAGE_SEM0, STAGE_SEM0 + len(names)))


def linker(eng, sem):
    count = [0]

    def link(ins):
        count[0] += 1
        ins.then_inc(sem, 1)
        eng.wait_ge(sem, count[0])
    return link


class Chip:

    def __init__(self, nc, t, ctx, cnames):
        self.nc, self.t = nc, t

        def sb(name, shape, dt=F32):
            return ctx.enter_context(nc.sbuf_tensor(name, shape, dt))

        self.ring = sb("ring", [P, RING, SLOT])
        self.X = sb("X", [P, KT, S])
        self.H = sb("H", [P, KT, S])
        self.big = sb("scratch", [P, NBUF * BUF])
        self.B = [self.big[:, i * BUF:(i + 1) * BUF] for i in range(NBUF)]
        self.PS = ctx.enter_context(nc.psum_tensor("PS", [P, 8, BANK], F32))
        self.vec = sb("vec", [P, NVEC])
        self.mod = sb("mod", [P, 48])
        self.small = sb("small", [P, 64])
        self.route = sb("route", [P, 136 + S])
        self.left = sb("left", [1, 20], I32)
        self.act_rows = sb("act_rows", [P, 512])
        self.ident = sb("ident", [P, P])
        self.ones = sb("ones", [P, P])
        self.ones64 = sb("ones64", [P, P])
        self.consts = t["consts"]
        self.cnames = cnames
        self.slot_loaded = [ctx.enter_context(nc.semaphore(f"slot_loaded{i}")) for i in range(RING)]
        self.slot_free = [ctx.enter_context(nc.semaphore(f"slot_free{i}")) for i in range(RING)]
        self.plan = []
        self.used = 0

    def v(self, name, j=0, w=1):
        at, _ = VCOL[name]
        return self.vec[:, at + j:at + j + w]

    def const(self, name):
        at, w = self.cnames[name]
        return self.consts[:, at:at + w]

    def row(self, name, j=0, w=None):
        at, ww = RCOL[name]
        w = ww if w is None else w
        return self.t["rows"][0:1, at + j:at + j + w].to_broadcast([P, w])

    def unit(self, u):
        _, a, b = self.plan[u].shape
        return self.ring[:, u % RING, 0:a * b].rearrange("p (a b) -> p a b", b=b)

    def loaded(self, eng, u):
        eng.wait_ge(self.slot_loaded[u % RING], 16 * (u // RING + 1))

    def freed(self, u):
        return self.slot_free[u % RING]

    def load(self, sp, v):
        if v >= len(self.plan):
            return
        if v >= RING:
            sp.wait_ge(self.slot_free[v % RING], v // RING)
        sp.dma_start(self.unit(v), self.plan[v]).then_inc(self.slot_loaded[v % RING], 16)

    def refill(self, sp, u0, n):
        for u in range(u0, u0 + n):
            self.load(sp, u + RING)


def w_units(w, widths=None):
    k, n = w.shape
    v = w.rearrange("(k p) n -> p k n", p=P)
    out, at = [], 0
    widths = widths or [min(SLOT // (k // P), n)] * (n // min(SLOT // (k // P), n))
    for b in widths:
        out.append(v[:, :, at:at + b])
        at += b
    assert at == n
    return out


def load_small(C, tag, items):
    with stage(C.nc, tag, "landed") as (block, landed):
        @block.sync
        def _(sp):
            for dst, src in items:
                sp.dma_start(dst, src).then_inc(landed, 16)
            sp.wait_ge(landed, 16 * len(items))



def project(C, tag, tiles, units, evict, on="act", nb=4):
    nc = C.nc
    u0 = C.used
    last_of = {}
    for i, (u, _, _, _) in enumerate(tiles):
        if u is not None:
            last_of[u] = i
    with stage(nc, tag, "summed evicted") as (block, summed, evicted):
        @block.sync
        def _(sp):
            C.refill(sp, u0, units)

        @block.tensor
        def _(pe):
            seen = -1
            for i, (u, pairs, M, N) in enumerate(tiles):
                if u is not None and u > seen:
                    C.loaded(pe, u0 + u)
                    seen = u
                if i >= nb:
                    pe.wait_ge(evicted, i - nb + 1)
                for k, (lhsT, rhs) in enumerate(pairs):
                    last = nc.tensor.matmul(C.PS[0:M, i % nb, 0:N], lhsT, rhs,
                                            start=(k == 0), stop=(k == len(pairs) - 1))
                last.then_inc(summed, 1)

        def evictions(eng):
            for i, (u, _, M, N) in enumerate(tiles):
                eng.wait_ge(summed, i + 1)
                if u is not None and last_of[u] == i:
                    eng.sem_inc(C.freed(u0 + u), 1)
                evict(eng, i, C.PS[0:M, i % nb, 0:N]).then_inc(evicted, 1)

        if on == "act":
            @block.scalar
            def _(act):
                evictions(act)
        else:
            @block.vector
            def _(dve):
                evictions(dve)
    C.used += units


def cm_tiles(C, u, x, cols=None, m=P, kt=KT, at=0):
    w = C.unit(C.used + u)
    cols = cols or w.shape[2] - at
    return [(u, [(w[:, k, at + j * m:at + (j + 1) * m], x[:, k, :]) for k in range(kt)], m, S)
            for j in range(cols // m)]


def tm_tiles(C, u, x, kt=KT, cols=slice(None)):
    w = C.unit(C.used + u)
    return [(u, [(x[:, k, tt * P:(tt + 1) * P], w[:, k, cols]) for k in range(kt)], P, w[:, 0, cols].free_size())
            for tt in range(TT)]



def norm(C, tag, src, groups, per, mat, n, eps, sq, out, post, center=None, floor=None):
    nc = C.nc
    v = lambda x: x if len(x.shape) == 3 else x.rearrange("p (j t) -> p j t", t=S)
    src, sq = v(src), v(sq)
    with stage(nc, tag, "chain squared mean_sum square_sum variance root") as (
            block, chain, squared, mean_sum, square_sum, variance, root):
        sums = C.PS[:, 0:max(1, groups * S // BANK), :].rearrange("p b (h t) -> p (b h) t", t=S)

        @block.vector
        def _(dve):
            link = linker(dve, chain)
            x = src
            if center is not None:
                dve.wait_ge(mean_sum, 1)
                x = v(center)
                for g in range(groups):
                    for j in range(g * per, (g + 1) * per):
                        link(nc.vector.scalar_tensor_tensor(x[:, j, :], sums[:, g, :], -1.0 / n, src[:, j, :],
                                                            ALU.mult, ALU.add))
            nc.vector.tensor_tensor(sq[:, 0:groups * per, :], x[:, 0:groups * per, :],
                                    x[:, 0:groups * per, :], ALU.mult).then_inc(squared, 1)
            dve.wait_ge(square_sum, 1)
            nc.vector.tensor_scalar(out, sums[:, 0:groups, :], 1.0 / n, eps, ALU.mult, ALU.add).then_inc(variance, 1)
            dve.wait_ge(root, 1)
            if floor is not None:
                link(nc.vector.tensor_scalar(out, out, floor, None, ALU.max))
            link(nc.vector.reciprocal(out, out))
            post(link)

        @block.scalar
        def _(act):
            act.wait_ge(variance, 1)
            nc.scalar.activation(out, out, ACT.Sqrt).then_inc(root, 1)

        @block.tensor
        def _(pe):
            if center is not None:
                for g in range(groups):
                    for j in range(per):
                        last = nc.tensor.matmul(sums[:, g, :], mat, src[:, g * per + j, :],
                                                start=(j == 0), stop=(j == per - 1))
                last.then_inc(mean_sum, 1)
            pe.wait_ge(squared, 1)
            for g in range(groups):
                for j in range(per):
                    last = nc.tensor.matmul(sums[:, g, :], mat, sq[:, g * per + j, :],
                                            start=(j == 0), stop=(j == per - 1))
            last.then_inc(square_sum, 1)


def modulated_norm(C, tag, gain, shift, scale):
    nc = C.nc
    a = C.small[:, 0:KT]
    r = C.B[1][:, 0:S]

    def post(link):
        link(nc.vector.tensor_scalar(a, scale, 1.0, None, ALU.add))
        link(nc.vector.tensor_tensor(a, a, gain, ALU.mult))
        link(nc.vector.tensor_tensor(C.H[:, :, :], C.X[:, :, :], r.unsqueeze(1).to_broadcast([P, KT, S]), ALU.mult))
        for k in range(KT):
            link(nc.vector.tensor_scalar(C.H[:, k, :], C.H[:, k, :], a[:, k:k + 1], shift[:, k:k + 1],
                                         ALU.mult, ALU.add))
    norm(C, tag, C.X[:, :, :], 1, KT, C.ones[:, :], D, EPS, C.B[0], r.unsqueeze(1), post)


def layer_norm(C, tag, src, g, b):
    nc = C.nc
    r = C.B[1][:, 0:S]
    cen = C.B[2].rearrange("p (j t) -> p j t", t=S)

    def post(link):
        link(nc.vector.tensor_tensor(cen, cen, r.unsqueeze(1).to_broadcast([P, KT, S]), ALU.mult))
        for k in range(KT):
            link(nc.vector.tensor_scalar(C.X[:, k, :], cen[:, k, :], g[:, k:k + 1], b[:, k:k + 1],
                                         ALU.mult, ALU.add))
    norm(C, tag, src, 1, KT, C.ones[:, :], D, LN_EPS, C.B[0], r.unsqueeze(1), post, center=C.B[2])



def ada(C, tag, l):
    nc = C.nc
    u0, n = C.used, 12
    cact = C.B[0][:, 0:256].rearrange("p (k r) -> p k r", r=32)
    sig = C.small[:, 8:16]
    rows = C.B[1][:, 0:1536]
    with stage(nc, tag, "silu copied summed taken turned") as (block, silu, copied, summed, taken, turned):
        @block.sync
        def _(sp):
            C.refill(sp, u0, n)

        @block.scalar
        def _(act):
            nc.scalar.activation(sig, C.v("c", 0, 8), ACT.Silu).then_inc(silu, 1)
            for b in range(3):
                act.wait_ge(summed, b + 1)
                for i in range(4):
                    act.sem_inc(C.freed(u0 + 4 * b + i), 1)
                nc.scalar.copy(rows[:, b * 512:(b + 1) * 512], C.PS[:, b, :]).then_inc(taken, 1)

        @block.tensor
        def _(pe):
            pe.wait_ge(copied, 1)
            for b in range(3):
                for i in range(4):
                    C.loaded(pe, u0 + 4 * b + i)
                for k in range(KT):
                    for i in range(4):
                        last = nc.tensor.matmul(C.PS[32 * i:32 * i + 32, b, :], cact[:, k, :], C.unit(u0 + 4 * b + i)[:, k, :],
                                                start=(k == 0), stop=(k == KT - 1))
                last.then_inc(summed, 1)
            for b in range(3):
                pe.wait_ge(taken, b + 1)
                for j in range(4):
                    last = nc.tensor.transpose(C.PS[:, 3 + b, j * P:(j + 1) * P],
                                               rows[:, b * 512 + j * P:b * 512 + (j + 1) * P], C.ident[:, :])
            last.then_inc(turned, 1)

        @block.vector
        def _(dve):
            dve.wait_ge(silu, 1)
            nc.vector.tensor_copy(cact, sig.unsqueeze(2).to_broadcast([P, KT, 32])).then_inc(copied, 1)
            dve.wait_ge(turned, 1)
            for b in range(3):
                got = C.PS[:, 3 + b, :].rearrange("p (j i r) -> p i j r", i=4, r=32)[:, :, :, 0]
                at = 16 * b
                nc.vector.tensor_tensor(C.mod[:, at:at + 16].rearrange("p (i j) -> p i j", i=4), got,
                                        C.v("b_ada", 48 * l + at, 16).rearrange("p (i j) -> p i j", i=4), ALU.add)
    C.used += n


def add_residual(C, gate):
    def evict(dve, i, ps):
        return C.nc.vector.scalar_tensor_tensor(C.X[:, i, :], ps, gate[:, i:i + 1], C.X[:, i, :], ALU.mult, ALU.add)
    return evict


def add_alpha(C, dst):
    def evict(dve, i, ps):
        return C.nc.vector.scalar_tensor_tensor(dst[:, i, :], C.X[:, i, :], ALPHA, ps, ALU.mult, ALU.add)
    return evict



def attention(C, tag, items, scale, causal, maps, scores, values, combine, buf, mask):
    nc = C.nc
    dest, lam = combine
    n = len(items)
    W = maps * 2 * P
    T = [buf[:, i * W:(i + 1) * W].rearrange("p (m k) -> p m k", m=maps) for i in range(2)]
    at = 2 * W
    E = [buf[:, at + i * W:at + (i + 1) * W].rearrange("p (m k) -> p m k", m=maps) for i in range(2)]
    at += 2 * W
    PT = [buf[:, at + i * 2 * P:at + (i + 1) * 2 * P].rearrange("p (b q) -> p b q", b=2) for i in range(2)]
    at += 4 * P
    st = buf[:, at:at + 16]
    mx = [st[:, 4 * i:4 * i + maps] for i in range(2)]
    sm = [st[:, 8 + 4 * i:8 + 4 * i + maps] for i in range(2)]
    nks = [(qb + 1 if causal else TT) for _, qb in items]
    with stage(nc, tag, "chain scored biased expd probs transposed probs_T pv_done out") as (
            block, chain, scored, biased, expd, probs, transposed, probs_T, pv_done, out):

        @block.tensor
        def _(pe):
            for i in range(n + 2):
                if i < n:
                    h, qb = items[i]
                    if i >= 2:
                        pe.wait_ge(biased, i - 1)
                    for m in range(maps):
                        pairs = scores(h, m, qb, nks[i])
                        for k, (lhsT, rhs) in enumerate(pairs):
                            last = nc.tensor.matmul(C.PS[:, 6 * m + i % 2, 0:nks[i] * P], lhsT, rhs,
                                                    start=(k == 0), stop=(k == len(pairs) - 1))
                    last.then_inc(scored, 1)
                if 1 <= i <= n:
                    j = i - 1
                    pe.wait_ge(probs, j + 1)
                    if j >= 2:
                        pe.wait_ge(probs_T, j - 1)
                    for b in range(nks[j]):
                        last = nc.tensor.transpose(C.PS[:, 2 + j % 2, b * P:(b + 1) * P],
                                                   E[j % 2][:, 0, b * P:(b + 1) * P], C.ident[:, :])
                    last.then_inc(transposed, 1)
                if i >= 2:
                    j = i - 2
                    h, qb = items[j]
                    pe.wait_ge(probs_T, j + 1)
                    if j >= 2:
                        pe.wait_ge(out, j - 1)
                    parts = values(h, 0)
                    for x in range(len(parts)):
                        for b in range(nks[j]):
                            vv, M, col = values(h, b)[x]
                            last = nc.tensor.matmul(C.PS[0:M, 4 + j % 2, col * P:(col + 1) * P], vv,
                                                    PT[j % 2][:, b, :], start=(b == 0), stop=(b == nks[j] - 1))
                    last.then_inc(pv_done, 1)

        @block.vector
        def _(dve):
            link = linker(dve, chain)
            for i in range(n + 1):
                if i < n:
                    qb, nk = items[i][1], nks[i]
                    dve.wait_ge(scored, i + 1)
                    if i >= 2:
                        dve.wait_ge(expd, i - 1)
                    for m in range(maps):
                        free = (nk - 1) * P if causal else nk * P
                        if free:
                            link(nc.vector.tensor_scalar(T[i % 2][:, m, 0:free], C.PS[:, 6 * m + i % 2, 0:free], scale, None, ALU.mult))
                        if causal:
                            link(nc.vector.scalar_tensor_tensor(T[i % 2][:, m, free:free + P], C.PS[:, 6 * m + i % 2, free:free + P],
                                                                scale, mask, ALU.mult, ALU.add))
                    link(nc.vector.tensor_reduce(mx[i % 2], T[i % 2][:, :, 0:nk * P], AX_X, ALU.max))
                    link(nc.vector.tensor_scalar(mx[i % 2], mx[i % 2], -1.0, None, ALU.mult))
                    dve.sem_inc(biased, 1)
                if i >= 1:
                    j = i - 1
                    e, s = E[j % 2], sm[j % 2]
                    w = nks[j] * P
                    dve.wait_ge(expd, j + 1)
                    link(nc.vector.reciprocal(s, s))
                    if maps == 2:
                        link(nc.vector.tensor_scalar(e[:, 1, 0:w], e[:, 1, 0:w], s[:, 1:2], lam, ALU.mult, ALU.mult))
                        link(nc.vector.scalar_tensor_tensor(e[:, 0, 0:w], e[:, 0, 0:w], s[:, 0:1], e[:, 1, 0:w],
                                                            ALU.mult, ALU.subtract))
                    else:
                        link(nc.vector.tensor_scalar(e[:, 0, 0:w], e[:, 0, 0:w], s[:, 0:1], None, ALU.mult))
                    dve.sem_inc(probs, 1)

        @block.scalar
        def _(act):
            for i in range(n + 2):
                if i < n:
                    act.wait_ge(biased, i + 1)
                    if i >= 2:
                        act.wait_ge(transposed, i - 1)
                    for m in range(maps):
                        last = nc.scalar.activation(E[i % 2][:, m, 0:nks[i] * P], T[i % 2][:, m, 0:nks[i] * P], ACT.Exp,
                                                    bias=mx[i % 2][:, m:m + 1], accum_out=sm[i % 2][:, m:m + 1])
                    last.then_inc(expd, 1)
                if 1 <= i <= n:
                    j = i - 1
                    act.wait_ge(transposed, j + 1)
                    if j >= 2:
                        act.wait_ge(pv_done, j - 1)
                    nc.scalar.copy(PT[j % 2][:, 0:nks[j], :],
                                   C.PS[:, 2 + j % 2, 0:nks[j] * P].rearrange("p (b q) -> p b q", q=P)).then_inc(probs_T, 1)
                if i >= 2:
                    j = i - 2
                    h, qb = items[j]
                    act.wait_ge(pv_done, j + 1)
                    _, M, _ = values(h, 0)[0]
                    parts = len(values(h, 0))
                    nc.scalar.copy(dest(h, qb), C.PS[0:M, 4 + j % 2, 0:parts * P].rearrange(
                        "p (b q) -> p b q", b=parts)).then_inc(out, 1)


def tiles3(x, j0=0, n=KT):
    return x[:, j0 * S:(j0 + n) * S].rearrange("p (j t) -> p j t", t=S)



def mlstm(C):
    nc, t = C.nc, C.t
    Q, K_ = tiles3(C.B[0], 0, 4), tiles3(C.B[0], 4, 4)
    V = C.B[1].rearrange("p (t v) -> p t v", t=TT)
    O = tiles3(C.B[2])
    NUM = tiles3(C.B[3])
    misc = C.B[4]
    wg = misc[:, 0:64].rearrange("p (k n) -> p k n", n=8)
    sel = misc[0:4, 64:64 + 512].rearrange("p (h m) -> p h m", h=4)
    key_le = misc[:, 576:704]
    key_le_row = key_le
    B5 = C.B[5]
    gi, gf, tmp, ones4 = (B5[0:4, i * S:(i + 1) * S] for i in range(4))
    u, negm, emt, bc = (B5[0:4, (4 + i) * S:(5 + i) * S] for i in range(4))
    ucol = misc[:, 704:712]
    load_small(C, "mlc", [(wg, t["a_w_in"].rearrange("(k p) n -> p k n", p=P)[:, :, 3072:3080]),
                          (sel, C.const("sel")[0:4, :].rearrange("p (h m) -> p h m", h=4)),
                          (key_le, C.const("key_le"))])

    tiles = cm_tiles(C, 0, C.H) + cm_tiles(C, 1, C.H) + tm_tiles(C, 2, C.H) + tm_tiles(C, 3, C.H) \
        + cm_tiles(C, 4, C.H) + cm_tiles(C, 5, C.H) \
        + [(None, [(wg[:, k, 4 * g:4 * g + 4], C.H[:, k, :]) for k in range(KT)], 4, S) for g in range(2)]

    def evict(act, i, ps):
        if i < 4:
            return nc.scalar.copy(Q[:, i, :], ps)
        if i < 8:
            return nc.scalar.mul(K_[:, i - 4, :], ps, 128 ** -0.5)
        if i < 12:
            a, tt = divmod(i - 8, 2)
            return nc.scalar.copy(V[:, tt, a * 512:(a + 1) * 512], ps)
        if i < 20:
            return nc.scalar.activation(O[:, i - 12, :], ps, ACT.Sigmoid)
        return nc.scalar.activation((gi, gf)[i - 20], ps, ACT.Identity, bias=C.v("b_if", i - 20)[0:4, :])
    project(C, "ml_in", tiles, 6, evict)

    with stage(nc, "ml_gate", "chain abs_z log1p u_ready u_T") as (block, chain, abs_z, log1p, u_ready, u_T):
        @block.vector
        def _(dve):
            link = linker(dve, chain)
            link(nc.vector.memset(ones4, 1.0))
            link(nc.vector.scalar_tensor_tensor(tmp, gf, -1.0, gf, ALU.mult, ALU.max))
            dve.sem_inc(abs_z, 1)
            dve.wait_ge(log1p, 2)
            link(nc.vector.scalar_tensor_tensor(tmp, gf, 0.0, tmp, ALU.min, ALU.subtract))
            link(nc.vector.tensor_tensor_scan(bc, ones4, tmp, 0.0, ALU.mult, ALU.add))
            link(nc.vector.tensor_tensor(u, gi, bc, ALU.subtract))
            dve.sem_inc(u_ready, 1)
            link(nc.vector.tensor_tensor_scan(negm, ones4, u, 0.0, ALU.mult, ALU.max))
            link(nc.vector.tensor_scalar(negm, negm, -1.0, None, ALU.mult))
            link(nc.vector.tensor_tensor(emt, negm, bc, ALU.subtract))
            dve.wait_ge(u_T, 1)
            link(nc.vector.tensor_copy(ucol, C.PS[:, 0, 0:8]))
            dve.sem_inc(u_ready, 1)

        @block.scalar
        def _(act):
            act.wait_ge(abs_z, 1)
            nc.scalar.activation(tmp, tmp, ACT.Exp, scale=-1.0).then_inc(log1p, 1)
            act.wait_ge(log1p, 1)
            nc.scalar.activation(tmp, tmp, ACT.Ln, bias=1.0).then_inc(log1p, 1)
            act.wait_ge(u_ready, 2)
            nc.scalar.activation(emt, emt, ACT.Exp)

        @block.tensor
        def _(pe):
            pe.wait_ge(u_ready, 1)
            for tt in range(TT):
                last = nc.tensor.transpose(C.PS[:, 0, 4 * tt:4 * tt + 4], u[:, tt * P:(tt + 1) * P], C.ident[0:4, 0:4])
            last.then_inc(u_T, 1)

    Dm = [tiles3(C.B[6], 2 * i, 2) for i in range(2)]
    Wm = [tiles3(C.B[6], 4 + 2 * i, 2) for i in range(2)]
    r = C.B[7][:, 0:S]
    dn = C.B[7][:, S:2 * S]
    with stage(nc, "ml_mix", "chain bcast clamped expd scored weighted summed taken") as (
            block, chain, bcast, clamped, expd, scored, weighted, summed, taken):
        @block.tensor
        def _(pe):
            for h in range(4):
                if h:
                    pe.wait_ge(taken, h)
                nc.tensor.matmul(C.PS[:, 0, 0:S], sel[:, h, :], negm, start=True, stop=True)
                nc.tensor.matmul(C.PS[:, 1, 0:S], sel[:, h, :], emt, start=True, stop=True).then_inc(bcast, 1)
                for st in range(TT):
                    last = nc.tensor.matmul(C.PS[:, 2 + st, 0:S], K_[:, h, st * P:(st + 1) * P], Q[:, h, :],
                                            start=True, stop=True)
                last.then_inc(scored, 1)
                pe.wait_ge(weighted, h + 1)
                w = Wm[h % 2]
                for st in range(TT):
                    nc.tensor.matmul(C.PS[:, 4, 0:S], C.ones[:, :], w[:, st, :], start=(st == 0), stop=(st == 1))
                for vt in range(2):
                    for st in range(TT):
                        last = nc.tensor.matmul(C.PS[:, 5 + vt, 0:S], V[:, st, h * 256 + vt * P:h * 256 + (vt + 1) * P],
                                                w[:, st, :], start=(st == 0), stop=(st == 1))
                last.then_inc(summed, 1)

        @block.vector
        def _(dve):
            link = linker(dve, chain)
            for h in range(4):
                d, w = Dm[h % 2], Wm[h % 2]
                dve.wait_ge(bcast, h + 1)
                for st in range(TT):
                    link(nc.vector.tensor_scalar(d[:, st, :], C.PS[:, 0, 0:S], ucol[:, 4 * st + h:4 * st + h + 1], 0.0,
                                                 ALU.add, ALU.min))
                dve.sem_inc(clamped, 1)
                dve.wait_ge(expd, h + 1)
                dve.wait_ge(scored, h + 1)
                for st in range(TT):
                    link(nc.vector.tensor_tensor(d[:, st, st * P:(st + 1) * P], d[:, st, st * P:(st + 1) * P], key_le, ALU.mult))
                link(nc.vector.memset(d[:, 1, 0:P], 0.0))
                for st in range(TT):
                    link(nc.vector.tensor_tensor(w[:, st, :], C.PS[:, 2 + st, 0:S], d[:, st, :], ALU.mult))
                dve.sem_inc(weighted, 1)
                dve.wait_ge(summed, h + 1)
                link(nc.vector.tensor_copy(r, C.PS[:, 4, 0:S]))
                link(nc.vector.scalar_tensor_tensor(dn, r, -1.0, r, ALU.mult, ALU.max))
                link(nc.vector.tensor_tensor(dn, dn, C.PS[:, 1, 0:S], ALU.max))
                link(nc.vector.reciprocal(r, dn))
                for vt in range(2):
                    link(nc.vector.tensor_tensor(NUM[:, 2 * h + vt, :], C.PS[:, 5 + vt, 0:S], r, ALU.mult))
                dve.sem_inc(taken, 1)

        @block.scalar
        def _(act):
            for h in range(4):
                act.wait_ge(clamped, h + 1)
                nc.scalar.activation(Dm[h % 2], Dm[h % 2], ACT.Exp).then_inc(expd, 1)

    R4 = tiles3(C.B[5], 0, 4)

    def post(link):
        for j in range(8):
            link(nc.vector.scalar_tensor_tensor(NUM[:, j, :], NUM[:, j, :], C.v("a_h_norm", j), R4[:, j // 2, :],
                                                ALU.mult, ALU.mult))
        link(nc.vector.tensor_tensor(NUM, NUM, O, ALU.mult))
    norm(C, "ml_norm", NUM, 4, 2, C.ones[:, :], 256, EPS, C.B[4], R4, post)
    tiles = cm_tiles(C, 0, NUM) + cm_tiles(C, 1, NUM)
    project(C, "ml_out", tiles, 2, add_residual(C, C.mod[:, 16:24]), on="dve")



def diff_attention(C):
    nc, t = C.nc, C.t
    Q, K_ = tiles3(C.B[0]), tiles3(C.B[1])
    V = C.B[2].rearrange("p (t v) -> p t v", t=TT)
    O = tiles3(C.B[3])
    m = C.B[9]
    rot, mask, inv = m[:, 0:P], m[:, P:2 * P], m[:, 256:257]
    cos, sin, ang, k = (m[:, 512 + i * S:512 + (i + 1) * S] for i in range(4))
    posi = m[:, 1536:1792].bitcast(I32)
    lamr = m[:, 1792:2048]
    lam = C.small[:, 16:24]
    load_small(C, "dac", [(rot, C.const("rot_b")), (mask, C.const("causal_add")), (m[:, 256:258], C.const("inv_b")),
                          (posi, t["positions"].to_broadcast([P, S])), (lamr, C.row("lam"))])

    tiles = sum([cm_tiles(C, u, C.H) for u in range(4)], []) + tm_tiles(C, 4, C.H) + tm_tiles(C, 5, C.H)

    def evict(act, i, ps):
        if i < 8:
            return nc.scalar.copy(Q[:, i, :], ps)
        if i < 16:
            return nc.scalar.copy(K_[:, i - 8, :], ps)
        a, tt = divmod(i - 16, 2)
        return nc.scalar.copy(V[:, tt, a * 512:(a + 1) * 512], ps)
    project(C, "da_in", tiles, 6, evict)

    c1 = 6.28125
    c2 = float(np.float32(np.round((2 * math.pi - c1) * 2 ** 21) / 2 ** 21))
    c3 = float(np.float32(2 * math.pi - c1 - c2))
    half = float(np.nextafter(np.float32(math.pi), np.float32(0)))
    with stage(nc, "da_rope", "chain reduced sines lam_sum lam_exp") as (block, chain, reduced, sines, lam_sum, lam_exp):
        @block.vector
        def _(dve):
            link = linker(dve, chain)
            link(nc.vector.tensor_copy(ang, posi))
            link(nc.vector.tensor_scalar(ang, ang, inv, None, ALU.mult))
            link(nc.vector.tensor_scalar(k, ang, 1 / (2 * math.pi), 12582912.0, ALU.mult, ALU.add))
            link(nc.vector.tensor_scalar(k, k, 12582912.0, None, ALU.subtract))
            for c in (c1, c2, c3):
                link(nc.vector.scalar_tensor_tensor(ang, k, -c, ang, ALU.mult, ALU.add))
            link(nc.vector.tensor_scalar(ang, ang, half, -half, ALU.min, ALU.max))
            link(nc.vector.scalar_tensor_tensor(k, ang, -1.0, ang, ALU.mult, ALU.max))
            link(nc.vector.tensor_scalar(k, k, -1.0, math.pi / 2, ALU.mult, ALU.add))
            dve.sem_inc(reduced, 1)
            for i in range(2):
                a, b = lamr[:, 128 * i:128 * i + 64], lamr[:, 128 * i + 64:128 * i + 128]
                link(nc.vector.tensor_tensor(a, a, b, ALU.mult))
                link(nc.vector.tensor_reduce(lam[:, i:i + 1], a, AX_X, ALU.add))
            dve.sem_inc(lam_sum, 1)
            dve.wait_ge(lam_exp, 1)
            link(nc.vector.tensor_scalar(lam[:, 4:5], lam[:, 2:3], lam[:, 3:4], LAM_INIT, ALU.subtract, ALU.add))
            link(nc.vector.tensor_scalar(C.small[:, 24:25], C.v("b_o_norm"), 1.0 - LAM_INIT, None, ALU.mult))

        @block.scalar
        def _(act):
            act.wait_ge(reduced, 1)
            nc.scalar.activation(sin, ang, ACT.Sin)
            nc.scalar.activation(cos, k, ACT.Sin)
            act.wait_ge(lam_sum, 1)
            nc.scalar.activation(lam[:, 2:4], lam[:, 0:2], ACT.Exp).then_inc(lam_exp, 1)

    R8 = tiles3(C.B[5])
    for name, X in (("q", Q), ("k", K_)):
        def post(link):
            link(nc.vector.scalar_tensor_tensor(X, X, C.v(f"b_{name}_norm"), R8, ALU.mult, ALU.mult))
        norm(C, f"da_{name}n", X, 8, 1, C.ones64[:, :], 64, EPS, C.B[4], R8, post)
        rope(C, f"da_{name}r", X, rot, cos, sin, C.B[4], P)

    attention(C, "da_att", [(h, qb) for h in range(8) for qb in range(TT)], 64 ** -0.5, True, 2,
              lambda h, mm, qb, nk: [(Q[64 * mm:64 * mm + 64, h, qb * P:(qb + 1) * P], K_[64 * mm:64 * mm + 64, h, 0:nk * P])],
              lambda h, kb: [(V[:, kb, h * P:(h + 1) * P], P, 0)],
              (lambda h, qb: O[:, h:h + 1, qb * P:(qb + 1) * P], lam[:, 4:5]), C.big[:, 5 * BUF:7 * BUF], mask)

    def post(link):
        link(nc.vector.scalar_tensor_tensor(O, O, C.small[:, 24:25], R8, ALU.mult, ALU.mult))
    norm(C, "da_on", O, 8, 1, C.ones[:, :], P, EPS, C.B[4], R8, post)
    project(C, "da_out", cm_tiles(C, 0, O) + cm_tiles(C, 1, O), 2, add_residual(C, C.mod[:, 16:24]), on="dve")


def rope(C, tag, X, rot, cos, sin, tmp, rows):
    nc = C.nc
    T = tiles3(tmp)
    rows = slice(0, rows)
    with stage(nc, tag, "chain turned") as (block, chain, turned):
        @block.tensor
        def _(pe):
            for j in range(8):
                last = nc.tensor.matmul(C.PS[rows, j // 2, (j % 2) * S:(j % 2 + 1) * S], rot[rows, rows], X[rows, j, :],
                                        start=True, stop=True)
            last.then_inc(turned, 1)

        @block.vector
        def _(dve):
            link = linker(dve, chain)
            dve.wait_ge(turned, 1)
            n = rows.stop
            ps = C.PS[rows, 0:4, :].rearrange("p b (h t) -> p (b h) t", t=S)
            link(nc.vector.tensor_tensor(T[rows, :, :], ps, sin[rows, :].unsqueeze(1).to_broadcast([n, 8, S]), ALU.mult))
            link(nc.vector.tensor_tensor(X[rows, :, :], X[rows, :, :], cos[rows, :].unsqueeze(1).to_broadcast([n, 8, S]), ALU.mult))
            link(nc.vector.tensor_tensor(X[rows, :, :], X[rows, :, :], T[rows, :, :], ALU.add))



def mla(C):
    nc, t = C.nc, C.t
    QS = [tiles3(C.B[0]), tiles3(C.B[1])]
    KS = [tiles3(C.B[2]), tiles3(C.B[3])]
    V = C.B[4].rearrange("p (t v) -> p t v", t=TT)
    CQ, CKV = tiles3(C.B[5], 0, 2), tiles3(C.B[5], 2, 2)
    kpe = C.B[5][:, 4 * S:5 * S]
    R = C.B[5][:, 5 * S:6 * S]
    O = tiles3(C.B[6])
    m = C.B[9]
    rot, mask = m[:, 0:P], m[:, P:2 * P]
    cos, sin = m[:, 256:512], m[:, 512:768]
    load_small(C, "mlac", [(rot, C.const("rot_m")), (mask, C.const("causal_add")), (cos, C.const("cos_m")),
                           (sin, C.const("sin_m"))])
    tiles = cm_tiles(C, 0, C.X) + cm_tiles(C, 1, C.X, m=96)

    def evict(act, i, ps):
        if i < 4:
            return nc.scalar.copy((CQ if i < 2 else CKV)[:, i % 2, :], ps)
        return nc.scalar.copy(kpe[0:96, :], ps)
    project(C, "mla_in", tiles, 2, evict)
    for name, X, w in (("q", CQ, "mla_q_norm_2"), ("kv", CKV, "mla_kv_norm_2")):
        def post(link):
            for j in range(2):
                link(nc.vector.scalar_tensor_tensor(X[:, j, :], X[:, j, :], C.v(w, j), R, ALU.mult, ALU.mult))
        norm(C, f"mla_{name}n", X, 1, 2, C.ones[:, :], 256, EPS, C.B[7], R.unsqueeze(1), post)

    wkv = C.unit(C.used + 1)
    tiles = cm_tiles(C, 0, CQ, m=96, kt=2) \
        + [(1, [(wkv[:, k, h * P:h * P + 64], CKV[:, k, :]) for k in range(2)], 64, S) for h in range(16)] \
        + [(1, [(CKV[:, k, tt * P:(tt + 1) * P],
                 wkv[:, k, g * 1024:(g + 1) * 1024].rearrange("p (h c) -> p h c", c=P)[:, :, 64:128]) for k in range(2)],
            P, 512) for g in range(2) for tt in range(TT)]

    def evict(act, i, ps):
        if i < 16:
            return nc.scalar.copy(QS[i // 8][0:96, i % 8, :], ps)
        if i < 32:
            return nc.scalar.copy(KS[(i - 16) // 8][0:64, i % 8, :], ps)
        g, tt = divmod(i - 32, 2)
        return nc.scalar.copy(V[:, tt, g * 512:(g + 1) * 512], ps)
    project(C, "mla_qkv", tiles, 2, evict)
    with stage(nc, "mla_kpe", "chain") as (block, chain):
        @block.vector
        def _(dve):
            for g in range(2):
                nc.vector.tensor_copy(KS[g][64:96, :, :], kpe[64:96, :].unsqueeze(1).to_broadcast([32, 8, S]))
    for g in range(2):
        rope(C, f"mla_rq{g}", QS[g], rot, cos, sin, C.B[7], 96)
        rope(C, f"mla_rk{g}", KS[g], rot, cos, sin, C.B[7], 96)
    attention(C, "mla_att", [(h, qb) for h in range(16) for qb in range(TT)], 96 ** -0.5, True, 1,
              lambda h, mm, qb, nk: [(QS[h // 8][0:96, h % 8, qb * P:(qb + 1) * P], KS[h // 8][0:96, h % 8, 0:nk * P])],
              lambda h, kb: [(V[:, kb, h * 64:(h + 1) * 64], 64, 0)],
              (lambda h, qb: O[64 * (h % 2):64 * (h % 2) + 64, h // 2:h // 2 + 1, qb * P:(qb + 1) * P], None),
              C.big[:, 7 * BUF:9 * BUF], mask)
    T = tiles3(C.B[0])
    project(C, "mla_out", cm_tiles(C, 0, O) + cm_tiles(C, 1, O), 2, add_alpha(C, T), on="dve")
    return T



def cross_attention(C, tag):
    nc = C.nc
    M = tiles3(C.B[0])
    Q, K_ = tiles3(C.B[1]), tiles3(C.B[2])
    V = C.B[3].rearrange("p (t v) -> p t v", t=TT)
    O = tiles3(C.B[4])
    load_small(C, tag + "m", [(M, C.t["mem_T"])])
    tiles = cm_tiles(C, 0, C.X) + cm_tiles(C, 1, C.X) + cm_tiles(C, 2, M) + cm_tiles(C, 3, M) \
        + tm_tiles(C, 4, M) + tm_tiles(C, 5, M)

    def evict(act, i, ps):
        if i < 8:
            return nc.scalar.copy(Q[:, i, :], ps)
        if i < 16:
            return nc.scalar.copy(K_[:, i - 8, :], ps)
        a, tt = divmod(i - 16, 2)
        return nc.scalar.copy(V[:, tt, a * 512:(a + 1) * 512], ps)
    project(C, tag + "in", tiles, 6, evict)
    attention(C, tag + "att", [(h, qb) for h in range(4) for qb in range(TT)], 256 ** -0.5, False, 1,
              lambda h, mm, qb, nk: [(Q[:, 2 * h + k, qb * P:(qb + 1) * P], K_[:, 2 * h + k, :]) for k in range(2)],
              lambda h, kb: [(V[:, kb, h * 256 + x * P:h * 256 + (x + 1) * P], P, x) for x in range(2)],
              (lambda h, qb: O[:, 2 * h:2 * h + 2, qb * P:(qb + 1) * P], None), C.big[:, 5 * BUF:7 * BUF], None)
    T = tiles3(C.B[0])
    project(C, tag + "out", cm_tiles(C, 0, O) + cm_tiles(C, 1, O), 2, add_alpha(C, T), on="dve")
    return T



class Moe:

    def __init__(self, C, E):
        self.E, self.cap = E, CAP
        self.htok = C.B[6].rearrange("p (t d) -> p t d", t=TT)
        self.yacc = tiles3(C.B[7])
        b = C.big[:, 8 * BUF:10 * BUF]
        self.xg = b[:, 0:1024].rearrange("p (k c) -> p k c", k=KT)
        self.yg = b[:, 1024:2048]
        self.gT = b[:, 2048:2048 + S]
        self.gT_next = b[:, 3840:3840 + S]
        self.pick = b[:, 2304:2560].rearrange("p (t c) -> p t c", t=TT)
        self.sil = b[:, 2560:3072]
        self.actT = b[:, 3072:3584].rearrange("p (f c) -> p f c", f=4)
        self.pick_w = b[:, 3584:3840].rearrange("p (t c) -> p t c", t=TT)
        self.act = C.act_rows[:, :]
        w = E + 2
        self.rank = C.route[:, 0:2 * w].rearrange("p (t e) -> p t e", t=TT)
        self.gate = C.route[:, 2 * w:4 * w].rearrange("p (t e) -> p t e", t=TT)
        self.iota = C.route[:, 136:136 + S]
        self.left = C.left
        self.ow = (C.big[:, 0:4096].rearrange("p (k n) -> p k n", k=KT),
                   C.big[:, 4096:8192].rearrange("p (k n) -> p k n", k=KT),
                   C.big[:, 8192:12288].rearrange("p (k n) -> p k n", k=4))


def pick_first(nc, link, v, iota1, hot, tmp, mx, shape):
    link(nc.vector.tensor_reduce(mx, v, AX_X, ALU.max))
    link(nc.vector.tensor_tensor(tmp, v, mx.unsqueeze(2).to_broadcast(shape), ALU.is_equal))
    link(nc.vector.scalar_tensor_tensor(tmp, tmp, -1000.0, iota1.unsqueeze(1).to_broadcast(shape), ALU.mult, ALU.add))
    link(nc.vector.tensor_reduce(mx, tmp, AX_X, ALU.min))
    link(nc.vector.tensor_tensor(hot, tmp, mx.unsqueeze(2).to_broadcast(shape), ALU.is_equal))


def route(C, tag, M, X, w_router, rows, hier):
    nc = C.nc
    E, G = M.E, 4
    per = E // G
    NL = E + G if hier else E
    b = C.B[0]
    wr = b[:, 0:KT * NL].rearrange("p (k n) -> p k n", k=KT)
    br = b[:, 288:288 + NL]
    lt = b[:, 384:384 + P]
    o = [512]

    def take(n, w=None):
        at = o[0]
        o[0] += TT * n
        return b[:, at:at + TT * n].rearrange("p (t n) -> p t n", t=TT)
    lg, sc = take(NL), take(NL)
    tmp, h1, h2, mk, sel, gs = take(E), take(E), take(E), take(E), take(E), take(E)
    pair = take(24)
    gtmp, ghot = take(G), take(G)
    mx, s1, s2, s3 = (take(1).rearrange("p t n -> p (t n)") for _ in range(4))
    cnt = take(E)
    load_small(C, tag + "c", [(wr[:, :, a:a + w.shape[1]], w.rearrange("(k p) n -> p k n", p=P)) for a, w in w_router]
               + rows(br) + [(lt, C.const("key_lt")), (M.iota, C.const("iota"))])
    iota1 = C.small[:, 32:32 + E]
    ghot_in = b[:, 1900:1912]
    sh, gsh = [P, TT, E], [P, TT, G]
    with stage(nc, tag, "chain logits sig chosen ranks ex") as (block, chain, logits, sig, chosen, ranks, ex):
        @block.tensor
        def _(pe):
            for tt in range(TT):
                for k in range(KT):
                    last = nc.tensor.matmul(C.PS[:, tt, 0:NL], X[:, k, tt * P:(tt + 1) * P], wr[:, k, :],
                                            start=(k == 0), stop=(k == KT - 1))
            last.then_inc(logits, 1)
            for tt in range(TT):
                for k in range(KT):
                    last = nc.tensor.transpose(C.PS[:, 4 + 2 * tt + k // 4, (k % 4) * P:(k % 4 + 1) * P],
                                               X[:, k, tt * P:(tt + 1) * P], C.ident[:, :])
            last.then_inc(logits, 1)
            pe.wait_ge(chosen, 1)
            nc.tensor.matmul(C.PS[:, 2, 0:E], lt, sel[:, 0, :], start=True, stop=True)
            nc.tensor.matmul(C.PS[:, 2, 64:64 + E], lt, sel[:, 1, :], start=True, stop=False)
            nc.tensor.matmul(C.PS[:, 2, 64:64 + E], C.ones[:, :], sel[:, 0, :], start=False, stop=True)
            for tt in range(TT):
                last = nc.tensor.matmul(C.PS[:, 3, 0:E], C.ones[:, :], sel[:, tt, :], start=(tt == 0), stop=(tt == 1))
            last.then_inc(ranks, 1)

        @block.scalar
        def _(act):
            act.wait_ge(logits, 1)
            lps = C.PS[:, 0:2, 0:NL]
            if hier:
                nc.scalar.copy(lg, lps).then_inc(sig, 1)
            else:
                nc.scalar.activation(lg, lps, ACT.Sigmoid).then_inc(sig, 1)
            act.wait_ge(logits, 2)
            for tt in range(TT):
                nc.scalar.copy(M.htok[:, tt, :], C.PS[:, 4 + 2 * tt:6 + 2 * tt, :].rearrange("p b n -> p (b n)"))
            if hier:
                act.wait_ge(ex, 1)
                nc.scalar.activation(ghot_in[:, 0:10], ghot_in[:, 0:10], ACT.Exp).then_inc(sig, 1)

        @block.vector
        def _(dve):
            link = linker(dve, chain)
            dve.wait_ge(sig, 1)
            link(nc.vector.tensor_scalar(iota1, M.iota[:, 0:E], 1001.0, None, ALU.add))
            link(nc.vector.tensor_tensor(sc, lg, br.unsqueeze(1).to_broadcast([P, TT, NL]), ALU.add))
            if hier:
                gsc, esc = sc[:, :, 0:G], sc[:, :, G:NL]
            else:
                esc = sc
                gsc = gtmp
                v = sc.rearrange("p t (g e) -> p (t g) e", e=per)
                pv = pair.rearrange("p t n -> p (t n)")[:, 0:48].rearrange("p (g n) -> p g n", n=6)
                TG = TT * G
                link(nc.vector.tensor_tensor(pv[:, :, 0:3], v[:, :, 1:4], v[:, :, 0:1].to_broadcast([P, TG, 3]), ALU.add))
                link(nc.vector.tensor_tensor(pv[:, :, 3:5], v[:, :, 2:4], v[:, :, 1:2].to_broadcast([P, TG, 2]), ALU.add))
                link(nc.vector.tensor_tensor(pv[:, :, 5:6], v[:, :, 3:4], v[:, :, 2:3], ALU.add))
                link(nc.vector.tensor_reduce(gsc.rearrange("p t g -> p (t g)"), pv, AX_X, ALU.max))
            gt = gs[:, :, 0:G]
            if hier:
                link(nc.vector.tensor_reduce(s3, gsc, AX_X, ALU.max))
                gin = ghot_in[:, 0:8].rearrange("p (t g) -> p t g", t=TT)
                link(nc.vector.tensor_tensor(gin, gsc, s3.unsqueeze(2).to_broadcast(gsh), ALU.subtract))
            pick_first(nc, link, gsc, iota1[:, 0:G], ghot, gt, mx, gsh)
            link(nc.vector.tensor_scalar(gt, ghot, 1.0, -NEG, ALU.subtract, ALU.mult))
            for tt in range(TT):
                g3 = lambda x: x[:, tt, :].rearrange("p (g e) -> p g e", e=per)
                link(nc.vector.tensor_tensor(g3(mk), g3(esc), ghot[:, tt, :].unsqueeze(2).to_broadcast([P, G, per]), ALU.mult))
                link(nc.vector.tensor_tensor(g3(mk), g3(mk), gt[:, tt, :].unsqueeze(2).to_broadcast([P, G, per]), ALU.add))
            if hier:
                link(nc.vector.tensor_reduce(s1, mk, AX_X, ALU.max))
            pick_first(nc, link, mk, iota1, h1, tmp, mx, sh)
            link(nc.vector.scalar_tensor_tensor(mk, h1, 2 * NEG, mk, ALU.mult, ALU.add))
            if hier:
                link(nc.vector.tensor_reduce(s2, mk, AX_X, ALU.max))
                link(nc.vector.tensor_tensor(ghot_in[:, 8:10], s2, s1, ALU.subtract))
                dve.sem_inc(ex, 1)
            pick_first(nc, link, mk, iota1, h2, tmp, mx, sh)
            link(nc.vector.tensor_tensor(sel, h1, h2, ALU.add))
            dve.sem_inc(chosen, 1)
            link(nc.vector.memset(M.gate[:, :, E:E + 2], 0.0))
            link(nc.vector.memset(M.rank[:, :, E:E + 2], -1.0))
            gate = M.gate[:, :, 0:E]
            if hier:
                dve.wait_ge(sig, 2)
                e2 = ghot_in[:, 8:10]
                link(nc.vector.tensor_reduce(s1, ghot_in[:, 0:8].rearrange("p (t g) -> p t g", t=TT), AX_X, ALU.add))
                link(nc.vector.tensor_scalar(s2, e2, 1.0, None, ALU.add))
                link(nc.vector.tensor_tensor(s1, s1, s2, ALU.mult))
                link(nc.vector.reciprocal(s1, s1))
                link(nc.vector.tensor_tensor(s2, s1, e2, ALU.mult))
                link(nc.vector.tensor_tensor(gate, h1, s1.unsqueeze(2).to_broadcast(sh), ALU.mult))
                link(nc.vector.tensor_tensor(tmp, h2, s2.unsqueeze(2).to_broadcast(sh), ALU.mult))
                link(nc.vector.tensor_tensor(gate, gate, tmp, ALU.add))
            else:
                link(nc.vector.tensor_tensor(tmp, lg, sel, ALU.mult))
                link(nc.vector.tensor_reduce(s1, tmp, AX_X, ALU.add))
                link(nc.vector.reciprocal(s1, s1))
                link(nc.vector.tensor_tensor(gate, tmp, s1.unsqueeze(2).to_broadcast(sh), ALU.mult))
            dve.wait_ge(ranks, 1)
            rank = M.rank[:, :, 0:E]
            link(nc.vector.scalar_tensor_tensor(tmp, C.PS[:, 2, 0:128].rearrange("p (t n) -> p t n", t=TT)[:, :, 0:E], 1.0,
                                                sel, ALU.add, ALU.mult))
            link(nc.vector.tensor_scalar(rank, tmp, -1.0, None, ALU.add))
            n = 3 * E
            o1 = lambda i: C.B[1][0:1, i * 96:i * 96 + n]
            live, before, key, hit, one = o1(0), o1(1), o1(2), o1(3), o1(4)
            r3 = lambda x: x.rearrange("p (b e) -> p b e", b=3)
            for i in range(3):
                link(nc.vector.tensor_scalar(live[:, i * E:(i + 1) * E], C.PS[0:1, 3, 0:E], float((i + 1) * M.cap), None,
                                             ALU.is_gt))
                link(nc.vector.tensor_copy(r3(key)[:, i, :], M.iota[0:1, 0:E]))
            link(nc.vector.memset(one, 1.0))
            link(nc.vector.tensor_tensor_scan(before, one, live, 0.0, ALU.mult, ALU.add))
            link(nc.vector.tensor_copy(M.left[:, 0:1], before[:, n - 1:n]))
            link(nc.vector.tensor_tensor(before, before, live, ALU.mult))
            lst = C.B[1][0:1, 512:512 + 16]
            for j in range(MAXLEFT):
                link(nc.vector.tensor_scalar(hit, before, float(j + 1), None, ALU.is_equal))
                link(nc.vector.tensor_tensor(one, hit, key, ALU.mult))
                link(nc.vector.tensor_reduce(lst[:, j:j + 1], one, AX_X, ALU.add))
                for i in range(3):
                    link(nc.vector.tensor_scalar(r3(one)[:, i, :], r3(hit)[:, i, :], float((i + 1) * M.cap), None, ALU.mult))
                link(nc.vector.tensor_reduce(lst[:, 8 + j:9 + j], one, AX_X, ALU.add))
            link(nc.vector.tensor_copy(M.left[:, 1:17], lst))


def build_pick(nc, M, e, done):
    for tt in range(TT):
        for x in range(2):
            col = bass.ds(e + x, 1)
            c = slice(64 * x, 64 * x + 64)
            nc.vector.tensor_scalar(M.pick[:, tt, c], M.iota[:, 0:64], M.rank[:, tt, col], None, ALU.is_equal)
            last = nc.vector.tensor_scalar(M.pick_w[:, tt, c], M.iota[:, 0:64], M.rank[:, tt, col], M.gate[:, tt, col],
                                           ALU.is_equal, ALU.mult)
    last.then_inc(done, 1)


def gather(C, M, w, done):
    nc = C.nc
    for k in range(KT):
        for tt in range(TT):
            nc.tensor.matmul(C.PS[:, k // 4, (k % 4) * P:(k % 4) * P + w], M.htok[:, tt, k * P:(k + 1) * P],
                             M.pick[:, tt, 0:w], start=(tt == 0), stop=(tt == 1))
    for tt in range(TT):
        last = nc.tensor.transpose(C.PS[0:w, 3, tt * P:(tt + 1) * P], M.pick_w[:, tt, 0:w], C.ident[:, :])
    last.then_inc(done, 1)


def take_gathered(C, M, w, done):
    nc = C.nc
    for g in range(2):
        nc.scalar.copy(M.xg[:, 4 * g:4 * g + 4, 0:w], C.PS[:, g, :].rearrange("p (k c) -> p k c", c=P)[:, :, 0:w])
    nc.scalar.copy(M.gT_next[0:w, :], C.PS[0:w, 3, 0:S]).then_inc(done, 1)


def row_product(C, x, ws, bank, col=slice(None)):
    nc = C.nc
    n = x.shape[1]
    for k in range(n):
        for i, w in enumerate(ws):
            last = nc.tensor.matmul(C.PS[64 * i:64 * i + 64, bank, :], x[:, k, 64 * i:64 * i + 64], w[:, k, col],
                                    start=(k == 0), stop=(k == n - 1))
    return last


def turn_act(C, M, w, bank):
    nc = C.nc
    for f in range(4):
        last = nc.tensor.transpose(C.PS[:, bank, f * P:f * P + w], M.act[0:w, f * P:(f + 1) * P], C.ident[0:w, 0:w])
    return last


def scatter_quarter(C, M, q, w, bank, gT):
    nc = C.nc
    for j in range(2):
        d = 2 * q + j
        last = nc.tensor.matmul(C.PS[:, bank, j * S:(j + 1) * S], M.yg[0:w, d * P:(d + 1) * P], gT[0:w, :],
                                start=True, stop=True)
    return last


def accumulate(C, M, q, bank, done):
    nc = C.nc
    y = M.yacc[:, 2 * q:2 * q + 2, :].rearrange("p j t -> p (j t)")
    nc.vector.tensor_tensor(y, y, C.PS[:, bank, :], ALU.add).then_inc(done, 1)


def experts(C, tag, M, sources):
    nc = C.nc
    E, u0 = M.E, C.used
    pairs = E // 2
    SB = (7, 5, 6, 7)
    names = "picked gathered taken gate_done up_done silu_done act_ready act_turned actT_ready down_done y_taken scattered added gT_moved"
    with stage(nc, tag, names) as (block, picked, gathered, taken, gate_done, up_done, silu_done, act_ready, act_turned,
                                   actT_ready, down_done, y_taken, scattered, added, gT_moved):
        @block.sync
        def _(sp):
            with sp.Fori(0, pairs - 1) as i:
                for j in range(6):
                    v = u0 + RING + j
                    src = sources[j // 2](2 * i + (2 + j % 2))
                    sp.wait_ge(C.slot_free[v % RING], i + v // RING)
                    sp.dma_start(C.unit(v), src).then_inc(C.slot_loaded[v % RING], 16)
            C.refill(sp, u0 + 6 * (pairs - 1), 6)

        @block.tensor
        def _(pe):
            def arrived(i, j):
                for u in (u0 + j, u0 + j + 1):
                    pe.wait_ge(C.slot_loaded[u % RING], i * 16 + 16 * (u // RING + 1))

            def scatter(p):
                pe.wait_ge(y_taken, 2 * p + 2)
                pe.wait_ge(added, 4 * p + 1)
                for q in range(4):
                    if q == 3:
                        pe.wait_ge(added, 4 * p + 2)
                    scatter_quarter(C, M, q, P, SB[q], M.gT).then_inc(scattered, 1)
            pe.wait_ge(picked, 1)
            gather(C, M, P, gathered)
            with pe.Fori(0, pairs) as p:
                pe.wait_ge(taken, p + 1)
                arrived(p, 0)
                row_product(C, M.xg, [C.unit(u0), C.unit(u0 + 1)], 2).then_inc(gate_done, 1)
                arrived(p, 2)
                row_product(C, M.xg, [C.unit(u0 + 2), C.unit(u0 + 3)], 3).then_inc(up_done, 1)
                scatter(p)
                pe.wait_ge(act_ready, p + 1)
                turn_act(C, M, P, 4).then_inc(act_turned, 1)
                pe.wait_ge(picked, p + 2)
                gather(C, M, P, gathered)
                pe.wait_ge(actT_ready, p + 1)
                pe.wait_ge(added, 4 * p + 4)
                arrived(p, 4)
                for half in range(2):
                    row_product(C, M.actT, [C.unit(u0 + 4), C.unit(u0 + 5)], 5 + half,
                                slice(half * 512, (half + 1) * 512)).then_inc(down_done, 1)
            scatter(pairs)

        @block.scalar
        def _(act):
            act.wait_ge(gathered, 1)
            take_gathered(C, M, P, taken)
            with act.Fori(0, pairs) as p:
                act.wait_ge(gate_done, p + 1)
                for j in range(2):
                    act.sem_inc(C.freed(u0 + j), 1)
                nc.scalar.activation(M.sil, C.PS[:, 2, :], ACT.Silu).then_inc(silu_done, 1)
                act.wait_ge(act_turned, p + 1)
                nc.scalar.copy(M.actT, C.PS[:, 4, :].rearrange("p (f c) -> p f c", c=P)).then_inc(actT_ready, 1)
                act.wait_ge(gathered, p + 2)
                nc.scalar.copy(M.gT, M.gT_next).then_inc(gT_moved, 1)
                act.wait_ge(gT_moved, p + 1)
                take_gathered(C, M, P, taken)
                for half in range(2):
                    act.wait_ge(down_done, 2 * p + (half + 1))
                    if half:
                        for j in range(4, 6):
                            act.sem_inc(C.freed(u0 + j), 1)
                    nc.scalar.copy(M.yg[:, half * 512:(half + 1) * 512], C.PS[:, 5 + half, :]).then_inc(y_taken, 1)

        @block.vector
        def _(dve):
            nc.vector.memset(M.gT, 0.0).then_inc(y_taken, 1)
            nc.vector.memset(M.yg, 0.0).then_inc(y_taken, 1)
            nc.vector.memset(M.yacc, 0.0).then_inc(added, 1)
            build_pick(nc, M, 0, picked)
            with dve.Fori(0, pairs) as p:
                dve.wait_ge(gathered, p + 1)
                build_pick(nc, M, 2 * p + 2, picked)
                dve.wait_ge(silu_done, p + 1)
                dve.wait_ge(up_done, p + 1)
                for j in range(2, 4):
                    dve.sem_inc(C.freed(u0 + j), 1)
                nc.vector.tensor_tensor(M.act, M.sil, C.PS[:, 3, :], ALU.mult).then_inc(act_ready, 1)
                for q in range(4):
                    dve.wait_ge(scattered, 4 * p + (q + 1))
                    accumulate(C, M, q, SB[q], added)
            for q in range(4):
                dve.wait_ge(scattered, 4 * pairs + q + 1)
                accumulate(C, M, q, SB[q], added)
    C.used += 6 * pairs


def experts_left(C, tag, M, sources):
    nc = C.nc
    names = "loaded picked gathered taken gate_done silu_done act_ready act_turned actT_ready down_done y_taken scattered added"
    with stage(nc, tag, names) as (block, loaded, picked, gathered, taken, gate_done, silu_done, act_ready, act_turned,
                                   actT_ready, down_done, y_taken, scattered, added):
        def blocks(eng, body):
            count = eng.value_load(M.left[0:1, 0:1], min_val=0, max_val=MAXLEFT)
            with eng.If(count > 0):
                with eng.Fori(0, count) as n:
                    body(n)

        def entry(eng, at, n, top):
            return eng.value_load(M.left[0:1, bass.ds(n + at, 1)], min_val=0, max_val=top)

        @block.sync
        def _(sp):
            def body(n):
                e = entry(sp, 1, n, M.E - 1)
                srcs = [s(e) for s in sources]
                sp.wait_ge(down_done, n + 1)
                for dst, src in zip(M.ow, srcs):
                    sp.dma_start(dst, src).then_inc(loaded, 16)
            blocks(sp, body)

        @block.tensor
        def _(pe):
            pe.sem_inc(down_done, 1)

            def body(n):
                pe.wait_ge(added, n + 1)
                pe.wait_ge(picked, n + 1)
                gather(C, M, 64, gathered)
                pe.wait_ge(taken, n + 1)
                pe.wait_ge(loaded, n * 48 + 48)
                row_product(C, M.xg, [M.ow[0]], 2)
                row_product(C, M.xg, [M.ow[1]], 3).then_inc(gate_done, 1)
                pe.wait_ge(act_ready, n + 1)
                turn_act(C, M, P, 4).then_inc(act_turned, 1)
                pe.wait_ge(actT_ready, n + 1)
                row_product(C, M.actT, [M.ow[2]], 5, slice(0, 512))
                row_product(C, M.actT, [M.ow[2]], 6, slice(512, 1024)).then_inc(down_done, 1)
                pe.wait_ge(y_taken, n + 1)
                for q in range(4):
                    last = scatter_quarter(C, M, q, 64, q, M.gT_next)
                last.then_inc(scattered, 1)
            blocks(pe, body)

        @block.scalar
        def _(act):
            def body(n):
                act.wait_ge(gathered, n + 1)
                take_gathered(C, M, 64, taken)
                act.wait_ge(gate_done, n + 1)
                nc.scalar.activation(M.sil[0:64, :], C.PS[0:64, 2, :], ACT.Silu).then_inc(silu_done, 1)
                act.wait_ge(act_turned, n + 1)
                nc.scalar.copy(M.actT[:, :, 0:64],
                               C.PS[:, 4, :].rearrange("p (f c) -> p f c", c=P)[:, :, 0:64]).then_inc(actT_ready, 1)
                act.wait_ge(down_done, n + 2)
                nc.scalar.copy(M.yg[0:64, :], C.PS[0:64, 5:7, :].rearrange("p b n -> p (b n)")).then_inc(y_taken, 1)
            blocks(act, body)

        @block.vector
        def _(dve):
            dve.sem_inc(added, 1)

            def body(n):
                e, first = entry(dve, 1, n, M.E - 1), entry(dve, 9, n, S - 64)
                for tt in range(TT):
                    col = bass.ds(e, 1)
                    want = M.iota[:, bass.ds(first, 64)]
                    nc.vector.tensor_scalar(M.pick[:, tt, 0:64], want, M.rank[:, tt, col], None, ALU.is_equal)
                    last = nc.vector.tensor_scalar(M.pick_w[:, tt, 0:64], want, M.rank[:, tt, col], M.gate[:, tt, col],
                                                   ALU.is_equal, ALU.mult)
                last.then_inc(picked, 1)
                dve.wait_ge(silu_done, n + 1)
                nc.vector.tensor_tensor(M.act[0:64, :], M.sil[0:64, :], C.PS[0:64, 3, :], ALU.mult).then_inc(act_ready, 1)
                dve.wait_ge(scattered, n + 1)
                y = M.yacc.rearrange("p j t -> p (j t)")
                nc.vector.tensor_tensor(y, y, C.PS[:, 0:4, :].rearrange("p b n -> p (b n)"), ALU.add).then_inc(added, 1)
            blocks(dve, body)


def moe1(C, tag, l):
    t = C.t
    M = Moe(C, 16)
    route(C, tag + "r", M, C.H, [(0, t["w_router"])], lambda br: [(br, C.row("router_bias"))], False)
    gu = t["moe_w_gu"][l].rearrange("e (k p) n -> e p k n", p=P)
    dn = t["moe_w_down"][l].rearrange("e (k p) n -> e p k n", p=P)
    src = (lambda e: gu[e, :, :, 0:512], lambda e: gu[e, :, :, 512:1024], lambda e: dn[e])
    experts(C, tag + "e", M, src)
    experts_left(C, tag + "o", M, src)
    nc = C.nc
    with stage(nc, tag + "x", "done") as (block, done):
        @block.vector
        def _(dve):
            for k in range(KT):
                nc.vector.scalar_tensor_tensor(C.X[:, k, :], M.yacc[:, k, :], C.mod[:, 40 + k:41 + k], C.X[:, k, :],
                                               ALU.mult, ALU.add)


def moe2(C, tag, l):
    t = C.t
    M = Moe(C, 32)
    route(C, tag + "r", M, C.X, [(0, t["moe_w_group_2"][l]), (4, t["moe_w_expert_2"][l])],
          lambda br: [(br[:, 0:4], C.row("moe_b_group_2", 4 * l, 4)), (br[:, 4:36], C.row("moe_b_expert_2", 32 * l, 32))], True)
    v = lambda w: w[l].rearrange("e (k p) n -> e p k n", p=P)
    g, u, d = v(t["moe_w_gate_2"]), v(t["moe_w_up_2"]), v(t["moe_w_down_2"])
    src = (lambda e: g[e], lambda e: u[e], lambda e: d[e])
    experts(C, tag + "e", M, src)
    experts_left(C, tag + "o", M, src)
    T = M.yacc
    nc = C.nc
    with stage(nc, tag + "x", "done") as (block, done):
        @block.vector
        def _(dve):
            nc.vector.scalar_tensor_tensor(T, C.X[:, :, :], ALPHA, T, ALU.mult, ALU.add)
    return T



def spatial_gating(C, U, Z, out):
    nc, t = C.nc, C.t
    W = C.B[3]
    ws = W[:, 0:512].rearrange("p (g t) -> p g t", g=4)
    lng, lnb = W[:, 512:1024], W[:, 1024:1536]
    bs = W[:, 1536:2048].rearrange("p (g t) -> p g t", g=4)
    q = C.B[4][:, 0:1024]
    le = C.B[4][:, 1024:1152]
    mean, var = C.B[4][:, 1152:1160], C.B[4][:, 1160:1168]
    load_small(C, "sgc", [(ws, t["sg_ws_T"]), (lng, C.row("sg_ln_g_2")), (lnb, C.row("sg_ln_b_2")),
                          (W[:, 1536:2048], C.row("sg_b_2")), (le, C.const("key_le"))])
    z = Z.rearrange("p t (g c) -> p (t g) c", g=4)
    q3 = q.rearrange("p (a c) -> p a c", c=P)
    full = lambda x: x.unsqueeze(2).to_broadcast([P, 8, P])
    with stage(nc, "sg", "chain var root gained mixed") as (block, chain, var_done, root, gained, mixed):
        @block.vector
        def _(dve):
            link = linker(dve, chain)
            link(nc.vector.tensor_tensor(ws, ws, le.unsqueeze(1).to_broadcast([P, 4, P]), ALU.mult))
            link(nc.vector.tensor_reduce(mean, z, AX_X, ALU.add))
            link(nc.vector.tensor_scalar(mean, mean, 1.0 / P, None, ALU.mult))
            link(nc.vector.tensor_tensor(z, z, full(mean), ALU.subtract))
            link(nc.vector.tensor_tensor(q3, z, z, ALU.mult))
            link(nc.vector.tensor_reduce(var, q3, AX_X, ALU.add))
            link(nc.vector.tensor_scalar(var, var, 1.0 / P, LN_EPS, ALU.mult, ALU.add))
            dve.sem_inc(var_done, 1)
            dve.wait_ge(root, 1)
            link(nc.vector.reciprocal(var, var))
            link(nc.vector.tensor_tensor(z, z, full(var), ALU.mult))
            for tt in range(TT):
                link(nc.vector.tensor_tensor(Z[:, tt, :], Z[:, tt, :], lng, ALU.mult))
                link(nc.vector.tensor_tensor(Z[:, tt, :], Z[:, tt, :], lnb, ALU.add))
            dve.sem_inc(gained, 1)
            dve.wait_ge(mixed, 1)
            for g in range(4):
                for tt in range(TT):
                    i = 2 * g + tt
                    c = slice(tt * P, (tt + 1) * P)
                    link(nc.vector.tensor_tensor(q3[:, i, :], C.PS[:, i // 4, (i % 4) * P:(i % 4 + 1) * P], bs[:, g, :], ALU.add))
                    link(nc.vector.tensor_tensor(out[:, g, c], q3[:, i, :], U[:, g, c], ALU.mult))

        @block.scalar
        def _(act):
            act.wait_ge(var_done, 1)
            nc.scalar.activation(var, var, ACT.Sqrt).then_inc(root, 1)

        @block.tensor
        def _(pe):
            pe.wait_ge(gained, 1)
            for g in range(4):
                for tt in range(TT):
                    i = 2 * g + tt
                    last = nc.tensor.matmul(C.PS[:, i // 4, (i % 4) * P:(i % 4 + 1) * P], Z[:, tt, g * P:(g + 1) * P],
                                            ws[:, g, :], start=True, stop=True)
            last.then_inc(mixed, 1)


def mixer_ab(C):
    nc, t = C.nc, C.t
    B = C.B
    half = lambda b, i: tiles3(b, 4 * i, 4)
    PR = C.big[:, 0:14 * S].rearrange("p (j t) -> p j t", t=S)
    DF = C.big[:, 3 * BUF:3 * BUF + 14 * S].rearrange("p (j t) -> p j t", t=S)
    U = half(B[2], 0)
    Z = B[2][:, 1024:2048].rearrange("p (t c) -> p t c", t=TT)
    MIX = tiles3(B[9])

    tiles = sum([cm_tiles(C, u, C.X) for u in range(5)], []) + tm_tiles(C, 5, C.X)

    def evict(act, i, ps):
        if i < 14:
            return nc.scalar.copy(PR[:, i, :], ps)
        if i < 18:
            return nc.scalar.activation(U[:, i - 14, :], ps, ACT.Gelu_apprx_tanh)
        return nc.scalar.activation(Z[:, i - 18, :], ps, ACT.Gelu_apprx_tanh)
    project(C, "ab_in", tiles, 6, evict)
    spatial_gating(C, U, Z, MIX[:, 4:8, :])

    w2, g2 = B[5][:, 0:512], B[5][:, 512:1024]
    load_small(C, "rwc", [(w2[0:64, :], t["rw_w2_2"]), (w2[64:128, :], t["rw_a2_2"]), (g2, t["rw_g2_2"])])
    with stage(nc, "rw_shift", "chain shifted") as (block, chain, shifted):
        @block.vector
        def _(dve):
            link = linker(dve, chain)
            link(nc.vector.tensor_tensor(DF[:, :, 1:S], PR[:, :, 0:S - 1], PR[:, :, 1:S], ALU.subtract))
            link(nc.vector.tensor_scalar(DF[:, :, 0:1], PR[:, :, 0:1], -1.0, None, ALU.mult))
            for j in range(14):
                link(nc.vector.scalar_tensor_tensor(PR[:, j, :], DF[:, j, :], C.v("ab_mu_2", j), PR[:, j, :],
                                                    ALU.mult, ALU.add))
            dve.sem_inc(shifted, 1)

        @block.scalar
        def _(act):
            act.wait_ge(shifted, 1)
            nc.scalar.activation(PR[0:64, 12, :], PR[0:64, 12, :], ACT.Tanh)
            nc.scalar.activation(PR[:, 13, :], PR[:, 13, :], ACT.Sigmoid)
    r, k, v = PR[:, 0:4, :], PR[:, 4:8, :], PR[:, 8:12, :]
    A, G = half(B[3], 0), half(B[3], 1)
    LW, CS = half(B[4], 0), half(B[4], 1)
    tiles = [(None, [(w2[0:64, j * P:(j + 1) * P], PR[0:64, 12, :])], P, S) for j in range(4)] \
        + [(None, [(w2[64:128, j * P:(j + 1) * P], PR[64:128, 12, :])], P, S) for j in range(4)] \
        + [(None, [(g2[:, j * P:(j + 1) * P], PR[:, 13, :])], P, S) for j in range(4)]

    def evict(act, i, ps):
        if i < 4:
            return nc.scalar.activation(LW[:, i, :], ps, ACT.Sigmoid, bias=C.v("rw_w0_2", i))
        if i < 8:
            return nc.scalar.activation(A[:, i - 4, :], ps, ACT.Sigmoid, bias=C.v("rw_a0_2", i - 4))
        return nc.scalar.copy(G[:, i - 8, :], ps)
    project(C, "rw_lora", tiles, 0, evict)

    KK, BV = half(B[5], 0), half(B[5], 1)
    K2, E = half(B[6], 0), half(B[6], 1)
    At, Bt, Kt, Rt = half(B[7], 0), half(B[7], 1), half(B[8], 0), half(B[8], 1)
    RN = half(B[8], 1)
    BON = A
    flat = lambda x: x.rearrange("p j t -> p (j t)")
    PC = C.small[:, 32:64].rearrange("p (j c) -> p j c", j=4)
    with stage(nc, "rw_kk", "chain") as (block, chain):
        @block.vector
        def _(dve):
            for j in range(4):
                nc.vector.tensor_scalar(KK[:, j, :], k[:, j, :], C.v("rw_k_k_2", j), None, ALU.mult)

    def post(link):
        link(nc.vector.tensor_tensor(KK, KK, RN, ALU.mult))
        link(nc.vector.tensor_tensor(BV, KK, A, ALU.mult))
        for j in range(4):
            link(nc.vector.tensor_scalar(K2[:, j, :], A[:, j, :], 1.0, C.v("rw_k_a_2", j), ALU.subtract, ALU.mult))
        link(nc.vector.scalar_tensor_tensor(K2, K2, 1.0, k, ALU.add, ALU.mult))
        link(nc.vector.tensor_scalar(LW, LW, -math.exp(-0.5), None, ALU.mult))
        link(nc.vector.memset(E, 1.0))
        link(nc.vector.memset(flat(E).rearrange("p (n c) -> p n c", c=RC)[:, :, 0:1], 0.0))
        link(nc.vector.tensor_tensor_scan(flat(CS), flat(E), flat(LW), 0.0, ALU.mult, ALU.add))
        link(nc.vector.tensor_tensor(LW, CS, LW, ALU.subtract))
        for j in range(4):
            link(nc.vector.scalar_tensor_tensor(E[:, j, :], r[:, j, :], C.v("rw_r_k_2", j), K2[:, j, :], ALU.mult, ALU.mult))
    norm(C, "rw_kkn", KK, 4, 1, C.ones64[:, :], 1, 0.0, At, RN, post, floor=1e-12)

    with stage(nc, "rw_scale", "chain expd used bonus") as (block, chain, expd, used, bonus):
        @block.tensor
        def _(pe):
            for j in range(4):
                last = nc.tensor.matmul(C.PS[:, j // 2, (j % 2) * S:(j % 2 + 1) * S], C.ones64[:, :], E[:, j, :],
                                        start=True, stop=True)
            last.then_inc(bonus, 1)

        @block.scalar
        def _(act):
            nc.scalar.activation(At, LW, ACT.Exp).then_inc(expd, 1)
            nc.scalar.activation(Rt, CS, ACT.Exp).then_inc(expd, 1)
            nc.scalar.activation(Bt, CS, ACT.Exp, scale=-1.0).then_inc(expd, 1)

        @block.vector
        def _(dve):
            link = linker(dve, chain)
            dve.wait_ge(bonus, 1)
            link(nc.vector.tensor_tensor(BON, C.PS[:, 0:2, :].rearrange("p b (h t) -> p (b h) t", t=S), v, ALU.mult))
            dve.wait_ge(expd, 3)
            link(nc.vector.tensor_copy(PC, flat(Rt).rearrange("p (j c u) -> p j c u", j=4, u=RC)[:, :, :, RC - 1]))
            link(nc.vector.tensor_tensor(Kt, K2, Bt, ALU.mult))
            link(nc.vector.tensor_tensor(Bt, BV, Bt, ALU.mult))
            link(nc.vector.tensor_tensor(Rt, r, Rt, ALU.mult))
            link(nc.vector.scalar_tensor_tensor(At, At, -1.0, KK, ALU.mult, ALU.mult))

    Btok, Ktok = (B[4][:, i * 1024:(i + 1) * 1024].rearrange("p (t c) -> p t c", t=TT) for i in range(2))
    Htok, Vtok = (B[2][:, i * 1024:(i + 1) * 1024].rearrange("p (t c) -> p t c", t=TT) for i in range(2))
    with stage(nc, "rw_tok", "turned") as (block, turned):
        srcs = ((v, Vtok), (Bt, Btok), (Kt, Ktok))

        @block.tensor
        def _(pe):
            for n, (src, _) in enumerate(srcs):
                for tt in range(TT):
                    for j in range(4):
                        last = nc.tensor.transpose(C.PS[:, 2 * n + tt, j * P:(j + 1) * P], src[:, j, tt * P:(tt + 1) * P],
                                                   C.ident[:, :])
                last.then_inc(turned, 1)

        @block.scalar
        def _(act):
            for n, (_, dst) in enumerate(srcs):
                act.wait_ge(turned, n + 1)
                nc.scalar.copy(dst, C.PS[:, 2 * n:2 * n + 2, :])

    m8 = lambda x: x.rearrange("p (h c) -> p h c", c=P)
    UM, UT = m8(B[0][:, 0:1024]), m8(B[0][:, 1024:2048])
    OT, NT = m8(B[1][:, 0:1024]), m8(B[1][:, 1024:2048])
    X0 = m8(B[9][:, 0:1024])
    Hf = C.H[:, :, :].rearrange("p j t -> p (j t)")
    WT = m8(Hf[:, 0:1024])
    masks = [Hf[:, 1024 + i * P:1024 + (i + 1) * P] for i in range(5)]
    load_small(C, "rwm", [(masks[i], C.const(n)) for i, n in enumerate(("rw_d", "rw_dT", "rw_oT", "rw_ltT", "rw_leT"))])
    m_d, m_dT, m_oT, m_ltT, m_leT = (x.unsqueeze(1).to_broadcast([P, 8, P]) for x in masks)
    ident8 = C.ident[:, :].unsqueeze(1).to_broadcast([P, 8, P])
    MB, MK = (b.rearrange("p (t h c) -> p t h c", t=TT, h=8) for b in (B[5], B[6]))
    GT = At
    Y, Zs = UM, UT

    def bank8(b):
        return C.PS[:, b:b + 2, :].rearrange("p b (h c) -> p (b h) c", c=P)

    for tb in range(TT):
        tc = slice(tb * P, (tb + 1) * P)
        rows = [(slice(64 * (i // 4), 64 * (i // 4) + 64), i % 4) for i in range(8)]
        hcol = [slice(P * (i % 4) + 64 * (i // 4), P * (i % 4) + 64 * (i // 4) + 64) for i in range(8)]

        def products(pe, bank, lhs, rhs):
            for i, (rw, pair) in enumerate(rows):
                last = nc.tensor.matmul(bank8(bank)[:, i, :], lhs[rw, pair, tc], rhs[rw, pair, tc], start=True, stop=True)
            return last

        def each(bank, lhs, rhs):
            for i in range(8):
                last = nc.tensor.matmul(bank8(bank)[:, i, 0:rhs.shape[2]], lhs[:, i, :], rhs[:, i, :], start=True, stop=True)
            return last

        with stage(nc, f"rw_mat{tb}", "chain product masked turned a_taken") as (block, chain, product, masked, turned, a_taken):
            @block.tensor
            def _(pe):
                products(pe, 0, Bt, At).then_inc(product, 1)
                products(pe, 2, At, Bt).then_inc(product, 1)
                products(pe, 4, Kt, At).then_inc(product, 1)
                products(pe, 6, Bt, Rt).then_inc(product, 1)
                pe.wait_ge(masked, 1)
                products(pe, 0, Kt, Rt).then_inc(product, 1)
                pe.wait_ge(masked, 2)
                for j in range(4):
                    last = nc.tensor.transpose(C.PS[:, 2, j * P:(j + 1) * P], At[:, j, tc], C.ident[:, :])
                last.then_inc(turned, 1)
                pe.wait_ge(masked, 3)
                for i in range(8):
                    last = nc.tensor.matmul(C.PS[:, 4, i * 64:(i + 1) * 64], NT[:, i, :], Vtok[:, tb, hcol[i]], start=True, stop=True)
                last.then_inc(turned, 1)

            @block.vector
            def _(dve):
                link = linker(dve, chain)
                dve.wait_ge(product, 1)
                link(nc.vector.tensor_tensor(UT, bank8(0), m_dT, ALU.mult))
                link(nc.vector.tensor_tensor(OT, bank8(0), m_oT, ALU.mult))
                dve.sem_inc(masked, 1)
                dve.wait_ge(product, 2)
                link(nc.vector.tensor_tensor(UM, bank8(2), m_d, ALU.mult))
                dve.sem_inc(masked, 1)
                dve.wait_ge(product, 3)
                link(nc.vector.tensor_tensor(NT, bank8(4), m_ltT, ALU.mult))
                dve.sem_inc(masked, 1)
                link(nc.vector.tensor_tensor(WT, UT, ident8, ALU.add))
                dve.wait_ge(product, 5)
                link(nc.vector.tensor_tensor(MB[:, tb, :, :], bank8(6), m_leT, ALU.mult))
                link(nc.vector.tensor_tensor(MK[:, tb, :, :], bank8(0), m_leT, ALU.mult))

            @block.scalar
            def _(act):
                act.wait_ge(turned, 1)
                for hh in range(2):
                    nc.scalar.copy(X0[:, 4 * hh:4 * hh + 4, 0:64],
                                   C.PS[:, 2, :].rearrange("p (j c) -> p j c", c=P)[:, :, 64 * hh:64 * hh + 64])
                act.wait_ge(turned, 2)
                nc.scalar.copy(X0[:, :, 64:128], C.PS[:, 4, :].rearrange("p (i c) -> p i c", c=64))

        with stage(nc, f"rw_inv{tb}", "chain squared grown taken applied solved gturned") as (
                block, chain, squared, grown, taken, applied, solved, gturned):
            @block.tensor
            def _(pe):
                for n in range(3):
                    if n:
                        pe.wait_ge(taken, 2 * n)
                    each(0, UT, UM)
                    if n < 2:
                        each(2, UM, UT)
                    last = nc.tensor.transpose(C.PS[:, 7, 0:P], C.ident[:, :], C.ident[:, :])
                    last.then_inc(squared, 1)
                    pe.wait_ge(taken, 2 * n + 2)
                    if n:
                        pe.wait_ge(grown, n)
                    each(4, UM, WT).then_inc(applied, 1)
                pe.wait_ge(grown, 3)
                each(0, WT, X0).then_inc(applied, 1)
                pe.wait_ge(solved, 1)
                each(2, OT, Y).then_inc(applied, 1)
                pe.wait_ge(solved, 2)
                each(4, WT, Zs).then_inc(applied, 1)
                pe.wait_ge(solved, 3)
                gt = X0.rearrange("p h c -> p (h c)")
                for j in range(4):
                    last = nc.tensor.transpose(C.PS[:, 6, j * P:(j + 1) * P], gt[:, j * P:(j + 1) * P], C.ident[:, :])
                last.then_inc(gturned, 1)

            @block.scalar
            def _(act):
                for n in range(3):
                    act.wait_ge(squared, n + 1)
                    if n:
                        act.wait_ge(applied, n)
                    nc.scalar.copy(UM, bank8(0)).then_inc(taken, 1)
                    if n < 2:
                        nc.scalar.copy(UT, bank8(2)).then_inc(taken, 1)
                    else:
                        act.sem_inc(taken, 1)
                act.wait_ge(gturned, 1)
                nc.scalar.copy(GT[:, :, tc], C.PS[:, 6, :].rearrange("p (j c) -> p j c", c=P))

            @block.vector
            def _(dve):
                link = linker(dve, chain)
                for n in range(3):
                    dve.wait_ge(applied, n + 1)
                    link(nc.vector.tensor_tensor(WT, WT, bank8(4), ALU.add))
                    dve.sem_inc(grown, 1)
                dve.wait_ge(applied, 4)
                link(nc.vector.tensor_copy(Y, bank8(0)))
                dve.sem_inc(solved, 1)
                dve.wait_ge(applied, 5)
                link(nc.vector.tensor_copy(Zs, bank8(2)))
                dve.sem_inc(solved, 1)
                dve.wait_ge(applied, 6)
                g = X0.rearrange("p h c -> p (h c)")[:, 0:512].rearrange("p (j x c) -> p x j c", x=2, c=64)
                hh = Htok[:, tb, :].rearrange("p (j x c) -> p x j c", x=2, c=64)
                for x in range(2):
                    ys, ps = Y[:, 4 * x:4 * x + 4, :], bank8(4)[:, 4 * x:4 * x + 4, :]
                    link(nc.vector.tensor_tensor(g[:, x], ys[:, :, 0:64], ps[:, :, 0:64], ALU.add))
                    link(nc.vector.tensor_tensor(hh[:, x], ys[:, :, 64:128], ps[:, :, 64:128], ALU.add))
                dve.sem_inc(solved, 1)

    ST = B[0][:, 0:512].rearrange("p (j c) -> p j c", c=P)
    TMP = B[0][:, 512:1024].rearrange("p (j c) -> p j c", c=P)
    YT, YI = half(B[1], 0), half(B[1], 1)
    bd = C.ones64[:, :].unsqueeze(1).to_broadcast([P, 4, P])
    ps4 = lambda b, rw=slice(0, P): C.PS[rw, b, :].rearrange("p (j c) -> p j c", c=P)
    with stage(nc, "rw_seq", "chain state read sa update all_sa intra") as (block, chain, state, read, sa, update, all_sa, intra):
        @block.tensor
        def _(pe):
            for c in range(S // RC):
                tb, at = divmod(c * RC, P)
                rw = slice(at, at + RC)
                col = slice(c * RC, (c + 1) * RC)
                pe.wait_ge(state, c + 1)
                for j in range(4):
                    last = nc.tensor.matmul(ps4(0, rw)[:, j, :], GT[:, j, col], ST[:, j, :], start=True, stop=True)
                last.then_inc(read, 1)
                for j in range(4):
                    last = nc.tensor.matmul(C.PS[:, 2 + j // 2, (j % 2) * S + c * RC:(j % 2) * S + (c + 1) * RC],
                                            ST[:, j, :], Rt[:, j, col], start=True, stop=True)
                pe.wait_ge(sa, c + 1)
                for j in range(4):
                    jc = slice(j * P, (j + 1) * P)
                    nc.tensor.matmul(ps4(1)[:, j, :], Ktok[rw, tb, jc], Vtok[rw, tb, jc], start=True, stop=False)
                    last = nc.tensor.matmul(ps4(1)[:, j, :], Btok[rw, tb, jc], Htok[rw, tb, jc], start=False, stop=True)
                last.then_inc(update, 1)
            for tb in range(TT):
                for i in range(8):
                    o = C.PS[64 * (i // 4):64 * (i // 4) + 64, 4 + (i % 4) // 2, ((i % 4) % 2) * S + tb * P:((i % 4) % 2) * S + (tb + 1) * P]
                    hc = slice(P * (i % 4) + 64 * (i // 4), P * (i % 4) + 64 * (i // 4) + 64)
                    nc.tensor.matmul(o, Htok[:, tb, hc], MB[:, tb, i, :], start=True, stop=False)
                    last = nc.tensor.matmul(o, Vtok[:, tb, hc], MK[:, tb, i, :], start=False, stop=True)
            last.then_inc(intra, 1)

        @block.vector
        def _(dve):
            link = linker(dve, chain)
            link(nc.vector.memset(ST, 0.0))
            dve.sem_inc(state, 1)
            for c in range(S // RC):
                tb, at = divmod(c * RC, P)
                rw = slice(at, at + RC)
                dve.wait_ge(read, c + 1)
                link(nc.vector.tensor_tensor(Htok[rw, tb, :], Htok[rw, tb, :], C.PS[rw, 0, :], ALU.add))
                dve.sem_inc(sa, 1)
                dve.wait_ge(update, c + 1)
                link(nc.vector.tensor_tensor(TMP, ps4(1), bd, ALU.mult))
                link(nc.vector.tensor_tensor(TMP, TMP, ST, ALU.add))
                link(nc.vector.tensor_tensor(ST, TMP, PC[:, :, c:c + 1].to_broadcast([P, 4, P]), ALU.mult))
                dve.sem_inc(state, 1)
            dve.wait_ge(intra, 1)
            t4 = lambda b: C.PS[:, b:b + 2, :].rearrange("p b (h t) -> p (b h) t", t=S)
            link(nc.vector.tensor_copy(YT, t4(4)))
            link(nc.vector.tensor_tensor(YT, YT, t4(2), ALU.add))

    def post(link):
        link(nc.vector.tensor_tensor(YI, YI, RN, ALU.mult))
        for j in range(4):
            link(nc.vector.tensor_scalar(YI[:, j, :], YI[:, j, :], C.v("rw_gn_g_2", j), C.v("rw_gn_b_2", j), ALU.mult, ALU.add))
        link(nc.vector.tensor_tensor(YI, YI, BON, ALU.add))
        link(nc.vector.tensor_tensor(MIX[:, 0:4, :], YI, G, ALU.mult))
    norm(C, "rw_gn", YT, 4, 1, C.ones64[:, :], 64, GN_EPS, B[7][:, 0:1024], RN, post, center=YI)
    T = tiles3(B[0])
    project(C, "ab_out", cm_tiles(C, 0, MIX) + cm_tiles(C, 1, MIX), 2, add_alpha(C, T), on="dve")
    return T



def weight_plan(t):
    plan = []
    for l in range(2):
        plan += w_units(t["w_ada"][l])
        if l == 0:
            plan += w_units(t["a_w_in"][:, 0:3072]) + w_units(t["a_w_out"])
        else:
            plan += w_units(t["b_w_in"]) + w_units(t["b_w_out"])
        gu = t["moe_w_gu"][l].rearrange("e (k p) n -> e p k n", p=P)
        dn = t["moe_w_down"][l].rearrange("e (k p) n -> e p k n", p=P)
        for e in range(0, 16, 2):
            plan += [w for x in (gu[:, :, :, 0:512], gu[:, :, :, 512:1024], dn) for w in (x[e], x[e + 1])]
    for l in range(2):
        if l == 0:
            plan += w_units(t["ab_w_in_2"], [512, 512, 512, 256, 512, 512]) + w_units(t["ab_w_out_2"])
        else:
            w = t["mla_w_in_2"]
            plan += w_units(w[:, 0:512]) + [w.rearrange("(k p) n -> p k n", p=P)[:, :, 448:544]]
            plan += w_units(t["mla_wq_b_2"]) + w_units(t["mla_wkv_b_2"]) + w_units(t["mla_w_out_2"])
        plan += w_units(t["xa_wq_2"][l]) + w_units(t["xa_wkv_2"][l]) + w_units(t["xa_wo_2"][l])
        v = [t[n][l].rearrange("e (k p) n -> e p k n", p=P) for n in ("moe_w_gate_2", "moe_w_up_2", "moe_w_down_2")]
        for e in range(0, 32, 2):
            plan += [w for x in v for w in (x[e], x[e + 1])]
    return plan


def two_blocks(nc, t, cnames, out):
    with ExitStack() as ctx:
        C = Chip(nc, t, ctx, cnames)
        C.plan = weight_plan(t)
        with stage(nc, "start", "landed") as (block, landed):
            @block.sync
            def _(sp):
                small = [(C.vec[:, :], t["vec"]), (C.ident[:, :], C.const("ident")), (C.ones[:, :], C.const("ones")),
                         (C.ones64[:, :], C.const("ones64")), (C.X[:, :, :], t["x_T"])]
                for dst, src in small:
                    sp.dma_start(dst, src).then_inc(landed, 16)
                for v in range(RING):
                    C.load(sp, v)
                sp.wait_ge(landed, 16 * len(small))
        for l in range(2):
            ada(C, f"ada{l}", l)
            modulated_norm(C, f"n1_{l}", C.v("norm1", 8 * l, 8), C.mod[:, 0:8], C.mod[:, 8:16])
            (mlstm, diff_attention)[l](C)
            modulated_norm(C, f"n2_{l}", C.v("norm2", 8 * l, 8), C.mod[:, 24:32], C.mod[:, 32:40])
            moe1(C, f"moe1_{l}", l)
        for l in range(2):
            ln = lambda n, src: layer_norm(C, f"ln{n}_{l}", src, C.v(f"ln{n}_g_2", 8 * l, 8), C.v(f"ln{n}_b_2", 8 * l, 8))
            ln(1, (mixer_ab, mla)[l](C))
            ln(2, cross_attention(C, f"xa{l}"))
            ln(3, moe2(C, f"moe2_{l}", l))
        assert C.used == len(C.plan)
        with stage(nc, "end", "stored") as (block, stored):
            @block.sync
            def _(sp):
                sp.dma_start(out, C.X[:, :, :]).then_inc(stored, 16)
                sp.wait_ge(stored, 16)



def column(a):
    return np.ascontiguousarray(np.asarray(a, np.float32).reshape(-1, P).T)


def lay_out(x):
    parts = []
    for n, w in VECTORS:
        if n == "b_if":
            a = np.zeros((P, 2), np.float32)
            a[0:4] = np.asarray(x["a_b_if"]).reshape(2, 4).T
        elif n in ("b_q_norm", "b_k_norm"):
            a = column(np.tile(np.asarray(x[n]).reshape(-1), 2))
        else:
            a = column(x[n])
        assert a.shape == (P, w), (n, a.shape)
        parts.append(a)
    arrays = {"vec": np.concatenate(parts, axis=1)}
    rows = []
    for n, w in ROWS:
        if n == "lam":
            a = np.concatenate([np.asarray(x["b_lam_" + s]).reshape(-1) for s in ("q1", "k1", "q2", "k2")])
        else:
            a = np.asarray(x[n]).reshape(-1)
        assert a.shape == (w,), n
        rows.append(a)
    arrays["rows"] = np.concatenate(rows)[None, :]
    by_channel = lambda a: np.ascontiguousarray(np.asarray(a).reshape(S, KT, P).transpose(2, 1, 0))
    arrays["x_T"] = by_channel(x["x"])
    arrays["mem_T"] = by_channel(x["mem_2"])
    arrays["positions"] = np.asarray(x["positions"]).reshape(1, S)
    arrays["sg_ws_T"] = np.ascontiguousarray(np.asarray(x["sg_ws_2"])[0].transpose(2, 0, 1))
    for n in ("w_ada", "a_w_in", "a_w_out", "b_w_in", "b_w_out", "w_router", "moe_w_gu", "moe_w_down", "ab_w_in_2",
              "rw_w2_2", "rw_a2_2", "rw_g2_2", "ab_w_out_2", "mla_w_in_2", "mla_wq_b_2", "mla_wkv_b_2", "mla_w_out_2",
              "xa_wq_2", "xa_wkv_2", "xa_wo_2", "moe_w_group_2", "moe_w_expert_2", "moe_w_gate_2", "moe_w_up_2",
              "moe_w_down_2"):
        a = np.asarray(x[n])
        arrays[n] = a.reshape(a.shape[1:]) if a.shape[0] == 1 else a
    return arrays


def prepare(nc, x):
    arrays = lay_out(x)
    cnames, consts = shape_constants()
    arrays["consts"] = consts
    t = {n: nc.dram_tensor(f"in_{n}", a.shape, mybir.dt.from_np(a.dtype), kind="ExternalInput").ap() for n, a in arrays.items()}
    return {f"in_{n}": a for n, a in arrays.items()}, t, cnames


def kernel(**inputs):
    import concourse.bacc as bacc
    from concourse.bass_utils import run_bass_kernel_spmd

    nc = bacc.Bacc("TRN2", target_bir_lowering=False, num_devices=1)
    arrays, t, cnames = prepare(nc, inputs)
    out = nc.dram_tensor("out_T", (P, KT, S), F32, kind="ExternalOutput").ap()
    two_blocks(nc, t, cnames, out)
    result = run_bass_kernel_spmd(nc, [arrays], core_ids=[0])
    y = result.results[0]["out_T"]
    return np.ascontiguousarray(y.transpose(2, 1, 0)).reshape(1, S, D)
```

```python
from contextlib import ExitStack, contextmanager
import math

import numpy as np

import concourse.bass as bass
from concourse import mybir

F32 = mybir.dt.float32
I32 = mybir.dt.int32
ALU = mybir.AluOpType
ACT = mybir.ActivationFunctionType
AX_X = mybir.AxisListType.X

P = 128
D = 1024
KT = D // P
S = 256
TT = S // P
RING = 6
SLOT = 4096
BUF = 2048
NBUF = 10
BANK = 512
STAGE_SEM0 = 200

EPS = 1e-6
LN_EPS = 1e-5
GN_EPS = 64e-5
ALPHA = 4 ** 0.25
LAM_INIT = 0.8 - 0.6 * math.exp(-0.3 * 1)
NEG = -1e30
RC = 32
EPS_COL, LN_EPS_COL, GN_EPS_COL, ONE_COL, WARM_COL = 26, 27, 28, 29, 30
CAP = 64
MAXLEFT = 2 * S // CAP



def shape_constants():
    p = np.arange(P)
    c = {}
    c["ident"] = np.eye(P)
    c["ones"] = np.ones((P, P))
    c["ones64"] = (p[:, None] // 64 == p[None, :] // 64) * 1.0
    c["causal_add"] = np.where(p[:, None] >= p[None, :], 0.0, NEG)
    c["key_le"] = (p[:, None] <= p[None, :]) * 1.0
    c["key_lt"] = (p[:, None] < p[None, :]) * 1.0
    c["iota"] = np.broadcast_to(np.arange(S)[None, :], (P, S))
    same32 = p[:, None] // RC == p[None, :] // RC
    same16 = p[:, None] // 16 == p[None, :] // 16
    c["rw_d"] = (same16 & (p[:, None] > p[None, :])) * 1.0
    c["rw_dT"] = (same16 & (p[:, None] < p[None, :])) * 1.0
    c["rw_oT"] = (same32 & ~same16 & (p[:, None] < p[None, :])) * 1.0
    c["rw_ltT"] = (same32 & (p[:, None] < p[None, :])) * 1.0
    c["rw_leT"] = (same32 & (p[:, None] <= p[None, :])) * 1.0
    rot = np.zeros((P, P))
    for b in (0, 64):
        for i in range(8):
            rot[b + i + 8, b + i] = -1.0
            rot[b + i, b + i + 8] = 1.0
    c["rot_b"] = rot
    rot = np.zeros((P, P))
    for i in range(16):
        rot[64 + i + 16, 64 + i] = -1.0
        rot[64 + i, 64 + i + 16] = 1.0
    c["rot_m"] = rot
    sel = np.zeros((P, 4 * P))
    for h in range(4):
        sel[h, h * P:(h + 1) * P] = 1.0
    c["sel"] = sel
    inv = (np.float32(500000.0) ** (-np.arange(0, 16, 2, dtype=np.float32) / np.float32(16))).astype(np.float32)
    f = np.zeros(P, np.float32)
    for b in (0, 64):
        f[b:b + 8] = inv
        f[b + 8:b + 16] = inv
    c["inv_b"] = np.ascontiguousarray(np.broadcast_to(f[:, None], (P, 2)))
    inv = (np.float32(10000.0) ** (-np.arange(16, dtype=np.float32) / np.float32(16))).astype(np.float32)
    f = np.zeros(P, np.float32)
    f[64:80] = inv
    f[80:96] = inv
    ang = (np.arange(S, dtype=np.float32)[None, :] * f[:, None]).astype(np.float32)
    c["cos_m"] = np.cos(ang)
    c["sin_m"] = np.sin(ang)
    names, at, parts = {}, 0, []
    for k, v in c.items():
        names[k] = (at, v.shape[1])
        at += v.shape[1]
        parts.append(np.asarray(v, np.float32))
    return names, np.ascontiguousarray(np.concatenate(parts, axis=1))


VECTORS = [
    ("c", 8), ("norm1", 16), ("norm2", 16), ("b_ada", 96), ("a_h_norm", 8),
    ("b_q_norm", 1), ("b_k_norm", 1), ("b_o_norm", 1),
    ("ab_mu_2", 14), ("rw_w0_2", 4), ("rw_a0_2", 4), ("rw_k_k_2", 4), ("rw_k_a_2", 4),
    ("rw_r_k_2", 4), ("rw_gn_g_2", 4), ("rw_gn_b_2", 4),
    ("mla_q_norm_2", 2), ("mla_kv_norm_2", 2),
    ("ln1_g_2", 16), ("ln1_b_2", 16), ("ln2_g_2", 16), ("ln2_b_2", 16), ("ln3_g_2", 16), ("ln3_b_2", 16),
    ("b_if", 2),
]
VCOL = {}
_at = 0
for _n, _w in VECTORS:
    VCOL[_n] = (_at, _w)
    _at += _w
NVEC = _at

ROWS = [
    ("router_bias", 16), ("moe_b_group_2", 8), ("moe_b_expert_2", 64),
    ("lam", 256), ("sg_ln_g_2", 512), ("sg_ln_b_2", 512), ("sg_b_2", 512),
]
RCOL = {}
_at = 0
for _n, _w in ROWS:
    RCOL[_n] = (_at, _w)
    _at += _w
NROW = _at


@contextmanager
def stage(nc, tag, names):
    names = names.split()
    with ExitStack() as held:
        sems = [held.enter_context(nc.semaphore(f"{tag}_{n}", num=STAGE_SEM0 + i)) for i, n in enumerate(names)]
        with nc.Block() as block:
            yield (block, *sems)
        nc.all_engine_barrier(sems_to_clear=range(STAGE_SEM0, STAGE_SEM0 + len(names)))


def linker(eng, sem):
    count = [0]

    def link(ins):
        count[0] += 1
        ins.then_inc(sem, 1)
        eng.wait_ge(sem, count[0])
    return link


def marker(eng, sem):
    count = [0]

    def mark(ins):
        count[0] += 1
        ins.then_inc(sem, 1)
        return count[0]

    def need(mark_no):
        eng.wait_ge(sem, mark_no)
    return mark, need


def warm(C, func):
    return C.nc.scalar.activation(C.small[:, WARM_COL:WARM_COL + 1], C.small[:, ONE_COL:ONE_COL + 1], func)


class Chip:

    def __init__(self, nc, t, ctx, cnames):
        self.nc, self.t = nc, t

        def sb(name, shape, dt=F32):
            return ctx.enter_context(nc.sbuf_tensor(name, shape, dt))

        self.ring = sb("ring", [P, RING, SLOT])
        self.X = sb("X", [P, KT, S])
        self.H = sb("H", [P, KT, S])
        self.big = sb("scratch", [P, NBUF * BUF])
        self.B = [self.big[:, i * BUF:(i + 1) * BUF] for i in range(NBUF)]
        self.PS = ctx.enter_context(nc.psum_tensor("PS", [P, 8, BANK], F32))
        self.vec = sb("vec", [P, NVEC])
        self.mod = sb("mod", [P, 96])
        self.small = sb("small", [P, 64])
        self.route = sb("route", [P, 136 + S])
        self.left = sb("left", [1, 20], I32)
        self.act_rows = sb("act_rows", [P, 512])
        self.ada_win = sb("ada_windows", [P, KT, 63])
        self.ada_ones = sb("ada_ones", [P, 63])
        self.ident = sb("ident", [P, P])
        self.ones = sb("ones", [P, P])
        self.ones64 = sb("ones64", [P, P])
        self.consts = t["consts"]
        self.cnames = cnames
        self.slot_loaded = [ctx.enter_context(nc.semaphore(f"slot_loaded{i}")) for i in range(RING)]
        self.slot_free = [ctx.enter_context(nc.semaphore(f"slot_free{i}")) for i in range(RING)]
        self.plan = []
        self.used = 0

    def v(self, name, j=0, w=1):
        at, _ = VCOL[name]
        return self.vec[:, at + j:at + j + w]

    def const(self, name):
        at, w = self.cnames[name]
        return self.consts[:, at:at + w]

    def row(self, name, j=0, w=None):
        at, ww = RCOL[name]
        w = ww if w is None else w
        return self.t["rows"][0:1, at + j:at + j + w].to_broadcast([P, w])

    def unit(self, u):
        _, a, b = self.plan[u].shape
        return self.ring[:, u % RING, 0:a * b].rearrange("p (a b) -> p a b", b=b)

    def loaded(self, eng, u):
        eng.wait_ge(self.slot_loaded[u % RING], 16 * (u // RING + 1))

    def freed(self, u):
        return self.slot_free[u % RING]

    def load(self, sp, v):
        if v >= len(self.plan):
            return
        if v >= RING:
            sp.wait_ge(self.slot_free[v % RING], v // RING)
        sp.dma_start(self.unit(v), self.plan[v]).then_inc(self.slot_loaded[v % RING], 16)

    def refill(self, sp, u0, n):
        for u in range(u0, u0 + n):
            self.load(sp, u + RING)


def w_units(w, widths=None):
    k, n = w.shape
    v = w.rearrange("(k p) n -> p k n", p=P)
    out, at = [], 0
    widths = widths or [min(SLOT // (k // P), n)] * (n // min(SLOT // (k // P), n))
    for b in widths:
        out.append(v[:, :, at:at + b])
        at += b
    assert at == n
    return out



def project(C, tag, tiles, units, evict, on="act", nb=4, loads=(), late={}, late_evict=None,
            vector=None, vector_end=None, scalar_at={}, tensor_at={}):
    nc = C.nc
    u0 = C.used
    last_of = {}
    for i, (u, _, _, _) in enumerate(tiles):
        if u is not None:
            last_of[u] = i
    with stage(nc, tag, "chain summed evicted late_evicted aside reply landed") as (
            block, chain, summed, evicted, late_evicted, aside, reply, landed):
        @block.sync
        def _(sp):
            for dst, src in loads:
                sp.dma_start(dst, src).then_inc(landed, 16)
            C.refill(sp, u0, units)
            if loads:
                sp.wait_ge(landed, 16 * len(loads))

        def gone(eng, i):
            if i in late:
                eng.wait_ge(late_evicted, sum(j in late for j in range(i + 1)))
            else:
                eng.wait_ge(evicted, sum(j not in late for j in range(i + 1)))

        @block.tensor
        def _(pe):
            seen = -1
            for i, (u, pairs, M, N) in enumerate(tiles):
                if i in tensor_at:
                    tensor_at[i](pe, aside, reply)
                if u is not None and u > seen:
                    C.loaded(pe, u0 + u)
                    seen = u
                if i >= nb:
                    gone(pe, i - nb)
                if late.get(i) is not None:
                    gone(pe, late[i]) if late[i] >= 0 else pe.wait_ge(aside, -late[i])
                for k, (lhsT, rhs) in enumerate(pairs):
                    last = nc.tensor.matmul(C.PS[0:M, i % nb, 0:N], lhsT, rhs,
                                            start=(k == 0), stop=(k == len(pairs) - 1))
                last.then_inc(summed, 1)

        def evictions(eng):
            for i, (u, _, M, N) in enumerate(tiles):
                if i in scalar_at:
                    scalar_at[i](eng, aside, evicted)
                if i in late:
                    continue
                eng.wait_ge(summed, i + 1)
                if u is not None and last_of[u] == i:
                    eng.sem_inc(C.freed(u0 + u), 1)
                evict(eng, i, C.PS[0:M, i % nb, 0:N]).then_inc(evicted, 1)

        if on == "act":
            @block.scalar
            def _(act):
                evictions(act)
        else:
            @block.vector
            def _(dve):
                evictions(dve)
        if late or vector:
            @block.vector
            def _(dve):
                link = linker(dve, chain)
                if vector:
                    vector(dve, link, evicted, aside, reply, landed)
                for i in sorted(late):
                    dve.wait_ge(summed, i + 1)
                    late_evict(link, i, C.PS[0:tiles[i][2], i % nb, 0:tiles[i][3]]).then_inc(late_evicted, 1)
                if vector_end:
                    vector_end(dve, link, evicted)
    C.used += units


def cm_tiles(C, u, x, cols=None, m=P, kt=KT, at=0):
    w = C.unit(C.used + u)
    cols = cols or w.shape[2] - at
    return [(u, [(w[:, k, at + j * m:at + (j + 1) * m], x[:, k, :]) for k in range(kt)], m, S)
            for j in range(cols // m)]


def tm_tiles(C, u, x, kt=KT, cols=slice(None)):
    w = C.unit(C.used + u)
    return [(u, [(x[:, k, tt * P:(tt + 1) * P], w[:, k, cols]) for k in range(kt)], P, w[:, 0, cols].free_size())
            for tt in range(TT)]



def norm(C, tag, src, groups, per, mat, n, eps, sq, out, post=None, affine=None, center=None, floor=None,
         setup=None, loads=(), before=None):
    nc = C.nc
    v = lambda x: x if len(x.shape) == 3 else x.rearrange("p (j t) -> p j t", t=S)
    src, sq = v(src), v(sq)
    x = src if center is None else v(center)
    gb = min(2, groups)
    banks = groups // gb
    by_root = floor is not None
    step = 2
    steps = per * gb // step
    with stage(nc, tag, "chain made mean_sum centered squared square_sum logged root scaled landed") as (
            block, chain, made, mean_sum, centered, squared, square_sum, logged, root, scaled, landed):
        view = lambda b0: C.PS[:, b0:b0 + banks, :].rearrange("p b (h t) -> p (b h) t", t=S)
        sums, means = view(0), view(4)

        if loads:
            @block.sync
            def _(sp):
                for dst, s in loads:
                    sp.dma_start(dst, s).then_inc(landed, 16)
                sp.wait_ge(landed, 16 * len(loads))

        @block.vector
        def _(dve):
            link = linker(dve, chain)
            if before is not None:
                for j in range(groups * per):
                    before(j).then_inc(made, 1)
                dve.wait_ge(made, groups * per)
            if setup is not None:
                setup(link)
            if center is not None:
                for b in range(banks):
                    dve.wait_ge(mean_sum, b + 1)
                    for i in range(steps):
                        j = b * gb * per + i * step
                        g = j // per
                        m = means[:, g:g + 2, :] if per == 1 else means[:, g:g + 1, :].to_broadcast([P, step, S])
                        nc.vector.scalar_tensor_tensor(x[:, j:j + step, :], m, -1.0 / n, src[:, j:j + step, :],
                                                       ALU.mult, ALU.add).then_inc(centered, 1)
                dve.wait_ge(centered, banks * steps)
            for b in range(banks):
                dve.wait_ge(root, b + 1)
                if by_root:
                    o = out[:, b * gb:b * gb + gb, :]
                    if floor is not None:
                        link(nc.vector.tensor_scalar(o, o, floor, None, ALU.max))
                    link(nc.vector.reciprocal(o, o))
                if affine is None:
                    post(link, b)
                    continue
                for k in range(per):
                    nc.vector.scalar_tensor_tensor(affine[0][:, k, :], x[:, k, :], affine[1][:, k:k + 1], out[:, 0, :],
                                                   ALU.mult, ALU.mult).then_inc(scaled, 1)

        @block.scalar
        def _(act):
            for b in range(banks):
                for i in range(steps):
                    j = b * gb * per + i * step
                    if center is not None:
                        act.wait_ge(centered, b * steps + i + 1)
                    elif before is not None:
                        act.wait_ge(made, j + step)
                    nc.scalar.activation(sq[:, j:j + step, :], x[:, j:j + step, :], ACT.Square).then_inc(squared, 1)
            warm(C, ACT.Sqrt if by_root else ACT.Ln)
            for b in range(banks):
                o, total = out[:, b * gb:b * gb + gb, :], sums[:, b * gb:b * gb + gb, :]
                act.wait_ge(square_sum, b + 1)
                bias = {} if eps is None else dict(bias=C.small[:, eps:eps + 1])
                nc.scalar.activation(o, total, ACT.Sqrt if by_root else ACT.Ln, scale=1.0 / n, **bias).then_inc(
                    root if by_root else logged, 1)
            if not by_root:
                for b in range(banks):
                    o = out[:, b * gb:b * gb + gb, :]
                    act.wait_ge(logged, b + 1)
                    nc.scalar.activation(o, o, ACT.Exp, scale=-0.5).then_inc(root, 1)
            if affine is not None:
                dst, _, bias = affine
                for k in range(per):
                    act.wait_ge(scaled, k + 1)
                    nc.scalar.activation(dst[:, k, :], dst[:, k, :], ACT.Identity, bias=bias[:, k:k + 1])

        @block.tensor
        def _(pe):
            if center is not None:
                for b in range(banks):
                    for g in range(b * gb, b * gb + gb):
                        for j in range(per):
                            if before is not None:
                                pe.wait_ge(made, g * per + j + 1)
                            last = nc.tensor.matmul(means[:, g, :], mat, src[:, g * per + j, :],
                                                    start=(j == 0), stop=(j == per - 1))
                    last.then_inc(mean_sum, 1)
            for b in range(banks):
                for g in range(b * gb, b * gb + gb):
                    for j in range(per):
                        tile = g * per + j
                        if tile % step == 0:
                            pe.wait_ge(squared, tile // step + 1)
                        last = nc.tensor.matmul(sums[:, g, :], mat, sq[:, tile, :],
                                                start=(j == 0), stop=(j == per - 1))
                last.then_inc(square_sum, 1)


def modulated_norm(C, tag, gain, shift, scale, loads=(), before=None):
    nc = C.nc
    a = C.small[:, 0:KT]
    r = C.B[1][:, 0:S]

    def setup(link):
        link(nc.vector.tensor_scalar(a, scale, 1.0, None, ALU.add))
        link(nc.vector.tensor_tensor(a, a, gain, ALU.mult))
    norm(C, tag, C.X[:, :, :], 1, KT, C.ones[:, :], D, EPS_COL, C.B[0], r.unsqueeze(1),
         affine=(C.H[:, :, :], a, shift), setup=setup, loads=loads, before=before)


def layer_norm(C, tag, src, g, b, loads=(), before=None):
    norm(C, tag, src, 1, KT, C.ones[:, :], D, LN_EPS_COL, C.B[1], C.B[3][:, 0:S].unsqueeze(1),
         affine=(C.X[:, :, :], g, b), center=C.B[2], loads=loads, before=before)



ADA_BANK = 7


def ada_start(C):
    nc = C.nc
    with stage(nc, "ada_start", "silu cleared") as (block, silu, cleared):
        @block.scalar
        def _(act):
            nc.scalar.activation(C.small[:, 8:16], C.v("c", 0, 8), ACT.Silu).then_inc(silu, 1)

        @block.vector
        def _(dve):
            nc.vector.memset(C.ada_ones[:, :], 0.0).then_inc(cleared, 1)
            nc.vector.memset(C.ada_win[:, :, :], 0.0).then_inc(cleared, 1)
            dve.wait_ge(silu, 1)
            dve.wait_ge(cleared, 2)
            nc.vector.memset(C.ada_ones[:, 31:32], 1.0)
            nc.vector.tensor_copy(C.ada_win[:, :, 31:32], C.small[:, 8:16].unsqueeze(2))


def ada_unit(C, pe, at, u, last_u=23):
    C.loaded(pe, at)
    w = C.unit(at)
    for k in range(2):
        for g in range(4):
            last = C.nc.tensor.matmul(C.PS[32 * g:32 * g + 32, ADA_BANK, :], C.ada_win[:, 2 * g + k, 31 - u:63 - u],
                                      w[:, 2 * g + k, :], start=(k == 0 and (u == 0 or u == 12 and g > 0)), stop=(u == last_u and k == 1))
    last.then_inc(C.freed(at), 1)


def ada_fold(C, dve, link, at, acc):
    C.loaded(dve, at)
    w = C.unit(at)
    for k in range(KT):
        c = C.small[:, 8 + k:9 + k]
        last = C.nc.vector.tensor_scalar(acc, w[:, k, :], c, None, ALU.mult) if k == 0 else \
            C.nc.vector.scalar_tensor_tensor(acc, w[:, k, :], c, acc, ALU.mult, ALU.add)
        if k < KT - 1:
            link(last)
    return last


def ada_finish(C, tag, units=0, first=0, n=24):
    nc = C.nc
    u0 = C.used
    rows = C.B[8][:, 512:1024]
    with stage(nc, tag, "chain summed taken turned") as (block, chain, summed, taken, turned):
        if units:
            @block.sync
            def _(sp):
                C.refill(sp, u0, units)

        @block.scalar
        def _(act):
            act.wait_ge(summed, 1)
            nc.scalar.copy(rows, C.PS[:, ADA_BANK, :]).then_inc(taken, 1)

        @block.tensor
        def _(pe):
            for u in range(units):
                ada_unit(C, pe, u0 + u, first + u, first + units - 1)
            nc.tensor.transpose(C.PS[:, 0, 0:P], C.ident[:, :], C.ident[:, :]).then_inc(summed, 1)
            pe.wait_ge(taken, 1)
            for j in range(4):
                last = nc.tensor.transpose(C.PS[:, 1, j * P:(j + 1) * P], rows[:, j * P:(j + 1) * P], C.ident[:, :])
            last.then_inc(turned, 1)

        @block.vector
        def _(dve):
            link = linker(dve, chain)
            dve.wait_ge(turned, 1)
            got = C.PS[:, 1, :].rearrange("p (j g u) -> p u j g", g=4, u=32)[:, first:first + n]
            m = C.mod[:, 4 * first:4 * (first + n)]
            link(nc.vector.tensor_reduce(m.rearrange("p (u j) -> p u j", j=4), got, AX_X, ALU.add))
            nc.vector.tensor_tensor(m, m, C.v("b_ada", 4 * first, 4 * n), ALU.add)
    C.used += units


def add_residual(C, gate):
    def evict(dve, i, ps):
        return C.nc.vector.scalar_tensor_tensor(C.X[:, i, :], ps, gate[:, i:i + 1], C.X[:, i, :], ALU.mult, ALU.add)
    return evict


def add_alpha(C, dst):
    def evict(dve, i, ps):
        return C.nc.vector.scalar_tensor_tensor(dst[:, i, :], C.X[:, i, :], ALPHA, ps, ALU.mult, ALU.add)
    return evict



def attention(C, tag, items, scale, causal, maps, scores, values, combine, buf, mask):
    nc = C.nc
    dest, lam = combine
    n = len(items)
    W = maps * 2 * P
    E = [buf[:, i * W:(i + 1) * W].rearrange("p (m k) -> p m k", m=maps) for i in range(4)]
    at = 4 * W
    PT = [buf[:, at + i * 2 * P:at + (i + 1) * 2 * P].rearrange("p (b q) -> p b q", b=2) for i in range(2)]
    at += 4 * P
    mx = [buf[:, at + 2 * i:at + 2 * i + maps] for i in range(4)]
    sm = [buf[:, at + 8 + 2 * i:at + 8 + 2 * i + maps] for i in range(4)]
    nks = [(qb + 1 if causal else TT) for _, qb in items]
    first = ((0, 1, 6, 7), (0, 6))[maps - 1]
    ahead = len(first)
    bank = lambda i, w0, w1: C.PS[:, first[i % ahead]:first[i % ahead] + maps, w0:w1]
    with stage(nc, tag, "chain scored limit expd probs transposed probs_T pv_done out") as (
            block, chain, scored, limit, expd, probs, transposed, probs_T, pv_done, out):

        @block.tensor
        def _(pe):
            for i in range(n + 4):
                if i < n:
                    h, qb = items[i]
                    if i >= ahead:
                        pe.wait_ge(expd, i - ahead + 1)
                    for m in range(maps):
                        pairs = scores(h, m, qb, nks[i])
                        for k, (lhsT, rhs) in enumerate(pairs):
                            last = nc.tensor.matmul(C.PS[:, first[i % ahead] + m, 0:nks[i] * P], lhsT, rhs,
                                                    start=(k == 0), stop=(k == len(pairs) - 1))
                    last.then_inc(scored, 1)
                if 3 <= i < n + 3:
                    j = i - 3
                    pe.wait_ge(probs, j + 1)
                    if j >= 2:
                        pe.wait_ge(probs_T, j - 1)
                    for b in range(nks[j]):
                        last = nc.tensor.transpose(C.PS[:, 2 + j % 2, b * P:(b + 1) * P],
                                                   E[j % 4][:, 0, b * P:(b + 1) * P], C.ident[:, :])
                    last.then_inc(transposed, 1)
                if i >= 4:
                    j = i - 4
                    h, qb = items[j]
                    pe.wait_ge(probs_T, j + 1)
                    if j >= 2:
                        pe.wait_ge(out, j - 1)
                    for x in range(len(values(h, 0))):
                        for b in range(nks[j]):
                            vv, M, col = values(h, b)[x]
                            last = nc.tensor.matmul(C.PS[0:M, 4 + j % 2, col * P:(col + 1) * P], vv,
                                                    PT[j % 2][:, b, :], start=(b == 0), stop=(b == nks[j] - 1))
                    last.then_inc(pv_done, 1)

        @block.vector
        def _(dve):
            mark, need = marker(dve, chain)
            for i in range(n + 2):
                j = i - 2
                if i < n:
                    nk = nks[i]
                    dve.wait_ge(scored, i + 1)
                    if causal:
                        diag = bank(i, (nk - 1) * P, nk * P)
                        masked = mark(nc.vector.tensor_tensor(diag, diag, mask.unsqueeze(1).to_broadcast([P, maps, P]), ALU.add))
                if j >= 0:
                    e, s = E[j % 4], sm[j % 4]
                    w = nks[j] * P
                    dve.wait_ge(expd, j + 1)
                    inverse = mark(nc.vector.reciprocal(s, s))
                if i < n:
                    if causal:
                        need(masked)
                    if i >= 4:
                        dve.wait_ge(expd, i - 3)
                    top = mark(nc.vector.tensor_reduce(mx[i % 4], bank(i, 0, nk * P), AX_X, ALU.max))
                if j >= 0:
                    need(inverse)
                    if maps == 2:
                        second = mark(nc.vector.tensor_scalar(e[:, 1, 0:w], e[:, 1, 0:w], s[:, 1:2], lam, ALU.mult, ALU.mult))
                    else:
                        nc.vector.tensor_scalar(e[:, 0, 0:w], e[:, 0, 0:w], s[:, 0:1], None, ALU.mult).then_inc(probs, 1)
                if i < n:
                    need(top)
                    nc.vector.tensor_scalar(mx[i % 4], mx[i % 4], -scale, None, ALU.mult).then_inc(limit, 1)
                if j >= 0 and maps == 2:
                    need(second)
                    nc.vector.scalar_tensor_tensor(e[:, 0, 0:w], e[:, 0, 0:w], s[:, 0:1], e[:, 1, 0:w],
                                                   ALU.mult, ALU.subtract).then_inc(probs, 1)

        @block.scalar
        def _(act):
            warm(C, ACT.Exp)
            for i in range(n + 4):
                if 3 <= i < n + 3:
                    j = i - 3
                    act.wait_ge(transposed, j + 1)
                    if j >= 2:
                        act.wait_ge(pv_done, j - 1)
                    nc.scalar.copy(PT[j % 2][:, 0:nks[j], :],
                                   C.PS[:, 2 + j % 2, 0:nks[j] * P].rearrange("p (b q) -> p b q", q=P)).then_inc(probs_T, 1)
                if i >= 4:
                    j = i - 4
                    h, qb = items[j]
                    act.wait_ge(pv_done, j + 1)
                    _, M, _ = values(h, 0)[0]
                    parts = len(values(h, 0))
                    nc.scalar.copy(dest(h, qb), C.PS[0:M, 4 + j % 2, 0:parts * P].rearrange(
                        "p (b q) -> p b q", b=parts)).then_inc(out, 1)
                if i < n:
                    act.wait_ge(limit, i + 1)
                    if i >= 4:
                        act.wait_ge(transposed, i - 3)
                    for m in range(maps):
                        last = nc.scalar.activation(E[i % 4][:, m, 0:nks[i] * P], C.PS[:, first[i % ahead] + m, 0:nks[i] * P],
                                                    ACT.Exp, bias=mx[i % 4][:, m:m + 1], scale=scale,
                                                    accum_out=sm[i % 4][:, m:m + 1])
                    last.then_inc(expd, 1)


def tiles3(x, j0=0, n=KT):
    return x[:, j0 * S:(j0 + n) * S].rearrange("p (j t) -> p j t", t=S)



def mlstm_loads(C):
    t, misc = C.t, C.B[4]
    return [(misc[:, 0:64].rearrange("p (k n) -> p k n", n=8),
             t["a_w_in"].rearrange("(k p) n -> p k n", p=P)[:, :, 3072:3080]),
            (misc[0:4, 64:64 + 512].rearrange("p (h m) -> p h m", h=4),
             C.const("sel")[0:4, :].rearrange("p (h m) -> p h m", h=4)),
            (misc[:, 576:704], C.const("key_le"))]


ML_UNITS = "wawawaawaawawa"


def mlstm(C):
    nc = C.nc
    Q, K_ = tiles3(C.B[0], 0, 4), tiles3(C.B[0], 4, 4)
    V = C.B[1].rearrange("p (t v) -> p t v", t=TT)
    O = tiles3(C.B[2])
    NUM = tiles3(C.B[3])
    misc = C.B[4]
    wg = misc[:, 0:64].rearrange("p (k n) -> p k n", n=8)
    sel = misc[0:4, 64:64 + 512].rearrange("p (h m) -> p h m", h=4)
    key_le = misc[:, 576:704]
    B5 = C.B[5]
    gi, gf, tmp, ones4 = (B5[0:4, i * S:(i + 1) * S] for i in range(4))
    u, negm, emt, bc = (B5[0:4, (4 + i) * S:(5 + i) * S] for i in range(4))
    ucol = misc[:, 704:712]
    at = [i for i, x in enumerate(ML_UNITS) if x == "w"]
    tiles = cm_tiles(C, at[0], C.H) + cm_tiles(C, at[1], C.H) + tm_tiles(C, at[2], C.H) + tm_tiles(C, at[3], C.H) \
        + cm_tiles(C, at[4], C.H) + cm_tiles(C, at[5], C.H) \
        + [(None, [(wg[:, k, 4 * g:4 * g + 4], C.H[:, k, :]) for k in range(KT)], 4, S) for g in range(2)]

    def evict(act, i, ps):
        if i < 4:
            return nc.scalar.copy(Q[:, i, :], ps)
        if i < 8:
            return nc.scalar.mul(K_[:, i - 4, :], ps, 128 ** -0.5)
        if i < 12:
            a, tt = divmod(i - 8, 2)
            return nc.scalar.copy(V[:, tt, a * 512:(a + 1) * 512], ps)
        if i < 20:
            return nc.scalar.activation(O[:, i - 12, :], ps, ACT.Sigmoid)
        return nc.scalar.activation((gi, gf)[i - 20], ps, ACT.Identity, bias=C.v("b_if", i - 20)[0:4, :])

    fold_at = [C.used + i for i, x in enumerate(ML_UNITS) if x == "a"]
    FOLD = [C.B[7][:, i * 512:(i + 1) * 512] for i in range(2)]

    def fold(dve, link, evicted, aside, reply, landed):
        for n, at in enumerate(fold_at):
            if n >= 2:
                dve.wait_ge(reply, n - 1)
            link(ada_fold(C, dve, link, at, FOLD[n % 2]))
            dve.sem_inc(C.freed(at), 1)
            dve.sem_inc(aside, 1)

    def add_up(n):
        def f(pe, aside, reply):
            u = 4 + n
            pe.wait_ge(aside, n + 1)
            nc.tensor.matmul(C.PS[0:32, ADA_BANK, :], C.ada_ones[:, 31 - u:63 - u], FOLD[n % 2],
                             start=(n == 0), stop=False).then_inc(reply, 1)
        return f
    project(C, "ml_in", tiles, len(ML_UNITS), evict, vector=fold,
            tensor_at={i: add_up(n) for n, i in enumerate((3, 5, 7, 9, 10, 11, 15, 18))})

    a0 = C.used
    with stage(nc, "ml_gate", "chain abs_z log1p u_ready u_T") as (block, chain, abs_z, log1p, u_ready, u_T):
        @block.vector
        def _(dve):
            link = linker(dve, chain)
            link(nc.vector.memset(ones4, 1.0))
            link(nc.vector.scalar_tensor_tensor(tmp, gf, -1.0, gf, ALU.mult, ALU.max))
            dve.sem_inc(abs_z, 1)
            dve.wait_ge(log1p, 2)
            link(nc.vector.scalar_tensor_tensor(tmp, gf, 0.0, tmp, ALU.min, ALU.subtract))
            link(nc.vector.tensor_tensor_scan(bc, ones4, tmp, 0.0, ALU.mult, ALU.add))
            link(nc.vector.tensor_tensor(u, gi, bc, ALU.subtract))
            dve.sem_inc(u_ready, 1)
            link(nc.vector.tensor_tensor_scan(negm, ones4, u, 0.0, ALU.mult, ALU.max))
            link(nc.vector.tensor_scalar(negm, negm, -1.0, None, ALU.mult))
            link(nc.vector.tensor_tensor(emt, negm, bc, ALU.subtract))
            dve.wait_ge(u_T, 1)
            link(nc.vector.tensor_copy(ucol, C.PS[:, 0, 0:8]))
            dve.sem_inc(u_ready, 1)

        @block.scalar
        def _(act):
            act.wait_ge(abs_z, 1)
            nc.scalar.activation(tmp, tmp, ACT.Exp, scale=-1.0).then_inc(log1p, 1)
            act.wait_ge(log1p, 1)
            nc.scalar.activation(tmp, tmp, ACT.Ln, bias=1.0).then_inc(log1p, 1)
            act.wait_ge(u_ready, 2)
            nc.scalar.activation(emt, emt, ACT.Exp)

        @block.sync
        def _(sp):
            C.refill(sp, a0, 2)

        @block.tensor
        def _(pe):
            for x in range(2):
                ada_unit(C, pe, a0 + x, 12 + x)
            pe.wait_ge(u_ready, 1)
            for tt in range(TT):
                last = nc.tensor.transpose(C.PS[:, 0, 4 * tt:4 * tt + 4], u[:, tt * P:(tt + 1) * P], C.ident[0:4, 0:4])
            last.then_inc(u_T, 1)

    Dm = [tiles3(C.B[6], 2 * i, 2) for i in range(2)]
    Wm = [tiles3(C.B[6], 4 + 2 * i, 2) for i in range(2)]
    r = C.B[7][:, 0:S]
    dn = C.B[7][:, S:2 * S]
    with stage(nc, "ml_mix", "chain bcast clamped expd scored weighted summed taken") as (
            block, chain, bcast, clamped, expd, scored, weighted, summed, taken):
        @block.sync
        def _(sp):
            C.refill(sp, a0 + 2, 10)

        @block.tensor
        def _(pe):
            def start(h):
                if h >= 2:
                    pe.wait_ge(taken, h - 1)
                nc.tensor.matmul(C.PS[:, h % 2, 0:S], sel[:, h, :], negm, start=True, stop=True)
                nc.tensor.matmul(C.PS[:, h % 2, S:2 * S], sel[:, h, :], emt, start=True, stop=True).then_inc(bcast, 1)
                for st in range(TT):
                    last = nc.tensor.matmul(C.PS[:, 2 + h % 2, st * S:(st + 1) * S], K_[:, h, st * P:(st + 1) * P],
                                            Q[:, h, :], start=True, stop=True)
                last.then_inc(scored, 1)
            start(0)
            for h in range(4):
                if h < 3:
                    start(h + 1)
                for x in range(2 + 5 * h // 2, 2 + 5 * (h + 1) // 2):
                    ada_unit(C, pe, a0 + x, 12 + x)
                pe.wait_ge(weighted, h + 1)
                if h:
                    pe.wait_ge(taken, h)
                w = Wm[h % 2]
                for st in range(TT):
                    nc.tensor.matmul(C.PS[:, 4, 0:S], C.ones[:, :], w[:, st, :], start=(st == 0), stop=(st == 1))
                for vt in range(2):
                    for st in range(TT):
                        last = nc.tensor.matmul(C.PS[:, 5 + vt, 0:S], V[:, st, h * 256 + vt * P:h * 256 + (vt + 1) * P],
                                                w[:, st, :], start=(st == 0), stop=(st == 1))
                last.then_inc(summed, 1)

        @block.vector
        def _(dve):
            link = linker(dve, chain)

            def clamp(h):
                dve.wait_ge(bcast, h + 1)
                for st in range(TT):
                    last = nc.vector.tensor_scalar(Dm[h % 2][:, st, :], C.PS[:, h % 2, 0:S],
                                                   ucol[:, 4 * st + h:4 * st + h + 1], 0.0, ALU.add, ALU.min)
                last.then_inc(clamped, 1)
            clamp(0)
            for h in range(4):
                d, w = Dm[h % 2], Wm[h % 2]
                dve.wait_ge(expd, h + 1)
                dve.wait_ge(scored, h + 1)
                for st in range(TT):
                    nc.vector.tensor_tensor(d[:, st, st * P:(st + 1) * P], d[:, st, st * P:(st + 1) * P], key_le, ALU.mult)
                link(nc.vector.memset(d[:, 1, 0:P], 0.0))
                nc.vector.tensor_tensor(w, C.PS[:, 2 + h % 2, :].rearrange("p (b t) -> p b t", t=S), d,
                                        ALU.mult).then_inc(weighted, 1)
                if h < 3:
                    clamp(h + 1)
                dve.wait_ge(summed, h + 1)
                link(nc.vector.tensor_copy(r, C.PS[:, 4, 0:S]))
                link(nc.vector.scalar_tensor_tensor(dn, r, -1.0, r, ALU.mult, ALU.max))
                link(nc.vector.tensor_tensor(dn, dn, C.PS[:, h % 2, S:2 * S], ALU.max))
                link(nc.vector.reciprocal(r, dn))
                link(nc.vector.tensor_tensor(NUM[:, 2 * h:2 * h + 2, :], C.PS[:, 5:7, 0:S],
                                             r.unsqueeze(1).to_broadcast([P, 2, S]), ALU.mult))
                dve.sem_inc(taken, 1)

        @block.scalar
        def _(act):
            for h in range(4):
                act.wait_ge(clamped, h + 1)
                nc.scalar.activation(Dm[h % 2], Dm[h % 2], ACT.Exp).then_inc(expd, 1)

    C.used += 12
    ada_finish(C, "ada_rest", first=4, n=20)

    R4 = tiles3(C.B[5], 0, 4)

    def post(link, b):
        for j in range(4 * b, 4 * b + 4):
            last = nc.vector.scalar_tensor_tensor(NUM[:, j, :], NUM[:, j, :], C.v("a_h_norm", j), R4[:, j // 2, :],
                                                  ALU.mult, ALU.mult)
        link(last)
        nc.vector.tensor_tensor(NUM[:, 4 * b:4 * b + 4, :], NUM[:, 4 * b:4 * b + 4, :], O[:, 4 * b:4 * b + 4, :], ALU.mult)
    norm(C, "ml_norm", NUM, 4, 2, C.ones[:, :], 256, EPS_COL, C.B[4], R4, post)
    tiles = cm_tiles(C, 0, NUM) + cm_tiles(C, 1, NUM)
    project(C, "ml_out", tiles, 2, add_residual(C, C.mod[:, 16:24]), on="dve")



def diff_attention_loads(C):
    m = C.B[9]
    return [(m[:, 0:P], C.const("rot_b")), (m[:, P:2 * P], C.const("causal_add")), (m[:, 256:258], C.const("inv_b")),
            (m[:, 1536:1792].bitcast(I32), C.t["positions"].to_broadcast([P, S])), (m[:, 1792:2048], C.row("lam"))]


def diff_attention(C):
    nc = C.nc
    Q, K_ = tiles3(C.B[0]), tiles3(C.B[1])
    V = C.B[2].rearrange("p (t v) -> p t v", t=TT)
    O = tiles3(C.B[3])
    m = C.B[9]
    rot, mask, inv = m[:, 0:P], m[:, P:2 * P], m[:, 256:257]
    cos, sin, ang, k = (m[:, 512 + i * S:512 + (i + 1) * S] for i in range(4))
    posi = m[:, 1536:1792].bitcast(I32)
    lamr = m[:, 1792:2048]
    lam = C.small[:, 16:24]
    tiles = sum([cm_tiles(C, u, C.H) for u in range(4)], []) + tm_tiles(C, 4, C.H) + tm_tiles(C, 5, C.H)

    def evict(act, i, ps):
        if i < 8:
            return nc.scalar.copy(Q[:, i, :], ps)
        if i < 16:
            return nc.scalar.copy(K_[:, i - 8, :], ps)
        a, tt = divmod(i - 16, 2)
        return nc.scalar.copy(V[:, tt, a * 512:(a + 1) * 512], ps)

    c1 = 6.28125
    c2 = float(np.float32(np.round((2 * math.pi - c1) * 2 ** 21) / 2 ** 21))
    c3 = float(np.float32(2 * math.pi - c1 - c2))
    half = float(np.nextafter(np.float32(math.pi), np.float32(0)))
    def tables(dve, link, aside):
        link(nc.vector.tensor_copy(ang, posi))
        link(nc.vector.tensor_scalar(ang, ang, inv, None, ALU.mult))
        link(nc.vector.tensor_scalar(k, ang, 1 / (2 * math.pi), 12582912.0, ALU.mult, ALU.add))
        link(nc.vector.tensor_scalar(k, k, 12582912.0, None, ALU.subtract))
        for c in (c1, c2, c3):
            link(nc.vector.scalar_tensor_tensor(ang, k, -c, ang, ALU.mult, ALU.add))
        link(nc.vector.tensor_scalar(ang, ang, half, -half, ALU.min, ALU.max))
        link(nc.vector.scalar_tensor_tensor(k, ang, -1.0, ang, ALU.mult, ALU.max))
        link(nc.vector.tensor_scalar(k, k, -1.0, math.pi / 2, ALU.mult, ALU.add))
        for i in range(2):
            a, b = lamr[:, 128 * i:128 * i + 64], lamr[:, 128 * i + 64:128 * i + 128]
            link(nc.vector.tensor_tensor(a, a, b, ALU.mult))
            link(nc.vector.tensor_reduce(lam[:, i:i + 1], a, AX_X, ALU.add))
        dve.sem_inc(aside, 1)
        dve.wait_ge(aside, 2)
        nc.vector.tensor_scalar(lam[:, 4:5], lam[:, 2:3], lam[:, 3:4], LAM_INIT, ALU.subtract, ALU.add)
        nc.vector.tensor_scalar(C.small[:, 24:25], C.v("b_o_norm"), 1.0 - LAM_INIT, None, ALU.mult)

    def sines(act, aside):
        act.wait_ge(aside, 1)
        nc.scalar.activation(sin, ang, ACT.Sin)
        nc.scalar.activation(cos, k, ACT.Sin)
        nc.scalar.activation(lam[:, 2:4], lam[:, 0:2], ACT.Exp).then_inc(aside, 1)

    R8 = tiles3(C.B[6])
    chunks = []
    for n, (X, gain) in enumerate(((Q, C.v("b_q_norm")), (K_, C.v("b_k_norm")))):
        SQ, RT = tiles3(C.B[4 + n]), tiles3(C.B[6 + n])
        chunks += [(X[:, j:j + 2, :], gain, SQ[:, j:j + 2, :], RT[:, j:j + 2, :]) for j in range(0, KT, 2)]
    two = lambda b: C.PS[:, b, :].rearrange("p (h t) -> p h t", t=S)
    wide = lambda x: x.unsqueeze(1).to_broadcast([P, 2, S])
    with ExitStack() as held:
        squared, square_sum, logged, root, normed, scaled, turned, roped = (
            held.enter_context(nc.semaphore(f"da_{n}")) for n in (
                "squared", "square_sum", "logged", "root", "normed", "scaled", "turned", "roped"))

        def square(c):
            nc.scalar.activation(chunks[c][2], chunks[c][0], ACT.Square).then_inc(squared, 1)

        def log(act, c):
            act.wait_ge(square_sum, c + 1)
            nc.scalar.activation(chunks[c][3], two(4 + c % 2), ACT.Ln, bias=C.small[:, EPS_COL:EPS_COL + 1],
                                 scale=1.0 / 64).then_inc(logged, 1)

        def inverse_roots(act, cs):
            for c in cs:
                act.wait_ge(logged, c + 1)
                nc.scalar.activation(chunks[c][3], chunks[c][3], ACT.Exp, scale=-0.5).then_inc(root, 1)

        def scalar_part(i):
            def f(act, aside, evicted):
                if i == 2:
                    sines(act, aside)
                if i % 2 == 0 and i <= 16:
                    act.wait_ge(evicted, i)
                    square(i // 2 - 1)
                if i % 2 and 3 <= i:
                    log(act, (i - 3) // 2)
                if i == 10:
                    inverse_roots(act, range(4))
                if i == 17:
                    inverse_roots(act, range(4, 8))
            return f

        def tensor_part(i):
            def f(pe, aside, reply):
                if i % 2 and 3 <= i <= 17:
                    c = (i - 3) // 2
                    pe.wait_ge(squared, c + 1)
                    if c >= 2:
                        pe.wait_ge(logged, c - 1)
                    nc.tensor.matmul(two(4 + c % 2), C.ones64[:, :], chunks[c][2], start=True, stop=True).then_inc(square_sum, 1)
                for c in {12: (0,), 13: (1,), 14: (2,), 15: (3,), 18: (4, 5), 19: (6, 7)}.get(i, ()):
                    pe.wait_ge(normed, c + 1)
                    if c >= 2:
                        pe.wait_ge(roped, c - 1)
                    nc.tensor.matmul(two(6 + c % 2), rot, chunks[c][0], start=True, stop=True).then_inc(turned, 1)
            return f

        def vector_part(dve, link, evicted, aside, reply, landed):
            tables(dve, link, aside)
            for cs in (range(4), range(4, 8)):
                for c in cs:
                    x, gain, _, r = chunks[c]
                    dve.wait_ge(root, c + 1)
                    nc.vector.scalar_tensor_tensor(x, x, gain, r, ALU.mult, ALU.mult).then_inc(normed, 1)
                    dve.wait_ge(normed, c + 1)
                    nc.vector.tensor_tensor(r, x, wide(cos), ALU.mult).then_inc(scaled, 1)
                for c in cs:
                    x, _, tmp, r = chunks[c]
                    dve.wait_ge(turned, c + 1)
                    link(nc.vector.tensor_tensor(tmp, two(6 + c % 2), wide(sin), ALU.mult))
                    dve.wait_ge(scaled, c + 1)
                    nc.vector.tensor_tensor(x, r, tmp, ALU.add).then_inc(roped, 1)
        project(C, "da_in", tiles, 6, evict, vector=vector_part, scalar_at={i: scalar_part(i) for i in range(2, 18)},
                tensor_at={i: tensor_part(i) for i in range(3, 20)})

    attention(C, "da_att", [(h, qb) for h in range(8) for qb in range(TT)], 64 ** -0.5, True, 2,
              lambda h, mm, qb, nk: [(Q[64 * mm:64 * mm + 64, h, qb * P:(qb + 1) * P], K_[64 * mm:64 * mm + 64, h, 0:nk * P])],
              lambda h, kb: [(V[:, kb, h * P:(h + 1) * P], P, 0)],
              (lambda h, qb: O[:, h:h + 1, qb * P:(qb + 1) * P], lam[:, 4:5]), C.big[:, 5 * BUF:7 * BUF], mask)

    def post(link, b):
        o = O[:, 2 * b:2 * b + 2, :]
        nc.vector.scalar_tensor_tensor(o, o, C.small[:, 24:25], R8[:, 2 * b:2 * b + 2, :], ALU.mult, ALU.mult)
    norm(C, "da_on", O, 8, 1, C.ones[:, :], P, EPS_COL, C.B[4], R8, post)
    project(C, "da_out", cm_tiles(C, 0, O) + cm_tiles(C, 1, O), 2, add_residual(C, C.mod[:, 64:72]), on="dve")



def mla_loads(C):
    m = C.B[9]
    return [(m[:, 0:P], C.const("rot_m")), (m[:, P:2 * P], C.const("causal_add")), (m[:, 256:512], C.const("cos_m")),
            (m[:, 512:768], C.const("sin_m"))]


def mla(C):
    nc = C.nc
    QS = [tiles3(C.B[0]), tiles3(C.B[1])]
    KS = [tiles3(C.B[2]), tiles3(C.B[3])]
    V = C.B[4].rearrange("p (t v) -> p t v", t=TT)
    CQ, CKV = tiles3(C.B[5], 0, 2), tiles3(C.B[5], 2, 2)
    kpe = C.B[5][:, 4 * S:5 * S]
    R = tiles3(C.B[5], 5, 2)
    O = tiles3(C.B[6])
    m = C.B[9]
    rot, mask = m[:, 0:P], m[:, P:2 * P]
    cos, sin = m[:, 256:512], m[:, 512:768]
    tiles = cm_tiles(C, 0, C.X) + cm_tiles(C, 1, C.X, m=96)

    def evict(act, i, ps):
        if i < 4:
            return nc.scalar.copy((CQ if i < 2 else CKV)[:, i % 2, :], ps)
        return nc.scalar.copy(kpe[0:96, :], ps)
    project(C, "mla_in", tiles, 2, evict)

    def post(link, b):
        for j in range(4):
            w = C.v("mla_q_norm_2" if j < 2 else "mla_kv_norm_2", j % 2)
            nc.vector.scalar_tensor_tensor(both[:, j, :], both[:, j, :], w, R[:, j // 2, :], ALU.mult, ALU.mult)
    both = tiles3(C.B[5], 0, 4)
    norm(C, "mla_n", both, 2, 2, C.ones[:, :], 256, EPS_COL, C.B[7], R, post)

    wkv = C.unit(C.used + 1)
    turn = [(None, [(rot[0:96, 0:96], kpe[0:96, :])], 96, S)] \
        + [(None, [(rot[0:96, 0:96], QS[j // 4][0:96, 2 * (j % 4):2 * (j % 4) + 2, :])], 96, 2 * S) for j in range(8)]
    tiles = cm_tiles(C, 0, CQ, m=96, kt=2)
    late = {}
    for h in range(16):
        tiles.append((1, [(wkv[:, k, h * P:h * P + 64], CKV[:, k, :]) for k in range(2)], 64, S))
        if h % 2:
            tiles.append(turn[1 + h // 2])
            late[len(tiles) - 1] = h
        elif h == 0:
            tiles.append(turn[0])
            late[len(tiles) - 1] = None
    for g in range(2):
        for tt in range(TT):
            tiles.append((1, [(CKV[:, k, tt * P:(tt + 1) * P],
                               wkv[:, k, g * 1024:(g + 1) * 1024].rearrange("p (h c) -> p h c", c=P)[:, :, 64:128])
                              for k in range(2)], P, 512))
    kind = [i for i in range(len(tiles)) if i not in late]

    def evict(act, i, ps):
        i = kind.index(i)
        if i < 16:
            return nc.scalar.copy(QS[i // 8][0:96, i % 8, :], ps)
        if i < 32:
            return nc.scalar.copy(KS[(i - 16) // 8][0:64, i % 8, :], ps)
        g, tt = divmod(i - 32, 2)
        return nc.scalar.copy(V[:, tt, g * 512:(g + 1) * 512], ps)
    r = slice(64, 96)
    T = tiles3(C.B[7])
    order = sorted(late)

    def late_evict(link, i, ps):
        j = order.index(i) - 1
        if j < 0:
            link(nc.vector.tensor_tensor(T[r, 0, :], ps[r, :], sin[r, :], ALU.mult))
            link(nc.vector.tensor_tensor(kpe[r, :], kpe[r, :], cos[r, :], ALU.mult))
            link(nc.vector.tensor_tensor(kpe[r, :], kpe[r, :], T[r, 0, :], ALU.add))
            for g in range(2):
                last = nc.vector.tensor_copy(KS[g][r, :, :], kpe[r, :].unsqueeze(1).to_broadcast([32, 8, S]))
            return last
        x = QS[j // 4][r, 2 * (j % 4):2 * (j % 4) + 2, :]
        tmp = T[r, 2 * (j % 4):2 * (j % 4) + 2, :]
        wide = lambda y: y[r, :].unsqueeze(1).to_broadcast([32, 2, S])
        link(nc.vector.tensor_tensor(tmp, ps[r, :].rearrange("p (h t) -> p h t", t=S), wide(sin), ALU.mult))
        link(nc.vector.tensor_tensor(x, x, wide(cos), ALU.mult))
        return nc.vector.tensor_tensor(x, x, tmp, ALU.add)
    project(C, "mla_qkv", tiles, 2, evict, nb=8, late=late, late_evict=late_evict)
    attention(C, "mla_att", [(h, qb) for h in range(16) for qb in range(TT)], 96 ** -0.5, True, 1,
              lambda h, mm, qb, nk: [(QS[h // 8][0:96, h % 8, qb * P:(qb + 1) * P], KS[h // 8][0:96, h % 8, 0:nk * P])],
              lambda h, kb: [(V[:, kb, h * 64:(h + 1) * 64], 64, 0)],
              (lambda h, qb: O[64 * (h % 2):64 * (h % 2) + 64, h // 2:h // 2 + 1, qb * P:(qb + 1) * P], None),
              C.big[:, 7 * BUF:9 * BUF], mask)
    T = tiles3(C.B[0])
    project(C, "mla_out", cm_tiles(C, 0, O) + cm_tiles(C, 1, O), 2, add_alpha(C, T), on="dve",
            loads=cross_attention_loads(C))
    return T



def cross_attention_loads(C):
    return [(tiles3(C.B[5]), C.t["mem_T"])]


def cross_attention(C, tag, src, gain, bias):
    nc = C.nc
    M = tiles3(C.B[5])
    Q, K_ = tiles3(C.B[1]), tiles3(C.B[2])
    V = C.B[3].rearrange("p (t v) -> p t v", t=TT)
    O = tiles3(C.B[4])
    tiles = cm_tiles(C, 0, M) + cm_tiles(C, 1, M) + tm_tiles(C, 2, M) + tm_tiles(C, 3, M)
    first_q = len(tiles)
    tiles += cm_tiles(C, 4, C.X) + cm_tiles(C, 5, C.X)

    def evict(act, i, ps):
        if i < 8:
            return nc.scalar.copy(K_[:, i, :], ps)
        if i >= first_q:
            return nc.scalar.copy(Q[:, i - first_q, :], ps)
        a, tt = divmod(i - 8, 2)
        return nc.scalar.copy(V[:, tt, a * 512:(a + 1) * 512], ps)

    cen, sq, r = tiles3(C.B[6]), tiles3(C.B[7]), C.B[8][:, 0:S]
    means, squares = C.PS[:, 4, 0:S], C.PS[:, 5, 0:S]
    with ExitStack() as held:
        mean_sum, centered, squared, square_sum, logged, root, scaled, normed = (
            held.enter_context(nc.semaphore(f"{tag}_ln_{n}")) for n in (
                "mean_sum", "centered", "squared", "square_sum", "logged", "root", "scaled", "normed"))

        def pe_means(pe, aside, reply):
            for j in range(KT):
                last = nc.tensor.matmul(means, C.ones[:, :], src[:, j, :], start=(j == 0), stop=(j == KT - 1))
            last.then_inc(mean_sum, 1)

        def pe_squares(pe, aside, reply):
            for j in range(KT):
                if j % 2 == 0:
                    pe.wait_ge(squared, j // 2 + 1)
                last = nc.tensor.matmul(squares, C.ones[:, :], sq[:, j, :], start=(j == 0), stop=(j == KT - 1))
            last.then_inc(square_sum, 1)

        def dve_norm(dve, link, evicted, aside, reply, landed):
            dve.wait_ge(mean_sum, 1)
            for j in range(0, KT, 2):
                nc.vector.scalar_tensor_tensor(cen[:, j:j + 2, :], means.unsqueeze(1).to_broadcast([P, 2, S]), -1.0 / D,
                                               src[:, j:j + 2, :], ALU.mult, ALU.add).then_inc(centered, 1)
            dve.wait_ge(centered, KT // 2)
            dve.wait_ge(root, 1)
            for j in range(KT):
                nc.vector.scalar_tensor_tensor(C.X[:, j, :], cen[:, j, :], gain[:, j:j + 1], r,
                                               ALU.mult, ALU.mult).then_inc(scaled, 1)

        def act_squares(act, aside, evicted):
            for j in range(0, KT, 2):
                act.wait_ge(centered, j // 2 + 1)
                nc.scalar.activation(sq[:, j:j + 2, :], cen[:, j:j + 2, :], ACT.Square).then_inc(squared, 1)

        def act_root(act, aside, evicted):
            act.wait_ge(square_sum, 1)
            nc.scalar.activation(r, squares, ACT.Ln, bias=C.small[:, LN_EPS_COL:LN_EPS_COL + 1], scale=1.0 / D).then_inc(logged, 1)
            act.wait_ge(logged, 1)
            nc.scalar.activation(r, r, ACT.Exp, scale=-0.5).then_inc(root, 1)

        def act_bias(act, aside, evicted):
            for j in range(KT):
                act.wait_ge(scaled, j + 1)
                nc.scalar.activation(C.X[:, j, :], C.X[:, j, :], ACT.Identity, bias=bias[:, j:j + 1]).then_inc(normed, 1)

        def pe_wait(pe, aside, reply):
            pe.wait_ge(normed, KT)
        project(C, tag + "in", tiles, 6, evict, vector=dve_norm,
                tensor_at={1: pe_means, 3: pe_squares, first_q: pe_wait},
                scalar_at={1: act_squares, 3: act_root, 5: act_bias})
    attention(C, tag + "att", [(h, qb) for h in range(4) for qb in range(TT)], 256 ** -0.5, False, 1,
              lambda h, mm, qb, nk: [(Q[:, 2 * h + k, qb * P:(qb + 1) * P], K_[:, 2 * h + k, :]) for k in range(2)],
              lambda h, kb: [(V[:, kb, h * 256 + x * P:h * 256 + (x + 1) * P], P, x) for x in range(2)],
              (lambda h, qb: O[:, 2 * h:2 * h + 2, qb * P:(qb + 1) * P], None), C.big[:, 5 * BUF:7 * BUF], None)
    T = tiles3(C.B[0])
    project(C, tag + "out", cm_tiles(C, 0, O) + cm_tiles(C, 1, O), 2, add_alpha(C, T), on="dve")
    return T



class Moe:

    def __init__(self, C, E):
        self.E, self.cap = E, CAP
        self.htok = C.B[6].rearrange("p (t d) -> p t d", t=TT)
        self.yacc = tiles3(C.B[7])
        b = C.big[:, 8 * BUF:10 * BUF]
        self.xg = b[:, 0:1024].rearrange("p (k c) -> p k c", k=KT)
        self.yg = b[:, 1024:2048]
        self.gT = b[:, 2048:2048 + S]
        self.gT_next = b[:, 3840:3840 + S]
        self.pick = b[:, 2304:2560].rearrange("p (t c) -> p t c", t=TT)
        self.sil = b[:, 2560:3072]
        self.actT = b[:, 3072:3584].rearrange("p (f c) -> p f c", f=4)
        self.pick_w = b[:, 3584:3840].rearrange("p (t c) -> p t c", t=TT)
        self.act = C.act_rows[:, :]
        w = E + 2
        self.rank = C.route[:, 0:2 * w].rearrange("p (t e) -> p t e", t=TT)
        self.gate = C.route[:, 2 * w:4 * w].rearrange("p (t e) -> p t e", t=TT)
        self.iota = C.route[:, 136:136 + S]
        self.left = C.left
        self.count = C.B[1][0:1, 544:544 + E]
        self.ow = (C.big[:, 0:4096].rearrange("p (k n) -> p k n", k=KT),
                   C.big[:, 4096:8192].rearrange("p (k n) -> p k n", k=KT),
                   C.big[:, 8192:12288].rearrange("p (k n) -> p k n", k=4))


def pick_first(nc, link, v, iota1, hot, tmp, mx, shape):
    link(nc.vector.tensor_reduce(mx, v, AX_X, ALU.max))
    link(nc.vector.tensor_tensor(tmp, v, mx.unsqueeze(2).to_broadcast(shape), ALU.is_equal))
    link(nc.vector.scalar_tensor_tensor(tmp, tmp, -1000.0, iota1.unsqueeze(1).to_broadcast(shape), ALU.mult, ALU.add))
    link(nc.vector.tensor_reduce(mx, tmp, AX_X, ALU.min))
    link(nc.vector.tensor_tensor(hot, tmp, mx.unsqueeze(2).to_broadcast(shape), ALU.is_equal))


def route_loads(C, M, w_router, rows, NL):
    b = C.B[4]
    wr = b[:, 0:KT * NL].rearrange("p (k n) -> p k n", k=KT)
    return [(wr[:, :, a:a + w.shape[1]], w.rearrange("(k p) n -> p k n", p=P)) for a, w in w_router] \
        + rows(b[:, 288:288 + NL]) + [(b[:, 384:384 + P], C.const("key_lt")), (M.iota, C.const("iota"))]


def moe1_loads(C):
    return route_loads(C, Moe(C, 16), [(0, C.t["w_router"])], lambda br: [(br, C.row("router_bias"))], 16)


def moe2_loads(C, l):
    t = C.t
    return route_loads(C, Moe(C, 32), [(0, t["moe_w_group_2"][l]), (4, t["moe_w_expert_2"][l])],
                       lambda br: [(br[:, 0:4], C.row("moe_b_group_2", 4 * l, 4)),
                                   (br[:, 4:36], C.row("moe_b_expert_2", 32 * l, 32))], 36)


def route(C, tag, M, X, hier):
    nc = C.nc
    E, G = M.E, 4
    per = E // G
    NL = E + G if hier else E
    b = C.B[4]
    wr = b[:, 0:KT * NL].rearrange("p (k n) -> p k n", k=KT)
    br = b[:, 288:288 + NL]
    lt = b[:, 384:384 + P]
    o = [512]

    def take(n, w=None):
        at = o[0]
        o[0] += TT * n
        return b[:, at:at + TT * n].rearrange("p (t n) -> p t n", t=TT)
    lg, sc = take(NL), take(NL)
    tmp, h1, h2, mk, sel, gs = take(E), take(E), take(E), take(E), take(E), take(E)
    pair = take(24)
    gtmp, ghot = take(G), take(G)
    mx, s1, s2, s3 = (take(1).rearrange("p t n -> p (t n)") for _ in range(4))
    iota1 = C.small[:, 32:32 + E]
    ghot_in = b[:, 1900:1912]
    sh, gsh = [P, TT, E], [P, TT, G]
    with stage(nc, tag, "chain logits sig chosen ranks ex") as (block, chain, logits, sig, chosen, ranks, ex):
        @block.tensor
        def _(pe):
            for tt in range(TT):
                for k in range(KT):
                    last = nc.tensor.matmul(C.PS[:, tt, 0:NL], X[:, k, tt * P:(tt + 1) * P], wr[:, k, :],
                                            start=(k == 0), stop=(k == KT - 1))
            last.then_inc(logits, 1)
            for tt in range(TT):
                for k in range(KT):
                    last = nc.tensor.transpose(C.PS[:, 4 + 2 * tt + k // 4, (k % 4) * P:(k % 4 + 1) * P],
                                               X[:, k, tt * P:(tt + 1) * P], C.ident[:, :])
            last.then_inc(logits, 1)
            pe.wait_ge(chosen, 1)
            nc.tensor.matmul(C.PS[:, 2, 0:E], lt, sel[:, 0, :], start=True, stop=True)
            nc.tensor.matmul(C.PS[:, 2, 64:64 + E], lt, sel[:, 1, :], start=True, stop=False)
            nc.tensor.matmul(C.PS[:, 2, 64:64 + E], C.ones[:, :], sel[:, 0, :], start=False, stop=True)
            for tt in range(TT):
                last = nc.tensor.matmul(C.PS[:, 3, 0:E], C.ones[:, :], sel[:, tt, :], start=(tt == 0), stop=(tt == 1))
            last.then_inc(ranks, 1)

        @block.scalar
        def _(act):
            act.wait_ge(logits, 1)
            lps = C.PS[:, 0:2, 0:NL]
            if hier:
                nc.scalar.copy(lg, lps).then_inc(sig, 1)
            else:
                nc.scalar.activation(lg, lps, ACT.Sigmoid).then_inc(sig, 1)
            act.wait_ge(logits, 2)
            for tt in range(TT):
                nc.scalar.copy(M.htok[:, tt, :], C.PS[:, 4 + 2 * tt:6 + 2 * tt, :].rearrange("p b n -> p (b n)"))
            if hier:
                act.wait_ge(ex, 1)
                nc.scalar.activation(ghot_in[:, 0:10], ghot_in[:, 0:10], ACT.Exp).then_inc(sig, 1)

        @block.vector
        def _(dve):
            link = linker(dve, chain)
            dve.wait_ge(sig, 1)
            link(nc.vector.tensor_scalar(iota1, M.iota[:, 0:E], 1001.0, None, ALU.add))
            link(nc.vector.tensor_tensor(sc, lg, br.unsqueeze(1).to_broadcast([P, TT, NL]), ALU.add))
            if hier:
                gsc, esc = sc[:, :, 0:G], sc[:, :, G:NL]
            else:
                esc = sc
                gsc = gtmp
                v = sc.rearrange("p t (g e) -> p (t g) e", e=per)
                pv = pair.rearrange("p t n -> p (t n)")[:, 0:48].rearrange("p (g n) -> p g n", n=6)
                TG = TT * G
                link(nc.vector.tensor_tensor(pv[:, :, 0:3], v[:, :, 1:4], v[:, :, 0:1].to_broadcast([P, TG, 3]), ALU.add))
                link(nc.vector.tensor_tensor(pv[:, :, 3:5], v[:, :, 2:4], v[:, :, 1:2].to_broadcast([P, TG, 2]), ALU.add))
                link(nc.vector.tensor_tensor(pv[:, :, 5:6], v[:, :, 3:4], v[:, :, 2:3], ALU.add))
                link(nc.vector.tensor_reduce(gsc.rearrange("p t g -> p (t g)"), pv, AX_X, ALU.max))
            gt = gs[:, :, 0:G]
            if hier:
                link(nc.vector.tensor_reduce(s3, gsc, AX_X, ALU.max))
                gin = ghot_in[:, 0:8].rearrange("p (t g) -> p t g", t=TT)
                link(nc.vector.tensor_tensor(gin, gsc, s3.unsqueeze(2).to_broadcast(gsh), ALU.subtract))
            pick_first(nc, link, gsc, iota1[:, 0:G], ghot, gt, mx, gsh)
            link(nc.vector.tensor_scalar(gt, ghot, 1.0, -NEG, ALU.subtract, ALU.mult))
            for tt in range(TT):
                g3 = lambda x: x[:, tt, :].rearrange("p (g e) -> p g e", e=per)
                link(nc.vector.tensor_tensor(g3(mk), g3(esc), ghot[:, tt, :].unsqueeze(2).to_broadcast([P, G, per]), ALU.mult))
                link(nc.vector.tensor_tensor(g3(mk), g3(mk), gt[:, tt, :].unsqueeze(2).to_broadcast([P, G, per]), ALU.add))
            if hier:
                link(nc.vector.tensor_reduce(s1, mk, AX_X, ALU.max))
            pick_first(nc, link, mk, iota1, h1, tmp, mx, sh)
            link(nc.vector.scalar_tensor_tensor(mk, h1, 2 * NEG, mk, ALU.mult, ALU.add))
            if hier:
                link(nc.vector.tensor_reduce(s2, mk, AX_X, ALU.max))
                link(nc.vector.tensor_tensor(ghot_in[:, 8:10], s2, s1, ALU.subtract))
                dve.sem_inc(ex, 1)
            pick_first(nc, link, mk, iota1, h2, tmp, mx, sh)
            link(nc.vector.tensor_tensor(sel, h1, h2, ALU.add))
            dve.sem_inc(chosen, 1)
            link(nc.vector.memset(M.gate[:, :, E:E + 2], 0.0))
            link(nc.vector.memset(M.rank[:, :, E:E + 2], -1.0))
            gate = M.gate[:, :, 0:E]
            if hier:
                dve.wait_ge(sig, 2)
                e2 = ghot_in[:, 8:10]
                link(nc.vector.tensor_reduce(s1, ghot_in[:, 0:8].rearrange("p (t g) -> p t g", t=TT), AX_X, ALU.add))
                link(nc.vector.tensor_scalar(s2, e2, 1.0, None, ALU.add))
                link(nc.vector.tensor_tensor(s1, s1, s2, ALU.mult))
                link(nc.vector.reciprocal(s1, s1))
                link(nc.vector.tensor_tensor(s2, s1, e2, ALU.mult))
                link(nc.vector.tensor_tensor(gate, h1, s1.unsqueeze(2).to_broadcast(sh), ALU.mult))
                link(nc.vector.tensor_tensor(tmp, h2, s2.unsqueeze(2).to_broadcast(sh), ALU.mult))
                link(nc.vector.tensor_tensor(gate, gate, tmp, ALU.add))
            else:
                link(nc.vector.tensor_tensor(tmp, lg, sel, ALU.mult))
                link(nc.vector.tensor_reduce(s1, tmp, AX_X, ALU.add))
                link(nc.vector.reciprocal(s1, s1))
                link(nc.vector.tensor_tensor(gate, tmp, s1.unsqueeze(2).to_broadcast(sh), ALU.mult))
            dve.wait_ge(ranks, 1)
            rank = M.rank[:, :, 0:E]
            link(nc.vector.scalar_tensor_tensor(tmp, C.PS[:, 2, 0:128].rearrange("p (t n) -> p t n", t=TT)[:, :, 0:E], 1.0,
                                                sel, ALU.add, ALU.mult))
            link(nc.vector.tensor_scalar(rank, tmp, -1.0, None, ALU.add))
            nc.vector.tensor_copy(M.count, C.PS[0:1, 3, 0:E])


def list_left(C, M, link):
    nc, E = C.nc, M.E
    n = 3 * E
    o1 = lambda i: C.B[1][0:1, i * 96:i * 96 + n]
    live, before, key, hit, one = (o1(i) for i in range(5))
    r3 = lambda x: x.rearrange("p (b e) -> p b e", b=3)
    for i in range(3):
        nc.vector.tensor_scalar(live[:, i * E:(i + 1) * E], M.count, float((i + 1) * M.cap), None, ALU.is_gt)
        nc.vector.tensor_copy(r3(key)[:, i, :], M.iota[0:1, 0:E])
    link(nc.vector.memset(one, 1.0))
    link(nc.vector.tensor_tensor_scan(before, one, live, 0.0, ALU.mult, ALU.add))
    link(nc.vector.tensor_copy(M.left[:, 0:1], before[:, n - 1:n]))
    link(nc.vector.tensor_tensor(before, before, live, ALU.mult))
    lst = C.B[1][0:1, 512:512 + 16]
    for j in range(MAXLEFT):
        link(nc.vector.tensor_scalar(hit, before, float(j + 1), None, ALU.is_equal))
        link(nc.vector.tensor_tensor(one, hit, key, ALU.mult))
        link(nc.vector.tensor_reduce(lst[:, j:j + 1], one, AX_X, ALU.add))
        for i in range(3):
            last = nc.vector.tensor_scalar(r3(one)[:, i, :], r3(hit)[:, i, :], float((i + 1) * M.cap), None, ALU.mult)
        link(last)
        link(nc.vector.tensor_reduce(lst[:, 8 + j:9 + j], one, AX_X, ALU.add))
    link(nc.vector.tensor_copy(M.left[:, 1:17], lst))


def build_pick(nc, M, e, done):
    for tt in range(TT):
        for x in range(2):
            col = bass.ds(e + x, 1)
            c = slice(64 * x, 64 * x + 64)
            nc.vector.tensor_scalar(M.pick[:, tt, c], M.iota[:, 0:64], M.rank[:, tt, col], None, ALU.is_equal)
            last = nc.vector.tensor_scalar(M.pick_w[:, tt, c], M.iota[:, 0:64], M.rank[:, tt, col], M.gate[:, tt, col],
                                           ALU.is_equal, ALU.mult)
    last.then_inc(done, 1)


def gather(C, M, w, done):
    nc = C.nc
    for k in range(KT):
        for tt in range(TT):
            nc.tensor.matmul(C.PS[:, k // 4, (k % 4) * P:(k % 4) * P + w], M.htok[:, tt, k * P:(k + 1) * P],
                             M.pick[:, tt, 0:w], start=(tt == 0), stop=(tt == 1))
    for tt in range(TT):
        last = nc.tensor.transpose(C.PS[0:w, 3, tt * P:(tt + 1) * P], M.pick_w[:, tt, 0:w], C.ident[:, :])
    last.then_inc(done, 1)


def take_gathered(C, M, w, done):
    nc = C.nc
    for g in range(2):
        nc.scalar.copy(M.xg[:, 4 * g:4 * g + 4, 0:w], C.PS[:, g, :].rearrange("p (k c) -> p k c", c=P)[:, :, 0:w])
    nc.scalar.copy(M.gT_next[0:w, :], C.PS[0:w, 3, 0:S]).then_inc(done, 1)


def row_product(C, x, ws, bank, col=slice(None)):
    nc = C.nc
    n = x.shape[1]
    for k in range(n):
        for i, w in enumerate(ws):
            last = nc.tensor.matmul(C.PS[64 * i:64 * i + 64, bank, :], x[:, k, 64 * i:64 * i + 64], w[:, k, col],
                                    start=(k == 0), stop=(k == n - 1))
    return last


def turn_act(C, M, w, bank):
    nc = C.nc
    for f in range(4):
        last = nc.tensor.transpose(C.PS[:, bank, f * P:f * P + w], M.act[0:w, f * P:(f + 1) * P], C.ident[0:w, 0:w])
    return last


def scatter_quarter(C, M, q, w, bank, gT):
    nc = C.nc
    for j in range(2):
        d = 2 * q + j
        last = nc.tensor.matmul(C.PS[:, bank, j * S:(j + 1) * S], M.yg[0:w, d * P:(d + 1) * P], gT[0:w, :],
                                start=True, stop=True)
    return last


def accumulate(C, M, q, bank, done):
    nc = C.nc
    y = M.yacc[:, 2 * q:2 * q + 2, :].rearrange("p j t -> p (j t)")
    nc.vector.tensor_tensor(y, y, C.PS[:, bank, :], ALU.add).then_inc(done, 1)


def experts(C, tag, M, sources):
    nc = C.nc
    E, u0 = M.E, C.used
    pairs = E // 2
    SB = (7, 5, 6, 7)
    names = "picked gathered taken gate_done up_done silu_done act_ready act_turned actT_ready down_done y_taken scattered added gT_moved chain"
    with stage(nc, tag, names) as (block, picked, gathered, taken, gate_done, up_done, silu_done, act_ready, act_turned,
                                   actT_ready, down_done, y_taken, scattered, added, gT_moved, chain):
        @block.sync
        def _(sp):
            with sp.Fori(0, pairs - 1) as i:
                for j in range(6):
                    v = u0 + RING + j
                    src = sources[j // 2](2 * i + (2 + j % 2))
                    sp.wait_ge(C.slot_free[v % RING], i + v // RING)
                    sp.dma_start(C.unit(v), src).then_inc(C.slot_loaded[v % RING], 16)
            C.refill(sp, u0 + 6 * (pairs - 1), 6)

        @block.tensor
        def _(pe):
            def arrived(i, j):
                for u in (u0 + j, u0 + j + 1):
                    pe.wait_ge(C.slot_loaded[u % RING], i * 16 + 16 * (u // RING + 1))

            def scatter(p):
                pe.wait_ge(y_taken, 2 * p + 2)
                pe.wait_ge(added, 4 * p + 1)
                for q in range(4):
                    if q == 3:
                        pe.wait_ge(added, 4 * p + 2)
                    scatter_quarter(C, M, q, P, SB[q], M.gT).then_inc(scattered, 1)
            pe.wait_ge(picked, 1)
            gather(C, M, P, gathered)
            with pe.Fori(0, pairs) as p:
                pe.wait_ge(taken, p + 1)
                arrived(p, 0)
                row_product(C, M.xg, [C.unit(u0), C.unit(u0 + 1)], 2).then_inc(gate_done, 1)
                arrived(p, 2)
                row_product(C, M.xg, [C.unit(u0 + 2), C.unit(u0 + 3)], 3).then_inc(up_done, 1)
                scatter(p)
                pe.wait_ge(act_ready, p + 1)
                turn_act(C, M, P, 4).then_inc(act_turned, 1)
                pe.wait_ge(picked, p + 2)
                gather(C, M, P, gathered)
                pe.wait_ge(actT_ready, p + 1)
                pe.wait_ge(added, 4 * p + 4)
                arrived(p, 4)
                for half in range(2):
                    row_product(C, M.actT, [C.unit(u0 + 4), C.unit(u0 + 5)], 5 + half,
                                slice(half * 512, (half + 1) * 512)).then_inc(down_done, 1)
            scatter(pairs)

        @block.scalar
        def _(act):
            act.wait_ge(gathered, 1)
            take_gathered(C, M, P, taken)
            with act.Fori(0, pairs) as p:
                act.wait_ge(gate_done, p + 1)
                for j in range(2):
                    act.sem_inc(C.freed(u0 + j), 1)
                nc.scalar.activation(M.sil, C.PS[:, 2, :], ACT.Silu).then_inc(silu_done, 1)
                act.wait_ge(act_turned, p + 1)
                nc.scalar.copy(M.actT, C.PS[:, 4, :].rearrange("p (f c) -> p f c", c=P)).then_inc(actT_ready, 1)
                act.wait_ge(gathered, p + 2)
                nc.scalar.copy(M.gT, M.gT_next).then_inc(gT_moved, 1)
                act.wait_ge(gT_moved, p + 1)
                take_gathered(C, M, P, taken)
                for half in range(2):
                    act.wait_ge(down_done, 2 * p + (half + 1))
                    if half:
                        for j in range(4, 6):
                            act.sem_inc(C.freed(u0 + j), 1)
                    nc.scalar.copy(M.yg[:, half * 512:(half + 1) * 512], C.PS[:, 5 + half, :]).then_inc(y_taken, 1)

        @block.vector
        def _(dve):
            build_pick(nc, M, 0, picked)
            nc.vector.memset(M.gT, 0.0).then_inc(y_taken, 1)
            nc.vector.memset(M.yg, 0.0).then_inc(y_taken, 1)
            nc.vector.memset(M.yacc, 0.0).then_inc(added, 1)
            list_left(C, M, linker(dve, chain))
            with dve.Fori(0, pairs) as p:
                dve.wait_ge(gathered, p + 1)
                build_pick(nc, M, 2 * p + 2, picked)
                dve.wait_ge(silu_done, p + 1)
                dve.wait_ge(up_done, p + 1)
                for j in range(2, 4):
                    dve.sem_inc(C.freed(u0 + j), 1)
                nc.vector.tensor_tensor(M.act, M.sil, C.PS[:, 3, :], ALU.mult).then_inc(act_ready, 1)
                for q in range(4):
                    dve.wait_ge(scattered, 4 * p + (q + 1))
                    accumulate(C, M, q, SB[q], added)
            for q in range(4):
                dve.wait_ge(scattered, 4 * pairs + q + 1)
                accumulate(C, M, q, SB[q], added)
    C.used += 6 * pairs


def experts_left(C, tag, M, sources):
    nc = C.nc
    names = "gate_in up_in down_in picked gathered taken gate_done silu_done act_ready act_turned actT_ready down_done y_taken scattered added"
    with stage(nc, tag, names) as (block, gate_in, up_in, down_in, picked, gathered, taken, gate_done, silu_done, act_ready, act_turned,
                                   actT_ready, down_done, y_taken, scattered, added):
        def blocks(eng, body):
            count = eng.value_load(M.left[0:1, 0:1], min_val=0, max_val=MAXLEFT)
            with eng.If(count > 0):
                with eng.Fori(0, count) as n:
                    body(n)

        def entry(eng, at, n, top):
            return eng.value_load(M.left[0:1, bass.ds(n + at, 1)], min_val=0, max_val=top)

        @block.sync
        def _(sp):
            def body(n):
                e = entry(sp, 1, n, M.E - 1)
                srcs = [s(e) for s in sources]
                sp.wait_ge(down_done, n + 1)
                for dst, src, loaded in zip(M.ow, srcs, (gate_in, up_in, down_in)):
                    sp.dma_start(dst, src).then_inc(loaded, 16)
            blocks(sp, body)

        @block.tensor
        def _(pe):
            pe.sem_inc(down_done, 1)

            def body(n):
                pe.wait_ge(added, n + 1)
                pe.wait_ge(picked, n + 1)
                gather(C, M, 64, gathered)
                pe.wait_ge(taken, n + 1)
                pe.wait_ge(gate_in, n * 16 + 16)
                row_product(C, M.xg, [M.ow[0]], 2)
                pe.wait_ge(up_in, n * 16 + 16)
                row_product(C, M.xg, [M.ow[1]], 3).then_inc(gate_done, 1)
                pe.wait_ge(act_ready, n + 1)
                turn_act(C, M, P, 4).then_inc(act_turned, 1)
                pe.wait_ge(actT_ready, n + 1)
                pe.wait_ge(down_in, n * 16 + 16)
                row_product(C, M.actT, [M.ow[2]], 5, slice(0, 512))
                row_product(C, M.actT, [M.ow[2]], 6, slice(512, 1024)).then_inc(down_done, 1)
                pe.wait_ge(y_taken, n + 1)
                for q in range(4):
                    last = scatter_quarter(C, M, q, 64, q, M.gT_next)
                last.then_inc(scattered, 1)
            blocks(pe, body)

        @block.scalar
        def _(act):
            def body(n):
                act.wait_ge(gathered, n + 1)
                take_gathered(C, M, 64, taken)
                act.wait_ge(gate_done, n + 1)
                nc.scalar.activation(M.sil[0:64, :], C.PS[0:64, 2, :], ACT.Silu).then_inc(silu_done, 1)
                act.wait_ge(act_turned, n + 1)
                nc.scalar.copy(M.actT[:, :, 0:64],
                               C.PS[:, 4, :].rearrange("p (f c) -> p f c", c=P)[:, :, 0:64]).then_inc(actT_ready, 1)
                act.wait_ge(down_done, n + 2)
                nc.scalar.copy(M.yg[0:64, :], C.PS[0:64, 5:7, :].rearrange("p b n -> p (b n)")).then_inc(y_taken, 1)
            blocks(act, body)

        @block.vector
        def _(dve):
            dve.sem_inc(added, 1)

            def body(n):
                e, first = entry(dve, 1, n, M.E - 1), entry(dve, 9, n, S - 64)
                for tt in range(TT):
                    col = bass.ds(e, 1)
                    want = M.iota[:, bass.ds(first, 64)]
                    nc.vector.tensor_scalar(M.pick[:, tt, 0:64], want, M.rank[:, tt, col], None, ALU.is_equal)
                    last = nc.vector.tensor_scalar(M.pick_w[:, tt, 0:64], want, M.rank[:, tt, col], M.gate[:, tt, col],
                                                   ALU.is_equal, ALU.mult)
                last.then_inc(picked, 1)
                dve.wait_ge(silu_done, n + 1)
                nc.vector.tensor_tensor(M.act[0:64, :], M.sil[0:64, :], C.PS[0:64, 3, :], ALU.mult).then_inc(act_ready, 1)
                dve.wait_ge(scattered, n + 1)
                y = M.yacc.rearrange("p j t -> p (j t)")
                nc.vector.tensor_tensor(y, y, C.PS[:, 0:4, :].rearrange("p b n -> p (b n)"), ALU.add).then_inc(added, 1)
            blocks(dve, body)


def moe1(C, tag, l):
    t = C.t
    M = Moe(C, 16)
    route(C, tag + "r", M, C.H, False)
    gu = t["moe_w_gu"][l].rearrange("e (k p) n -> e p k n", p=P)
    dn = t["moe_w_down"][l].rearrange("e (k p) n -> e p k n", p=P)
    src = (lambda e: gu[e, :, :, 0:512], lambda e: gu[e, :, :, 512:1024], lambda e: dn[e])
    experts(C, tag + "e", M, src)
    experts_left(C, tag + "o", M, src)

    def close(k):
        return C.nc.vector.scalar_tensor_tensor(C.X[:, k, :], M.yacc[:, k, :], C.mod[:, 48 * l + 40 + k:48 * l + 41 + k],
                                                C.X[:, k, :], ALU.mult, ALU.add)
    return close


def moe2(C, tag, l):
    t = C.t
    M = Moe(C, 32)
    route(C, tag + "r", M, C.X, True)
    v = lambda w: w[l].rearrange("e (k p) n -> e p k n", p=P)
    g, u, d = v(t["moe_w_gate_2"]), v(t["moe_w_up_2"]), v(t["moe_w_down_2"])
    src = (lambda e: g[e], lambda e: u[e], lambda e: d[e])
    experts(C, tag + "e", M, src)
    experts_left(C, tag + "o", M, src)
    T = M.yacc

    def close(k):
        return C.nc.vector.scalar_tensor_tensor(T[:, k, :], C.X[:, k, :], ALPHA, T[:, k, :], ALU.mult, ALU.add)
    return T, close



def mixer_ab_loads(C):
    t = C.t
    W, w2, g2 = C.B[3], C.B[9][:, 0:512], C.B[9][:, 512:1024]
    Hf = C.H[:, :, :].rearrange("p j t -> p (j t)")
    return [(W[:, 0:512].rearrange("p (g t) -> p g t", g=4), t["sg_ws_T"]), (W[:, 512:1024], C.row("sg_ln_g_2")),
            (W[:, 1024:1536], C.row("sg_ln_b_2")), (W[:, 1536:2048], C.row("sg_b_2")),
            (C.B[4][:, 1024:1152], C.const("key_le")),
            (w2[0:64, :], t["rw_w2_2"]), (w2[64:128, :], t["rw_a2_2"]), (g2, t["rw_g2_2"])] \
        + [(Hf[:, 1024 + i * P:1024 + (i + 1) * P], C.const(n))
           for i, n in enumerate(("rw_d", "rw_dT", "rw_oT", "rw_ltT", "rw_leT"))]


def mixer_ab(C, close):
    nc = C.nc
    B = C.B
    half = lambda b, i: tiles3(b, 4 * i, 4)
    PR = C.big[:, 0:14 * S].rearrange("p (j t) -> p j t", t=S)
    U = half(B[2], 0)
    Z = B[2][:, 1024:2048].rearrange("p (t c) -> p t c", t=TT)
    MIX = tiles3(B[9])
    DF = [tiles3(B[8], 4, 2), half(B[6], 0), half(B[6], 1), half(B[8], 0)]

    ws = B[3][:, 0:512].rearrange("p (g t) -> p g t", g=4)
    lng, lnb = B[3][:, 512:1024], B[3][:, 1024:1536]
    bs = B[3][:, 1536:2048].rearrange("p (g t) -> p g t", g=4)
    q3 = B[4][:, 0:1024].rearrange("p (a c) -> p a c", c=P)
    le = B[4][:, 1024:1152]
    mean, var = B[4][:, 1152:1160], B[4][:, 1160:1168]
    z = Z.rearrange("p t (g c) -> p (t g) c", g=4)
    full = lambda x: x.unsqueeze(2).to_broadcast([P, 8, P])
    tiles = cm_tiles(C, 0, C.X) + tm_tiles(C, 1, C.X) + cm_tiles(C, 2, C.X)
    tiles += cm_tiles(C, 3, C.X) + cm_tiles(C, 4, C.X, cols=256)
    first_mix = len(tiles)
    tiles += [(None, [(Z[:, tt, g * P:(g + 1) * P], ws[:, g, :])], P, P) for g in range(4) for tt in range(TT)]
    late = {i: -3 for i in range(first_mix, len(tiles))}
    tiles += cm_tiles(C, 4, C.X, cols=256, at=256) + cm_tiles(C, 5, C.X)
    kind = [i for i in range(len(tiles)) if i not in late]

    def evict(act, i, ps):
        i = kind.index(i)
        if i < 4:
            return nc.scalar.activation(U[:, i, :], ps, ACT.Gelu_apprx_tanh)
        if i < 6:
            return nc.scalar.activation(Z[:, i - 4, :], ps, ACT.Gelu_apprx_tanh)
        return nc.scalar.copy(PR[:, 12 + i - 6 if i < 8 else i - 8, :], ps)

    def shift(dve, link, j0, n, df):
        pr = PR[:, j0:j0 + n, :]
        nc.vector.tensor_tensor(df[:, :, 1:S], pr[:, :, 0:S - 1], pr[:, :, 1:S], ALU.subtract)
        link(nc.vector.tensor_scalar(df[:, :, 0:1], pr[:, :, 0:1], -1.0, None, ALU.mult))
        for j in range(n):
            last = nc.vector.scalar_tensor_tensor(pr[:, j, :], df[:, j, :], C.v("ab_mu_2", j0 + j), pr[:, j, :],
                                                  ALU.mult, ALU.add)
        return last

    def gate_norm(dve, link, evicted, aside, reply, landed):
        for k in range(KT):
            close(k).then_inc(reply, 1)
        dve.wait_ge(landed, 16 * len(mixer_ab_loads(C)))
        dve.wait_ge(evicted, 6)
        nc.vector.tensor_tensor(ws, ws, le.unsqueeze(1).to_broadcast([P, 4, P]), ALU.mult)
        link(nc.vector.tensor_reduce(mean, z, AX_X, ALU.add))
        link(nc.vector.tensor_scalar(mean, mean, 1.0 / P, None, ALU.mult))
        link(nc.vector.tensor_tensor(z, z, full(mean), ALU.subtract))
        link(nc.vector.tensor_tensor(q3, z, z, ALU.mult))
        link(nc.vector.tensor_reduce(var, q3, AX_X, ALU.add))
        nc.vector.tensor_scalar(var, var, 1.0 / P, LN_EPS, ALU.mult, ALU.add).then_inc(aside, 1)
        dve.wait_ge(aside, 2)
        link(nc.vector.reciprocal(var, var))
        link(nc.vector.tensor_tensor(z, z, full(var), ALU.mult))
        both = lambda x: x.unsqueeze(1).to_broadcast([P, TT, 512])
        link(nc.vector.tensor_tensor(Z, Z, both(lng), ALU.mult))
        nc.vector.tensor_tensor(Z, Z, both(lnb), ALU.add).then_inc(aside, 1)
        dve.wait_ge(evicted, 8)
        shift(dve, link, 12, 2, DF[0]).then_inc(aside, 1)

    def whole(pe, aside, reply):
        pe.wait_ge(reply, KT)

    def gate_root(act, aside, evicted):
        act.wait_ge(aside, 1)
        nc.scalar.activation(var, var, ACT.Sqrt).then_inc(aside, 1)

    def low_rank(act, aside, evicted):
        act.wait_ge(aside, 4)
        nc.scalar.activation(PR[0:64, 12, :], PR[0:64, 12, :], ACT.Tanh)
        nc.scalar.activation(PR[:, 13, :], PR[:, 13, :], ACT.Sigmoid)

    def mixed(link, i, ps):
        g, tt = divmod(i - first_mix, 2)
        c = slice(tt * P, (tt + 1) * P)
        link(nc.vector.tensor_tensor(q3[:, i - first_mix, :], ps, bs[:, g, :], ALU.add))
        return nc.vector.tensor_tensor(MIX[:, 4 + g, c], q3[:, i - first_mix, :], U[:, g, c], ALU.mult)

    def shifts(dve, link, evicted):
        for n in range(3):
            dve.wait_ge(evicted, 12 + 4 * n)
            shift(dve, link, 4 * n, 4, DF[1 + n])
    project(C, "ab_in", tiles, 6, evict, loads=mixer_ab_loads(C), late=late, late_evict=mixed, vector=gate_norm,
            vector_end=shifts, scalar_at={9: gate_root, first_mix + 8: low_rank}, tensor_at={0: whole})

    w2, g2 = B[9][:, 0:512], B[9][:, 512:1024]
    r, k, v = PR[:, 0:4, :], PR[:, 4:8, :], PR[:, 8:12, :]
    A, G = half(B[3], 0), half(B[3], 1)
    LW, CS = half(B[4], 0), half(B[4], 1)
    tiles = [(None, [(w2[0:64, j * P:(j + 1) * P], PR[0:64, 12, :])], P, S) for j in range(4)] \
        + [(None, [(w2[64:128, j * P:(j + 1) * P], PR[64:128, 12, :])], P, S) for j in range(4)] \
        + [(None, [(g2[:, j * P:(j + 1) * P], PR[:, 13, :])], P, S) for j in range(4)]

    def evict(act, i, ps):
        if i < 4:
            return nc.scalar.activation(LW[:, i, :], ps, ACT.Sigmoid, bias=C.v("rw_w0_2", i))
        if i < 8:
            return nc.scalar.activation(A[:, i - 4, :], ps, ACT.Sigmoid, bias=C.v("rw_a0_2", i - 4))
        return nc.scalar.copy(G[:, i - 8, :], ps)

    KK, BV = half(B[5], 0), half(B[5], 1)
    K2, E = half(B[6], 0), half(B[6], 1)
    At, Bt, Kt, Rt = half(B[7], 0), half(B[7], 1), half(B[8], 0), half(B[8], 1)
    RN = half(B[8], 1)
    BON = A
    flat = lambda x: x.rearrange("p j t -> p (j t)")
    PC = C.small[:, 32:64].rearrange("p (j c) -> p j c", j=4)

    def decays(dve, link, evicted, aside, reply, landed):
        for j in range(4):
            nc.vector.tensor_scalar(KK[:, j, :], k[:, j, :], C.v("rw_k_k_2", j), None, ALU.mult)
        link(nc.vector.memset(E, 1.0))
        link(nc.vector.memset(flat(E).rearrange("p (n c) -> p n c", c=RC)[:, :, 0:1], 0.0))
        dve.wait_ge(evicted, 4)
        link(nc.vector.tensor_scalar(LW, LW, -math.exp(-0.5), None, ALU.mult))
        link(nc.vector.tensor_tensor_scan(flat(CS), flat(E), flat(LW), 0.0, ALU.mult, ALU.add))
        nc.vector.tensor_tensor(LW, CS, LW, ALU.subtract)
        dve.wait_ge(evicted, 8)
        for j in range(4):
            last = nc.vector.tensor_scalar(K2[:, j, :], A[:, j, :], 1.0, C.v("rw_k_a_2", j), ALU.subtract, ALU.mult)
        link(last)
        link(nc.vector.scalar_tensor_tensor(K2, K2, 1.0, k, ALU.add, ALU.mult))
        for j in range(4):
            nc.vector.scalar_tensor_tensor(E[:, j, :], r[:, j, :], C.v("rw_r_k_2", j), K2[:, j, :], ALU.mult, ALU.mult)
    project(C, "rw_lora", tiles, 0, evict, vector=decays)

    def post(link, b):
        w = slice(2 * b, 2 * b + 2)
        link(nc.vector.tensor_tensor(KK[:, w, :], KK[:, w, :], RN[:, w, :], ALU.mult))
        nc.vector.tensor_tensor(BV[:, w, :], KK[:, w, :], A[:, w, :], ALU.mult)
    norm(C, "rw_kkn", KK, 4, 1, C.ones64[:, :], 1, None, At, RN, post, floor=1e-12)

    Btok, Ktok = (B[4][:, i * 1024:(i + 1) * 1024].rearrange("p (t c) -> p t c", t=TT) for i in range(2))
    Htok, Vtok = (B[2][:, i * 1024:(i + 1) * 1024].rearrange("p (t c) -> p t c", t=TT) for i in range(2))
    with stage(nc, "rw_scale", "chain expd bonus made turned") as (block, chain, expd, bonus, made, turned):
        @block.tensor
        def _(pe):
            for j in range(4):
                last = nc.tensor.matmul(C.PS[:, j // 2, (j % 2) * S:(j % 2 + 1) * S], C.ones64[:, :], E[:, j, :],
                                        start=True, stop=True)
            last.then_inc(bonus, 1)
            for n, src in enumerate((v, Bt, Kt)):
                if n:
                    pe.wait_ge(made, n)
                for tt in range(TT):
                    for j in range(4):
                        last = nc.tensor.transpose(C.PS[:, 2 + 2 * n + tt, j * P:(j + 1) * P],
                                                   src[:, j, tt * P:(tt + 1) * P], C.ident[:, :])
                last.then_inc(turned, 1)

        @block.scalar
        def _(act):
            nc.scalar.activation(Bt, CS, ACT.Exp, scale=-1.0).then_inc(expd, 1)
            nc.scalar.activation(Rt, CS, ACT.Exp).then_inc(expd, 1)
            nc.scalar.activation(At, LW, ACT.Exp).then_inc(expd, 1)
            act.wait_ge(expd, 3)
            for n, dst in enumerate((Vtok, Btok, Ktok)):
                act.wait_ge(turned, n + 1)
                nc.scalar.copy(dst, C.PS[:, 2 + 2 * n:4 + 2 * n, :])

        @block.vector
        def _(dve):
            link = linker(dve, chain)
            dve.wait_ge(expd, 1)
            link(nc.vector.tensor_tensor(Kt, K2, Bt, ALU.mult))
            nc.vector.tensor_tensor(Bt, BV, Bt, ALU.mult).then_inc(made, 2)
            dve.wait_ge(bonus, 1)
            nc.vector.tensor_tensor(BON, C.PS[:, 0:2, :].rearrange("p b (h t) -> p (b h) t", t=S), v, ALU.mult)
            dve.wait_ge(expd, 3)
            link(nc.vector.tensor_copy(PC, flat(Rt).rearrange("p (j c u) -> p j c u", j=4, u=RC)[:, :, :, RC - 1]))
            nc.vector.tensor_tensor(Rt, r, Rt, ALU.mult)
            nc.vector.scalar_tensor_tensor(At, At, -1.0, KK, ALU.mult, ALU.mult)

    m8 = lambda x: x.rearrange("p (h c) -> p h c", c=P)
    UM, UT = m8(B[0][:, 0:1024]), m8(B[0][:, 1024:2048])
    OT, NT = m8(B[1][:, 0:1024]), m8(B[1][:, 1024:2048])
    X0 = m8(B[9][:, 0:1024])
    Hf = C.H[:, :, :].rearrange("p j t -> p (j t)")
    WT = m8(Hf[:, 0:1024])
    masks = [Hf[:, 1024 + i * P:1024 + (i + 1) * P] for i in range(5)]
    m_d, m_dT, m_oT, m_ltT, m_leT = (x.unsqueeze(1).to_broadcast([P, 8, P]) for x in masks)
    ident8 = C.ident[:, :].unsqueeze(1).to_broadcast([P, 8, P])
    MB, MK = (b.rearrange("p (t h c) -> p t h c", t=TT, h=8) for b in (B[5], B[6]))
    GT = At
    Y, Zs = UM, UT

    def bank8(b):
        return C.PS[:, b:b + 2, :].rearrange("p b (h c) -> p (b h) c", c=P)

    for tb in range(TT):
        tc = slice(tb * P, (tb + 1) * P)
        rows = [(slice(64 * (i // 4), 64 * (i // 4) + 64), i % 4) for i in range(8)]
        hcol = [slice(P * (i % 4) + 64 * (i // 4), P * (i % 4) + 64 * (i // 4) + 64) for i in range(8)]

        def products(pe, bank, lhs, rhs):
            for i, (rw, pair) in enumerate(rows):
                last = nc.tensor.matmul(bank8(bank)[:, i, :], lhs[rw, pair, tc], rhs[rw, pair, tc], start=True, stop=True)
            return last

        def each(bank, lhs, rhs):
            for i in range(8):
                last = nc.tensor.matmul(bank8(bank)[:, i, 0:rhs.shape[2]], lhs[:, i, :], rhs[:, i, :], start=True, stop=True)
            return last

        with stage(nc, f"rw_mat{tb}", "chain product masked turned") as (block, chain, product, masked, turned):
            @block.tensor
            def _(pe):
                products(pe, 0, Bt, At).then_inc(product, 1)
                products(pe, 2, At, Bt).then_inc(product, 1)
                products(pe, 4, Kt, At).then_inc(product, 1)
                products(pe, 6, Bt, Rt).then_inc(product, 1)
                pe.wait_ge(masked, 1)
                products(pe, 0, Kt, Rt).then_inc(product, 1)
                pe.wait_ge(masked, 2)
                for j in range(4):
                    last = nc.tensor.transpose(C.PS[:, 2, j * P:(j + 1) * P], At[:, j, tc], C.ident[:, :])
                last.then_inc(turned, 1)
                pe.wait_ge(masked, 3)
                for i in range(8):
                    last = nc.tensor.matmul(C.PS[:, 4, i * 64:(i + 1) * 64], NT[:, i, :], Vtok[:, tb, hcol[i]], start=True, stop=True)
                last.then_inc(turned, 1)

            @block.vector
            def _(dve):
                link = linker(dve, chain)
                dve.wait_ge(product, 1)
                link(nc.vector.tensor_tensor(UT, bank8(0), m_dT, ALU.mult))
                link(nc.vector.tensor_tensor(OT, bank8(0), m_oT, ALU.mult))
                dve.sem_inc(masked, 1)
                dve.wait_ge(product, 2)
                link(nc.vector.tensor_tensor(UM, bank8(2), m_d, ALU.mult))
                dve.sem_inc(masked, 1)
                dve.wait_ge(product, 3)
                link(nc.vector.tensor_tensor(NT, bank8(4), m_ltT, ALU.mult))
                dve.sem_inc(masked, 1)
                link(nc.vector.tensor_tensor(WT, UT, ident8, ALU.add))
                dve.wait_ge(product, 5)
                link(nc.vector.tensor_tensor(MB[:, tb, :, :], bank8(6), m_leT, ALU.mult))
                link(nc.vector.tensor_tensor(MK[:, tb, :, :], bank8(0), m_leT, ALU.mult))

            @block.scalar
            def _(act):
                act.wait_ge(turned, 1)
                for hh in range(2):
                    nc.scalar.copy(X0[:, 4 * hh:4 * hh + 4, 0:64],
                                   C.PS[:, 2, :].rearrange("p (j c) -> p j c", c=P)[:, :, 64 * hh:64 * hh + 64])
                act.wait_ge(turned, 2)
                nc.scalar.copy(X0[:, :, 64:128], C.PS[:, 4, :].rearrange("p (i c) -> p i c", c=64))

        with stage(nc, f"rw_inv{tb}", "chain squared grown taken taken_T applied solved gturned") as (
                block, chain, squared, grown, taken, taken_T, applied, solved, gturned):
            @block.tensor
            def _(pe):
                for n in range(3):
                    if n:
                        pe.wait_ge(taken_T, n)
                    last = each(0, UT, UM)
                    if n < 2:
                        last = each(2, UM, UT)
                    last.then_inc(squared, 1)
                    pe.wait_ge(taken, n + 1)
                    if n:
                        pe.wait_ge(grown, n)
                    each(4, UM, WT).then_inc(applied, 1)
                pe.wait_ge(grown, 3)
                each(0, WT, X0).then_inc(applied, 1)
                pe.wait_ge(solved, 2)
                each(2, OT, Y).then_inc(applied, 1)
                pe.wait_ge(solved, 4)
                each(4, WT, Zs).then_inc(applied, 1)
                pe.wait_ge(solved, 5)
                gt = X0.rearrange("p h c -> p (h c)")
                for j in range(4):
                    last = nc.tensor.transpose(C.PS[:, 6, j * P:(j + 1) * P], gt[:, j * P:(j + 1) * P], C.ident[:, :])
                last.then_inc(gturned, 1)

            @block.scalar
            def _(act):
                for n in range(3):
                    act.wait_ge(squared, n + 1)
                    if n:
                        act.wait_ge(applied, n)
                    nc.scalar.copy(UM, bank8(0)).then_inc(taken, 1)
                for n, (dst, b) in enumerate(((Y, 0), (Zs, 2))):
                    act.wait_ge(applied, 4 + n)
                    nc.scalar.copy(dst[:, 0:4, :], bank8(b)[:, 0:4, :]).then_inc(solved, 1)
                act.wait_ge(gturned, 1)
                nc.scalar.copy(GT[:, :, tc], C.PS[:, 6, :].rearrange("p (j c) -> p j c", c=P))

            @block.vector
            def _(dve):
                link = linker(dve, chain)
                for n in range(3):
                    if n < 2:
                        dve.wait_ge(squared, n + 1)
                        if n:
                            dve.wait_ge(applied, n)
                        nc.vector.tensor_copy(UT, bank8(2)).then_inc(taken_T, 1)
                    dve.wait_ge(applied, n + 1)
                    link(nc.vector.tensor_tensor(WT, WT, bank8(4), ALU.add))
                    dve.sem_inc(grown, 1)
                for n, (dst, b) in enumerate(((Y, 0), (Zs, 2))):
                    dve.wait_ge(applied, 4 + n)
                    nc.vector.tensor_copy(dst[:, 4:8, :], bank8(b)[:, 4:8, :]).then_inc(solved, 1)
                dve.wait_ge(applied, 6)
                g = X0.rearrange("p h c -> p (h c)")[:, 0:512].rearrange("p (j x c) -> p x j c", x=2, c=64)
                hh = Htok[:, tb, :].rearrange("p (j x c) -> p x j c", x=2, c=64)
                for x in range(2):
                    ys, ps = Y[:, 4 * x:4 * x + 4, :], bank8(4)[:, 4 * x:4 * x + 4, :]
                    link(nc.vector.tensor_tensor(g[:, x], ys[:, :, 0:64], ps[:, :, 0:64], ALU.add))
                    link(nc.vector.tensor_tensor(hh[:, x], ys[:, :, 64:128], ps[:, :, 64:128], ALU.add))
                dve.sem_inc(solved, 1)

    ST = B[0][:, 0:512].rearrange("p (j c) -> p j c", c=P)
    TMP = B[0][:, 512:1024].rearrange("p (j c) -> p j c", c=P)
    DEC = B[0][:, 1024:1536].rearrange("p (j c) -> p j c", c=P)
    YT, YI = half(B[1], 0), half(B[1], 1)
    bd = C.ones64[:, :].unsqueeze(1).to_broadcast([P, 4, P])
    ps4 = lambda b, rw=slice(0, P): C.PS[rw, b, :].rearrange("p (j c) -> p j c", c=P)
    with stage(nc, "rw_seq", "chain state read sa update shown intra") as (block, chain, state, read, sa, update, shown, intra):
        @block.tensor
        def _(pe):
            for c in range(S // RC):
                tb, at = divmod(c * RC, P)
                rw = slice(at, at + RC)
                col = slice(c * RC, (c + 1) * RC)
                pe.wait_ge(state, c + 1)
                for j in range(4):
                    last = nc.tensor.matmul(ps4(0, rw)[:, j, :], GT[:, j, col], ST[:, j, :], start=True, stop=True)
                last.then_inc(read, 1)
                for j in range(4):
                    jc = slice(j * P, (j + 1) * P)
                    nc.tensor.matmul(ps4(1)[:, j, :], Ktok[rw, tb, jc], Vtok[rw, tb, jc], start=(j == 0), stop=False)
                pe.wait_ge(sa, c + 1)
                for j in range(4):
                    jc = slice(j * P, (j + 1) * P)
                    last = nc.tensor.matmul(ps4(1)[:, j, :], Btok[rw, tb, jc], Htok[rw, tb, jc], start=False, stop=(j == 3))
                last.then_inc(update, 1)
                for j in range(4):
                    last = nc.tensor.matmul(C.PS[:, 2 + j // 2, (j % 2) * S + c * RC:(j % 2) * S + (c + 1) * RC],
                                            ST[:, j, :], Rt[:, j, col], start=True, stop=True)
                last.then_inc(shown, 1)
            for tb in range(TT):
                for i in range(8):
                    o = C.PS[64 * (i // 4):64 * (i // 4) + 64, 4 + (i % 4) // 2, ((i % 4) % 2) * S + tb * P:((i % 4) % 2) * S + (tb + 1) * P]
                    hc = slice(P * (i % 4) + 64 * (i // 4), P * (i % 4) + 64 * (i // 4) + 64)
                    nc.tensor.matmul(o, Htok[:, tb, hc], MB[:, tb, i, :], start=True, stop=False)
                    last = nc.tensor.matmul(o, Vtok[:, tb, hc], MK[:, tb, i, :], start=False, stop=True)
            last.then_inc(intra, 1)

        @block.vector
        def _(dve):
            link = linker(dve, chain)
            link(nc.vector.memset(ST, 0.0))
            dve.sem_inc(state, 1)
            for c in range(S // RC):
                tb, at = divmod(c * RC, P)
                rw = slice(at, at + RC)
                dve.wait_ge(read, c + 1)
                link(nc.vector.tensor_tensor(Htok[rw, tb, :], Htok[rw, tb, :], C.PS[rw, 0, :], ALU.add))
                dve.sem_inc(sa, 1)
                decay = PC[:, :, c:c + 1].to_broadcast([P, 4, P])
                nc.vector.tensor_tensor(TMP, ST, decay, ALU.mult)
                link(nc.vector.tensor_tensor(DEC, bd, decay, ALU.mult))
                dve.wait_ge(update, c + 1)
                link(nc.vector.tensor_tensor(DEC, ps4(1), DEC, ALU.mult))
                dve.wait_ge(shown, c + 1)
                link(nc.vector.tensor_tensor(ST, TMP, DEC, ALU.add))
                dve.sem_inc(state, 1)
            dve.wait_ge(intra, 1)
            t4 = lambda b: C.PS[:, b:b + 2, :].rearrange("p b (h t) -> p (b h) t", t=S)
            link(nc.vector.tensor_copy(YT, t4(4)))
            link(nc.vector.tensor_tensor(YT, YT, t4(2), ALU.add))

    def setup(link):
        for j in range(4):
            last = nc.vector.tensor_scalar(BON[:, j, :], BON[:, j, :], C.v("rw_gn_b_2", j), None, ALU.add)
        link(last)

    def post(link, b):
        w = slice(2 * b, 2 * b + 2)
        for j in range(2 * b, 2 * b + 2):
            last = nc.vector.scalar_tensor_tensor(YI[:, j, :], YI[:, j, :], C.v("rw_gn_g_2", j), RN[:, j, :], ALU.mult, ALU.mult)
        link(last)
        link(nc.vector.tensor_tensor(YI[:, w, :], YI[:, w, :], BON[:, w, :], ALU.add))
        nc.vector.tensor_tensor(MIX[:, w, :], YI[:, w, :], G[:, w, :], ALU.mult)
    norm(C, "rw_gn", YT, 4, 1, C.ones64[:, :], 64, GN_EPS_COL, B[7][:, 0:1024], RN, post, center=YI, setup=setup)
    T = tiles3(B[0])
    project(C, "ab_out", cm_tiles(C, 0, MIX) + cm_tiles(C, 1, MIX), 2, add_alpha(C, T), on="dve",
            loads=cross_attention_loads(C))
    return T



def weight_plan(t):
    plan = []
    ada0 = w_units(t["w_ada"][0])
    plan += ada0[:4]
    for l in range(2):
        if l == 0:
            w_in, rest = iter(w_units(t["a_w_in"][:, 0:3072])), iter(ada0[4:])
            plan += [next(w_in if x == "w" else rest) for x in ML_UNITS] + w_units(t["w_ada"][1]) + w_units(t["a_w_out"])
        else:
            plan += w_units(t["b_w_in"]) + w_units(t["b_w_out"])
        gu = t["moe_w_gu"][l].rearrange("e (k p) n -> e p k n", p=P)
        dn = t["moe_w_down"][l].rearrange("e (k p) n -> e p k n", p=P)
        for e in range(0, 16, 2):
            plan += [w for x in (gu[:, :, :, 0:512], gu[:, :, :, 512:1024], dn) for w in (x[e], x[e + 1])]
    for l in range(2):
        if l == 0:
            w = w_units(t["ab_w_in_2"], [512, 512, 512, 256, 512, 512])
            plan += w[4:6] + w[3:4] + w[0:3] + w_units(t["ab_w_out_2"])
        else:
            w = t["mla_w_in_2"]
            plan += w_units(w[:, 0:512]) + [w.rearrange("(k p) n -> p k n", p=P)[:, :, 448:544]]
            plan += w_units(t["mla_wq_b_2"]) + w_units(t["mla_wkv_b_2"]) + w_units(t["mla_w_out_2"])
        plan += w_units(t["xa_wkv_2"][l]) + w_units(t["xa_wq_2"][l]) + w_units(t["xa_wo_2"][l])
        v = [t[n][l].rearrange("e (k p) n -> e p k n", p=P) for n in ("moe_w_gate_2", "moe_w_up_2", "moe_w_down_2")]
        for e in range(0, 32, 2):
            plan += [w for x in v for w in (x[e], x[e + 1])]
    return plan


def two_blocks(nc, t, cnames, out):
    with ExitStack() as ctx:
        C = Chip(nc, t, ctx, cnames)
        C.plan = weight_plan(t)
        with stage(nc, "start", "landed") as (block, landed):
            @block.sync
            def _(sp):
                small = [(C.vec[:, :], t["vec"]), (C.ident[:, :], C.const("ident")), (C.ones[:, :], C.const("ones")),
                         (C.ones64[:, :], C.const("ones64")), (C.X[:, :, :], t["x_T"])] + mlstm_loads(C)
                for dst, src in small:
                    sp.dma_start(dst, src).then_inc(landed, 16)
                for v in range(RING):
                    C.load(sp, v)
                sp.wait_ge(landed, 16 * len(small))
            @block.vector
            def _(dve):
                for col, value in ((EPS_COL, EPS), (LN_EPS_COL, LN_EPS), (GN_EPS_COL, GN_EPS), (ONE_COL, 1.0)):
                    nc.vector.memset(C.small[:, col:col + 1], value)
        ada_start(C)
        ada_finish(C, "ada_first", 4, n=4)
        close = None
        for l in range(2):
            mod = C.mod[:, 48 * l:48 * l + 48]
            modulated_norm(C, f"n1_{l}", C.v("norm1", 8 * l, 8), mod[:, 0:8], mod[:, 8:16],
                           diff_attention_loads(C) if l else (), close)
            (mlstm, diff_attention)[l](C)
            modulated_norm(C, f"n2_{l}", C.v("norm2", 8 * l, 8), mod[:, 24:32], mod[:, 32:40], moe1_loads(C))
            close = moe1(C, f"moe1_{l}", l)
        for l in range(2):
            gb = lambda n: (C.v(f"ln{n}_g_2", 8 * l, 8), C.v(f"ln{n}_b_2", 8 * l, 8))
            T = mla(C) if l else mixer_ab(C, close)
            T = cross_attention(C, f"xa{l}", T, *gb(1))
            layer_norm(C, f"ln2_{l}", T, *gb(2), moe2_loads(C, l))
            T, last = moe2(C, f"moe2_{l}", l)
            layer_norm(C, f"ln3_{l}", T, *gb(3), () if l else mla_loads(C), last)
        assert C.used == len(C.plan)
        with stage(nc, "end", "stored") as (block, stored):
            @block.sync
            def _(sp):
                sp.dma_start(out, C.X[:, :, :]).then_inc(stored, 16)
                sp.wait_ge(stored, 16)



def column(a):
    return np.ascontiguousarray(np.asarray(a, np.float32).reshape(-1, P).T)


def lay_out(x):
    parts = []
    for n, w in VECTORS:
        if n == "b_if":
            a = np.zeros((P, 2), np.float32)
            a[0:4] = np.asarray(x["a_b_if"]).reshape(2, 4).T
        elif n in ("b_q_norm", "b_k_norm"):
            a = column(np.tile(np.asarray(x[n]).reshape(-1), 2))
        else:
            a = column(x[n])
        assert a.shape == (P, w), (n, a.shape)
        parts.append(a)
    arrays = {"vec": np.concatenate(parts, axis=1)}
    rows = []
    for n, w in ROWS:
        if n == "lam":
            a = np.concatenate([np.asarray(x["b_lam_" + s]).reshape(-1) for s in ("q1", "k1", "q2", "k2")])
        else:
            a = np.asarray(x[n]).reshape(-1)
        assert a.shape == (w,), n
        rows.append(a)
    arrays["rows"] = np.concatenate(rows)[None, :]
    by_channel = lambda a: np.ascontiguousarray(np.asarray(a).reshape(S, KT, P).transpose(2, 1, 0))
    arrays["x_T"] = by_channel(x["x"])
    arrays["mem_T"] = by_channel(x["mem_2"])
    arrays["positions"] = np.asarray(x["positions"]).reshape(1, S)
    arrays["sg_ws_T"] = np.ascontiguousarray(np.asarray(x["sg_ws_2"])[0].transpose(2, 0, 1))
    for n in ("w_ada", "a_w_in", "a_w_out", "b_w_in", "b_w_out", "w_router", "moe_w_gu", "moe_w_down", "ab_w_in_2",
              "rw_w2_2", "rw_a2_2", "rw_g2_2", "ab_w_out_2", "mla_w_in_2", "mla_wq_b_2", "mla_wkv_b_2", "mla_w_out_2",
              "xa_wq_2", "xa_wkv_2", "xa_wo_2", "moe_w_group_2", "moe_w_expert_2", "moe_w_gate_2", "moe_w_up_2",
              "moe_w_down_2"):
        a = np.asarray(x[n])
        arrays[n] = a.reshape(a.shape[1:]) if a.shape[0] == 1 else a
    return arrays


def prepare(nc, x):
    arrays = lay_out(x)
    cnames, consts = shape_constants()
    arrays["consts"] = consts
    t = {n: nc.dram_tensor(f"in_{n}", a.shape, mybir.dt.from_np(a.dtype), kind="ExternalInput").ap() for n, a in arrays.items()}
    return {f"in_{n}": a for n, a in arrays.items()}, t, cnames


def kernel(**inputs):
    import concourse.bacc as bacc
    from concourse.bass_utils import run_bass_kernel_spmd

    nc = bacc.Bacc("TRN2", target_bir_lowering=False, num_devices=1)
    arrays, t, cnames = prepare(nc, inputs)
    out = nc.dram_tensor("out_T", (P, KT, S), F32, kind="ExternalOutput").ap()
    two_blocks(nc, t, cnames, out)
    result = run_bass_kernel_spmd(nc, [arrays], core_ids=[0])
    y = result.results[0]["out_T"]
    return np.ascontiguousarray(y.transpose(2, 1, 0)).reshape(1, S, D)
```
